# Optimizing a Trainium2 kernel written in Bass

```python
import jax, jax.numpy as jnp
from jax import lax
import numpy as np

D_MODEL = 1024
BATCH = 1
SEQ = 512
DEPTH = 1

MIX_WIDTH = D_MODEL
CONV_WIDTH = D_MODEL // 2
CONV_GROUPS = 8
CONV_GROUP_DIM = CONV_WIDTH // CONV_GROUPS
CONV_KSIZE = 31
GMLP_WIDTH = MIX_WIDTH - CONV_WIDTH
GMLP_HEADS = 8
GMLP_HEAD_DIM = GMLP_WIDTH // GMLP_HEADS
CHUNK = 128
N_GROUPS = 4
EXPERTS_PER_GROUP = 8
N_EXPERTS = N_GROUPS * EXPERTS_PER_GROUP
TOP_K_INNER = 2
D_EXPERT = D_MODEL // 4
N_MOD = 6
EPS = 1e-6

kernel_name = "hybrid_conv_gmlp_hmoe_block"

def rms_norm(x, g):
    xf = x.astype(jnp.float32)
    y = xf * lax.rsqrt(jnp.mean(xf * xf, axis=-1, keepdims=True) + EPS)
    return (y * g.astype(jnp.float32)).astype(x.dtype)

def layer_norm(x, g, b):
    xf = x.astype(jnp.float32)
    mu = jnp.mean(xf, axis=-1, keepdims=True)
    var = jnp.mean(jnp.square(xf - mu), axis=-1, keepdims=True)
    y = (xf - mu) * lax.rsqrt(var + EPS)
    return (y * g.astype(jnp.float32) + b.astype(jnp.float32)).astype(x.dtype)

def modulate(h, shift, scale):
    return h * (1 + scale[:, None, :]) + shift[:, None, :]

def conv_module(z, w_dw, b_dw, ln_g, ln_b):
    a, g = jnp.split(z, 2, axis=-1)
    y = a * jax.nn.sigmoid(g)
    y = lax.conv_general_dilated(
        y, w_dw[:, None, :].astype(y.dtype), window_strides=(1,),
        padding=((CONV_KSIZE - 1, 0),),
        dimension_numbers=("NWC", "WIO", "NWC"),
        feature_group_count=CONV_WIDTH) + b_dw
    B, S, _ = y.shape
    y = layer_norm(y.reshape(B, S, CONV_GROUPS, CONV_GROUP_DIM), ln_g, ln_b)
    return jax.nn.silu(y.reshape(B, S, CONV_WIDTH))

def chunked_sgu(z, ln_g, ln_b, w_s, b_s):
    u, v = jnp.split(jax.nn.gelu(z), 2, axis=-1)
    B, S, _ = u.shape
    v = v.reshape(B, S // CHUNK, CHUNK, GMLP_HEADS, GMLP_HEAD_DIM)
    v = layer_norm(v, ln_g, ln_b)
    w = w_s * jnp.tril(jnp.ones((CHUNK, CHUNK), dtype=w_s.dtype))
    mixed = jnp.einsum("hts,bcshd->bcthd", w, v) + b_s.T[None, None, :, :, None]
    return u * mixed.reshape(B, S, GMLP_WIDTH)

def hier_moe(h, w_coarse, b_coarse, w_fine, b_fine, w_gate, w_up, w_down):
    B, S, D = h.shape
    t = h.reshape(B * S, D)
    coarse_p = jax.nn.softmax((t @ w_coarse + b_coarse).astype(jnp.float32), axis=-1)
    grp = jnp.argmax(coarse_p, axis=-1)
    p_grp = jnp.max(coarse_p, axis=-1)
    fine_logits = (jnp.einsum("td,gde->tge", t, w_fine) + b_fine).astype(jnp.float32)
    fine_sel = jnp.take_along_axis(fine_logits, grp[:, None, None], axis=1)[:, 0]
    fine_p = jax.nn.softmax(fine_sel, axis=-1)
    top_v, top_i = lax.top_k(fine_p, TOP_K_INNER)
    top_v = top_v / jnp.sum(top_v, axis=-1, keepdims=True)
    inner = jnp.sum(jax.nn.one_hot(top_i, EXPERTS_PER_GROUP, dtype=jnp.float32) * top_v[..., None], axis=1)
    gates = (jax.nn.one_hot(grp, N_GROUPS, dtype=jnp.float32)[:, :, None]
             * (p_grp[:, None, None] * inner[:, None, :])).reshape(B * S, N_EXPERTS).astype(h.dtype)
    y = jnp.zeros_like(t)
    for e in range(N_EXPERTS):
        hid = jax.nn.silu(t @ w_gate[e]) * (t @ w_up[e])
        y = y + gates[:, e:e + 1] * (hid @ w_down[e])
    return y.reshape(B, S, D)

def setup_inputs(seed: int = 0) -> dict:
    key = jax.random.key(seed)
    ks = jax.random.split(key, 24)
    f32 = jnp.float32
    L, D = DEPTH, D_MODEL
    n = lambda k, shape, s: jax.random.normal(k, shape, f32) * s
    return {
        "x": n(ks[0], (BATCH, SEQ, D), 1.0),
        "c": n(ks[1], (BATCH, D), 1.0),
        "w_ada": n(ks[2], (L, D, N_MOD * D), 0.5 * D ** -0.5),
        "b_ada": n(ks[3], (L, N_MOD * D), 0.01),
        "g_mix": 1.0 + n(ks[4], (L, D), 0.02),
        "w_in": n(ks[5], (L, D, 2 * MIX_WIDTH), D ** -0.5),
        "conv_w": n(ks[6], (L, CONV_KSIZE, CONV_WIDTH), CONV_KSIZE ** -0.5),
        "conv_b": n(ks[7], (L, CONV_WIDTH), 0.01),
        "conv_ln_g": 1.0 + n(ks[8], (L, CONV_GROUPS, CONV_GROUP_DIM), 0.02),
        "conv_ln_b": n(ks[9], (L, CONV_GROUPS, CONV_GROUP_DIM), 0.01),
        "sgu_ln_g": 1.0 + n(ks[10], (L, GMLP_HEADS, GMLP_HEAD_DIM), 0.02),
        "sgu_ln_b": n(ks[11], (L, GMLP_HEADS, GMLP_HEAD_DIM), 0.01),
        "sgu_w": n(ks[12], (L, GMLP_HEADS, CHUNK, CHUNK), CHUNK ** -0.5),
        "sgu_b": 1.0 + n(ks[13], (L, GMLP_HEADS, CHUNK), 0.1),
        "w_out": n(ks[14], (L, MIX_WIDTH, D), MIX_WIDTH ** -0.5),
        "g_ffn": 1.0 + n(ks[15], (L, D), 0.02),
        "w_coarse": n(ks[16], (L, D, N_GROUPS), D ** -0.5),
        "b_coarse": n(ks[17], (L, N_GROUPS), 0.01),
        "w_fine": n(ks[18], (L, N_GROUPS, D, EXPERTS_PER_GROUP), D ** -0.5),
        "b_fine": n(ks[19], (L, N_GROUPS, EXPERTS_PER_GROUP), 0.01),
        "w_gate": n(ks[20], (L, N_EXPERTS, D, D_EXPERT), D ** -0.5),
        "w_up": n(ks[21], (L, N_EXPERTS, D, D_EXPERT), D ** -0.5),
        "w_down": n(ks[22], (L, N_EXPERTS, D_EXPERT, D), D_EXPERT ** -0.5),
        "g_final": 1.0 + n(ks[23], (D,), 0.02),
    }

def reference(x, c, w_ada, b_ada, g_mix, w_in, conv_w, conv_b, conv_ln_g, conv_ln_b,
              sgu_ln_g, sgu_ln_b, sgu_w, sgu_b, w_out, g_ffn, w_coarse, b_coarse,
              w_fine, b_fine, w_gate, w_up, w_down, g_final):
    c_act = jax.nn.silu(c)
    for l in range(DEPTH):
        mod = c_act @ w_ada[l] + b_ada[l]
        sh1, sc1, gt1, sh2, sc2, gt2 = jnp.split(mod, N_MOD, axis=-1)
        h = modulate(rms_norm(x, g_mix[l]), sh1, sc1)
        z = h @ w_in[l]
        z_conv = z[..., :2 * CONV_WIDTH]
        z_sgu = z[..., 2 * CONV_WIDTH:]
        y_conv = conv_module(z_conv, conv_w[l], conv_b[l], conv_ln_g[l], conv_ln_b[l])
        y_sgu = chunked_sgu(z_sgu, sgu_ln_g[l], sgu_ln_b[l], sgu_w[l], sgu_b[l])
        mix = jnp.concatenate([y_conv, y_sgu], axis=-1) @ w_out[l]
        x = x + gt1[:, None, :] * mix
        h = modulate(rms_norm(x, g_ffn[l]), sh2, sc2)
        x = x + gt2[:, None, :] * hier_moe(h, w_coarse[l], b_coarse[l], w_fine[l], b_fine[l],
                                           w_gate[l], w_up[l], w_down[l])
    return rms_norm(x, g_final)


_drawn_inputs = setup_inputs


def setup_inputs(seed=0):
    import zlib

    import numpy as np

    out = dict(_drawn_inputs(seed))
    spreads = {}
    factors = {'b_ada': 4.465,
     'g_mix': 7.957,
     'conv_b': 8.0,
     'conv_ln_g': 8.0,
     'conv_ln_b': 64.0,
     'sgu_ln_g': 8.0,
     'sgu_ln_b': 8.0,
     'sgu_b': 3.194,
     'g_ffn': 5.961,
     'b_coarse': 8.0,
     'b_fine': 8.0,
     'g_final': 8.541}
    for name, (base, spread) in spreads.items():
        noise = np.random.default_rng([zlib.crc32(name.encode()), seed]).standard_normal(out[name].shape)
        drawn = base * np.exp(spread * noise) if base else spread * noise
        out[name] = __import__('jax').numpy.asarray(drawn.astype(out[name].dtype))
    for name, factor in factors.items():
        out[name] = (out[name] * factor).astype(out[name].dtype)
    return out
```

```python
from contextlib import ExitStack, contextmanager

import concourse.bass as bass
from concourse import mybir

P = 128
F32 = mybir.dt.float32
F16 = mybir.dt.float16
I32 = mybir.dt.int32
U32 = mybir.dt.uint32
ALU = mybir.AluOpType
ACT = mybir.ActivationFunctionType
AX_X = mybir.AxisListType.X


def build_block(nc, x, c, w_ada, b_ada, g_mix, w_in, conv_w, conv_b, conv_ln_g, conv_ln_b,
                sgu_ln_g, sgu_ln_b, sgu_w, sgu_b, w_out, g_ffn, w_coarse, b_coarse,
                w_fine, b_fine, w_gate, w_up, w_down, g_final, out):
    S, D = x.shape[1], x.shape[2]
    KC = D // P
    T = S // P
    CW = conv_w.shape[2]
    CT = CW // P
    TAPS = conv_w.shape[1]
    PAD = TAPS - 1
    HEADS = sgu_w.shape[1]
    HD = CW // HEADS
    G = w_coarse.shape[2]
    EG = w_fine.shape[3]
    NE = G * EG
    DE = w_gate.shape[3]
    FC = DE // P
    HALF = D // 2
    SLOTS = 64
    NR = G + NE
    EPS = 1e-6
    RING = 6
    SLOT_W = 2 * KC * DE + FC * D
    GU_W = 2 * KC * DE
    ADA_BUFS = 5
    ROUND = 4 * HALF
    ROUNDS = w_ada.shape[2] // ROUND
    AHEAD = 3
    OOB = 2 * S * 2
    XG = 3
    assert (S, D, CW, HD, NE, DE, OOB) == (512, 1024, 512, 64, 32, 256, 2048)

    xn_rows = nc.dram_tensor("xn_rows", [S, D], F32).ap()
    y_rows = nc.dram_tensor("y_rows", [2 * 2 * S, HALF], F32).ap()

    with ExitStack() as ctx:
        def sb(name, shape, dt=F32):
            return ctx.enter_context(nc.sbuf_tensor(name, shape, dt))

        def sem(name):
            return ctx.enter_context(nc.semaphore(name))

        ps = ctx.enter_context(nc.psum_tensor("ps", [P, 8, HALF], F32))

        ring = sb("ring", [P, RING * SLOT_W])
        work = sb("work", [P, 12288])
        x_sb = sb("x_sb", [P, T, D])
        mod2 = sb("mod2", [P, HALF])
        ident = sb("ident", [P, P])
        ones = sb("ones", [P, P])
        group_mean = sb("group_mean", [P, P])
        slot_iota = sb("slot_iota", [P, P])
        before16 = sb("before16", [P, P], F16)
        ones16 = sb("ones16", [P, P], F16)
        w_router = sb("w_router", [P, KC, NR])
        conv_c = sb("conv_c", [P, CT, TAPS + 3])
        b_router = sb("b_router", [P, NR])
        c_col = sb("c_col", [P, KC])
        logits = sb("logits", [P, T, NR])
        gmix_col = sb("gmix_col", [P, KC])
        gffn_col = sb("gffn_col", [P, KC])
        mod_col = sb("mod_col", [P, 4, KC])
        a1_col = sb("a1_col", [P, KC])
        a2_col = sb("a2_col", [P, KC])
        eps_col = sb("eps_col", [P, 1])
        row_off = sb("row_off", [P, 1])
        tok_id = sb("tok_id", [P, T])
        stat = sb("stat", [P, 8, T])
        ln_stat = sb("ln_stat", [P, 2, HEADS])

        def ring_at(off, n):
            return ring[:, off:off + n]

        def ada_buf(b):
            return ring_at(b * ROUND, ROUND)
        o = ADA_BUFS * ROUND
        bada_sb = ring_at(o, ROUNDS * HALF).rearrange("p (r n) -> p r n", r=ROUNDS)
        c_rep = ring_at(o + ROUNDS * HALF, KC * 32).rearrange("p (k m) -> p k m", k=KC)
        o = 2 * SLOT_W
        win_u = ring_at(o, KC * CW).rearrange("p (k n) -> p k n", k=KC)
        win_v = ring_at(o + 4096, KC * CW).rearrange("p (k n) -> p k n", k=KC)
        h_t = ring_at(o + 8192, KC * S).rearrange("p (k n) -> p k n", k=KC)
        o = 4 * SLOT_W
        win_a = ring_at(o, KC * CW).rearrange("p (k n) -> p k n", k=KC)
        win_g = ring_at(o + 4096, KC * CW).rearrange("p (k n) -> p k n", k=KC)
        y_pad = ring_at(o + 8192, CT * (S + PAD)).rearrange("p (i n) -> p i n", i=CT)
        mod01 = ring_at(o + 10368, 2 * HALF).rearrange("p (r n) -> p r n", r=2)
        v_sb = ring_at(o, T * CW).rearrange("p (t n) -> p t n", t=T)
        v_sq = ring_at(o + 2048, CW)
        conv_sq = ring_at(o + 2560, S)
        w_sgu_t = ring_at(o + 4096, HEADS * P).rearrange("p (h n) -> p h n", h=HEADS)
        ln_g_row = ring_at(o + 5120, CW)
        ln_b_row = ring_at(o + 5632, CW)
        sgu_b_row = ring_at(o + 6144, CT * P).rearrange("p (i n) -> p i n", i=CT)
        conv_yc = ring_at(o + 6656, 2 * S).rearrange("p (b n) -> p b n", b=2)
        conv_rs = ring_at(o + 7680, S)
        xn2 = ring_at(o + 10240, D).rearrange("p (k n) -> p k n", k=KC)
        gt1b = ring_at(o + 11264, D)

        wout_sb = work[:, 0:8192].rearrange("p (m n) -> p m n", m=KC)
        y_cat = work[:, 8192:12288].rearrange("p (m n) -> p m n", m=KC)
        xn = work[:, 0:4096].rearrange("p (t n) -> p t n", t=T)
        sig = work[:, 4096:5120].rearrange("p (b n) -> p b n", b=2)
        w_sgu_raw = work[:, 5120:6144].rearrange("p (h n) -> p h n", h=HEADS)
        conv_raw = work[0:TAPS + 3, 6144:6656]
        fine_raw = work[:, 6656:6912].rearrange("p (g k e) -> p g k e", g=G, k=KC)
        coarse_raw = work[:, 6912:6944].rearrange("p (k g) -> p k g", k=KC)

        tri = work[:, 6944:7072]

        xg = work[:, 0:XG * D].rearrange("p (b k n) -> p b k n", b=XG, k=KC)
        xt = work[:, 3072:4096].rearrange("p (b k n) -> p b k n", b=2, k=KC)
        gate_act = work[:, 4096:4352].rearrange("p (b n) -> p b n", b=2)
        hid = work[:, 4352:4608].rearrange("p (b n) -> p b n", b=2)
        hid_t = work[:, 4608:4864].rearrange("p (b n) -> p b n", b=2)
        y_exp = work[:, 4864:5888].rearrange("p (b n) -> p b n", b=2)
        picks = work[:, 5888:6400].bitcast(F16).rearrange("p (b t n) -> p b t n", b=2, t=T)
        o = [6400]

        def rt(n, dt=F32):
            a = work[:, o[0]:o[0] + n]
            o[0] += n
            return a if dt == F32 else a.bitcast(dt)
        coarse8 = rt(T * 8).rearrange("p (t n) -> p t n", t=T)
        top_c = rt(T * 8).rearrange("p (t n) -> p t n", t=T)
        top_ci = rt(T * 8, U32).rearrange("p (t n) -> p t n", t=T)
        c_exp = rt(T * 8).rearrange("p (t n) -> p t n", t=T)
        neg_max = rt(T)
        p_grp = rt(T)
        grp = rt(T)
        grp_hot = rt(T * G).rearrange("p (t g) -> p t g", t=T)
        fine_m = rt(T * NE).rearrange("p (t g e) -> p t g e", t=T, g=G)
        fine_s = rt(T * EG).rearrange("p (t e) -> p t e", t=T)
        top_f = rt(T * 8).rearrange("p (t n) -> p t n", t=T)
        top_fi = rt(T * 8, U32).rearrange("p (t n) -> p t n", t=T)
        gate_k = rt(2 * T).rearrange("p (k t) -> p k t", k=2)
        expert_k = rt(2 * T).rearrange("p (k t) -> p k t", k=2)
        e_diff = rt(T)
        hot0 = rt(T * NE).rearrange("p (t e) -> p t e", t=T)
        hot1 = rt(T * NE).rearrange("p (t e) -> p t e", t=T)
        place = rt(T * NE).rearrange("p (t e) -> p t e", t=T)
        hot16 = rt(T * NE // 2, F16).rearrange("p (t e) -> p t e", t=T)
        pre16 = rt((T + 1) * NE // 2, F16).rearrange("p (t e) -> p t e", t=T + 1)
        row_vals = rt(T * NE, F16).rearrange("p (t e v) -> p t e v", t=T, v=2)
        row_idx = rt(2 * RING, U32).rearrange("p (b v) -> p b v", v=2)
        blocks_f = rt(2 * NE).rearrange("p (v e) -> p v e", v=2)
        block_info = rt(2 * NE, I32).rearrange("p (v e) -> p v e", v=2)
        row_idx_x = rt(2, U32)
        xg_x = rt(D).rearrange("p (k n) -> p k n", k=KC)
        xt_x = rt(KC * SLOTS).rearrange("p (k n) -> p k n", k=KC)
        gate_act_x, hid_x, hid_t_x = rt(P), rt(P), rt(P)
        y_exp_x = rt(HALF)
        picks_x = rt(T * P // 2, F16).rearrange("p (t n) -> p t n", t=T)
        assert o[0] <= 12288

        y_back = ring_at(0, T * 2 * D).rearrange("p (t k h n) -> p t k h n", t=T, k=2, h=2)
        acc = ring_at(T * 2 * D, 2 * D).rearrange("p (b n) -> p b n", b=2)
        gt2b = ring_at(T * 2 * D + 2 * D, D)
        gfin = ring_at(T * 2 * D + 3 * D, D)
        sq_junk = ring_at(T * 2 * D + 4 * D, D)

        x_in = [sem(f"x_in{t}") for t in range(T)]
        consts_in = sem("consts_in")
        bada_in = sem("bada_in")
        ada_in = [sem(f"ada_in{b}") for b in range(ADA_BUFS)]
        win_in = [sem(f"win_in_{n}") for n in "aguv"]
        sgu_rows_in = sem("sgu_rows_in")
        wout_in = sem("wout_in")
        expert_in = [sem(f"expert_in{r}") for r in range(RING)]
        pool_consts = sem("pool_consts")
        pool_order = sem("pool_order")
        bada_zero = sem("bada_zero")
        router_packed = sem("router_packed")
        act_order = sem("act_order")
        dve_order = sem("dve_order")
        c_act_ready = sem("c_act_ready")
        c_rep_ready = sem("c_rep_ready")
        x_squared = sem("x_squared")
        x_root = sem("x_root")
        xn_ready = sem("xn_ready")
        conv_c_turned = sem("conv_c_turned")
        conv_c_ready = sem("conv_c_ready")
        xn_turned = sem("xn_turned")
        xnt_ready_dve = sem("xnt_ready_dve")
        ada_used = sem("ada_used")
        mod_rows_ready = sem("mod_rows_ready")
        mod_cols_in = [sem(f"mod_cols_in{r}") for r in range(3)]
        a1_ready = sem("a1_ready")
        h_dve = sem("h_dve")
        h_act = sem("h_act")
        z_done = sem("z_done")
        sig_ready = sem("sig_ready")
        glu_ready = sem("glu_ready")
        gelu_ready = sem("gelu_ready")
        conv_step = sem("conv_step")
        sgu_w_turned = sem("sgu_w_turned")
        sgu_w_ready = sem("sgu_w_ready")
        gt1_spread = sem("gt1_spread")
        gt1_ready = sem("gt1_ready")
        v_centred = sem("v_centred")
        v_squared = sem("v_squared")
        v_var = sem("v_var")
        v_root = sem("v_root")
        v_rstd = sem("v_rstd")
        v_ready = sem("v_ready")
        conv_mean = sem("conv_mean")
        conv_centred = sem("conv_centred")
        conv_squared = sem("conv_squared")
        conv_var = sem("conv_var")
        conv_root = sem("conv_root")
        conv_normed = sem("conv_normed")
        conv_out = sem("conv_out")
        sgu_mixed = sem("sgu_mixed")
        sgu_out = sem("sgu_out")
        mix_done = sem("mix_done")
        x2_ready = sem("x2_ready")
        x2_squared = sem("x2_squared")
        x2_root = sem("x2_root")
        xn2_ready = sem("xn2_ready")
        xn2_stored = sem("xn2_stored")
        xn2_turned = sem("xn2_turned")
        a2_ready = sem("a2_ready")
        h2_dve = sem("h2_dve")
        h2_act = sem("h2_act")
        logits_done = sem("logits_done")
        logits_ready = sem("logits_ready")
        neg_max_ready = sem("neg_max_ready")
        c_exp_ready = sem("c_exp_ready")
        diff_ready = sem("diff_ready")
        diff_exp = sem("diff_exp")
        hot_ready = sem("hot_ready")
        counted = sem("counted")
        routed = sem("routed")
        picks_ready = sem("picks_ready")
        rows_found = sem("rows_found")
        rows_ready = sem("rows_ready")
        gathered = [sem(f"gathered{b}") for b in range(XG)]
        xg_turned = sem("xg_turned")
        xt_ready = sem("xt_ready")
        gate_up_done = sem("gate_up_done")
        silu_ready = sem("silu_ready")
        hid_ready = sem("hid_ready")
        hid_turned = sem("hid_turned")
        hid_t_ready = sem("hid_t_ready")
        down_done = sem("down_done")
        y_ready = sem("y_ready")
        scattered = [sem(f"scattered{b}") for b in range(2)]
        ov_place = sem("ov_place")
        ov_free = sem("ov_free")
        ov_picks = sem("ov_picks")
        ov_found = sem("ov_found")
        ov_rows = sem("ov_rows")
        ov_gathered = sem("ov_gathered")
        ov_turned = sem("ov_turned")
        ov_xt = sem("ov_xt")
        ov_gate_up = sem("ov_gate_up")
        ov_silu = sem("ov_silu")
        ov_hid = sem("ov_hid")
        ov_hid_turned = sem("ov_hid_turned")
        ov_hid_t = sem("ov_hid_t")
        ov_down = sem("ov_down")
        ov_y = sem("ov_y")
        ov_scattered = sem("ov_scattered")
        ov_passed = sem("ov_passed")
        pool_go = sem("pool_go")
        tokens_here = sem("tokens_here")
        all_scattered = sem("all_scattered")
        gfin_in = sem("gfin_in")
        gt2_spread = sem("gt2_spread")
        gt2_ready = sem("gt2_ready")
        y_in = [sem(f"y_in{t}") for t in range(T)]
        y0_scaled = sem("y0_scaled")
        x3_ready = sem("x3_ready")
        x3_squared = sem("x3_squared")
        x3_root = sem("x3_root")
        out_ready = sem("out_ready")
        out_stored = sem("out_stored")

        x_rows = x.rearrange("b (t p) d -> (b t) p d", p=P)
        out_rows = out.rearrange("b (t p) d -> (b t) p d", p=P)
        ada_v = w_ada.rearrange("l (p k) n -> (l p) k n", k=KC)
        win_dram = w_in.rearrange("l (p k) n -> (l p) k n", k=KC)
        wout_dram = w_out.rearrange("l (m p) n -> (l p) m n", p=P)
        gate_dram = w_gate.rearrange("l e (p k) f -> (l e) p (k f)", k=KC)
        up_dram = w_up.rearrange("l e (p k) f -> (l e) p (k f)", k=KC)
        down_dram = w_down.rearrange("l e (c p) n -> (l e) p c n", p=P)

        def col_of(v):
            return v.rearrange("l (p k) -> (l p) k", k=KC)

        def load_gate_up(eng, e, slot, done):
            base = ring[:, slot * SLOT_W:(slot + 1) * SLOT_W]
            eng.dma_start(base[:, 0:GU_W // 2], gate_dram[e]).then_inc(done, 16)
            eng.dma_start(base[:, GU_W // 2:GU_W], up_dram[e]).then_inc(done, 16)

        def load_down(eng, e, slot, done):
            base = ring[:, slot * SLOT_W:(slot + 1) * SLOT_W]
            eng.dma_start(base[:, GU_W:SLOT_W].rearrange("p (c n) -> p c n", c=FC),
                          down_dram[e]).then_inc(done, 16)

        def load_expert(eng, e, slot, done):
            load_gate_up(eng, e, slot, done)
            load_down(eng, e, slot, done)

        block = ctx.enter_context(nc.Block())

        @contextmanager
        def extra_blocks(eng, e):
            blocks = eng.value_load(block_info[0:1, 0, bass.ds(e, 1)], min_val=0, max_val=S // SLOTS)
            with eng.If(blocks > 1):
                before = eng.value_load(block_info[0:1, 1, bass.ds(e, 1)], min_val=0, max_val=2 * S // SLOTS)
                with eng.Fori(1, blocks) as j:
                    yield before + j - 1

        @block.sync
        def _(sp):
            for t in range(T):
                sp.dma_start(x_sb[:, t, :], x_rows[t]).then_inc(x_in[t], 16)

            def ada_unit(n):
                b = n % ADA_BUFS
                if n >= ADA_BUFS:
                    sp.wait_ge(ada_used, n - ADA_BUFS + 1)
                r, k = n // KC, n % KC
                sp.dma_start(ada_buf(b), ada_v[:, k, r * ROUND:(r + 1) * ROUND]).then_inc(ada_in[b], 16)

            for n in range(KC):
                ada_unit(n)
            for q, dst, first in ((0, win_a, 0), (1, win_g, CW), (2, win_u, 2 * CW), (3, win_v, 3 * CW)):
                sp.dma_start(dst, win_dram[:, :, first:first + CW]).then_inc(win_in[q], 16)
            for n in range(KC, ROUNDS * KC):
                ada_unit(n)
            sp.wait_ge(z_done, 2 * CT)
            sp.dma_start(ln_g_row, sgu_ln_g.rearrange("l h d -> l (h d)").to_broadcast([P, CW])
                         ).then_inc(sgu_rows_in, 16)
            sp.dma_start(ln_b_row, sgu_ln_b.rearrange("l h d -> l (h d)").to_broadcast([P, CW])
                         ).then_inc(sgu_rows_in, 16)
            for h in range(HEADS):
                rows = slice(HD * (h % 2), HD * (h % 2) + HD)
                sp.dma_start(sgu_b_row[rows, h // 2, :], sgu_b[0, h:h + 1, :].to_broadcast([HD, P])
                             ).then_inc(sgu_rows_in, 16)
            sp.wait_ge(glu_ready, CT)
            sp.wait_ge(sgu_w_ready, 2)
            sp.wait_ge(router_packed, 1)
            sp.dma_start(wout_sb, wout_dram).then_inc(wout_in, 16)

            sp.wait_ge(ada_used, ROUNDS * KC)
            sp.wait_ge(mod_rows_ready, ROUNDS)
            load_expert(sp, 0, 0, expert_in[0])
            load_expert(sp, 1, 1, expert_in[1])
            sp.wait_ge(z_done, 2 * CT + CT + T)
            load_expert(sp, 2, 2, expert_in[2])
            load_expert(sp, 3, 3, expert_in[3])
            sp.wait_ge(conv_out, CT)
            sp.wait_ge(sgu_out, CT)
            sp.wait_ge(mod_cols_in[1], 32)
            sp.wait_ge(gt1_spread, 1)
            sp.wait_ge(mod_cols_in[0], 64)
            load_expert(sp, 4, 4, expert_in[4])
            load_gate_up(sp, 5, 5, expert_in[5])
            sp.wait_ge(xn2_turned, T)
            sp.wait_ge(xn2_stored, 16 * T)
            sp.wait_ge(x2_ready, 2 * T)
            load_down(sp, 5, 5, expert_in[5])

            with sp.Fori(0, (NE - RING) // RING) as i:
                for r in range(RING):
                    e = RING + RING * i + r
                    sp.wait_ge(down_done, RING * i + r + 1)
                    load_expert(sp, e, r, expert_in[r])
            for e in range(NE - NE % RING, NE):
                sp.wait_ge(down_done, e - RING + 1)
                load_expert(sp, e, e % RING, expert_in[e % RING])

            sp.wait_ge(all_scattered, 1)
            back = y_rows.rearrange("(h k t p) n -> t k p h n", h=2, k=2, p=P)
            for t in range(T):
                for k in range(2):
                    sp.dma_start(y_back[:, t, k], back[t, k]).then_inc(y_in[t], 16)
            for t in range(T):
                sp.wait_ge(out_ready, t + 1)
                sp.dma_start(out_rows[t], x_sb[:, t, :]).then_inc(out_stored, 16)
            sp.wait_ge(out_stored, 16 * T)

        @block.gpsimd
        def _(pool):
            done = [0]

            def link(ins):
                ins.then_inc(pool_order, 1)
                done[0] += 1
                pool.wait_ge(pool_order, done[0])

            link(pool.memset(ident[:], 1.0))
            link(pool.affine_select(out=ident[:], in_=ident[:], compare_op=ALU.is_equal, fill=0.0, base=0,
                                    pattern=[[1, P]], channel_multiplier=-1))
            link(pool.memset(bada_sb, 0.0))
            pool.memset(ones[:], 1.0).then_inc(bada_zero, 1)
            link(pool.memset(eps_col[:], EPS))
            link(pool.memset(group_mean[:], 0.0))
            link(pool.memset(group_mean[0:HD, 0:HD], 1.0 / HD))
            link(pool.memset(group_mean[HD:P, HD:P], 1.0 / HD))
            link(pool.memset(tri, 1.0))
            link(pool.affine_select(out=tri, in_=tri, compare_op=ALU.is_ge, fill=0.0, base=0,
                                    pattern=[[1, P]], channel_multiplier=-1))
            link(pool.memset(ones16[:], 1.0))
            link(pool.affine_select(out=before16[:], in_=ones16[:], compare_op=ALU.is_gt, fill=0.0, base=0,
                                    pattern=[[1, P]], channel_multiplier=-1))
            slot_i = slot_iota[:].bitcast(I32)
            link(pool.iota(slot_i, pattern=[[0, 2], [1, SLOTS]], base=0, channel_multiplier=0))
            link(pool.tensor_copy(slot_iota[:], slot_i))
            tok_i = tok_id[:].bitcast(I32)
            link(pool.iota(tok_i, pattern=[[P, T]], base=0, channel_multiplier=1))
            link(pool.tensor_copy(tok_id[:], tok_i))
            link(pool.memset(row_off[0:SLOTS, :], float(OOB)))
            link(pool.memset(row_off[SLOTS:P, :], float(OOB + 2 * S)))
            pool.memset(y_pad[:, :, 0:PAD], 0.0).then_inc(pool_consts, 1)
            pool.wait_ge(consts_in, 16 * 15)
            link(pool.tensor_copy(w_router[:, :, 0:G], coarse_raw))
            for g in range(G):
                copied = pool.tensor_copy(w_router[:, :, G + g * EG:G + (g + 1) * EG], fine_raw[:, g])
                if g < G - 1:
                    link(copied)
            copied.then_inc(router_packed, 1)

            pool.wait_ge(sgu_rows_in, 16 * (2 + HEADS))
            for t in range(T):
                vt = v_sb[:, t, :].rearrange("p (h d) -> p h d", h=HEADS)
                pool.wait_ge(v_rstd, t + 1)
                link(pool.tensor_tensor(vt, vt, ln_stat[:, t % 2, :].unsqueeze(2).to_broadcast([P, HEADS, HD]),
                                        ALU.mult))
                link(pool.tensor_tensor(v_sb[:, t, :], v_sb[:, t, :], ln_g_row, ALU.mult))
                pool.tensor_tensor(v_sb[:, t, :], v_sb[:, t, :], ln_b_row, ALU.add).then_inc(v_ready, 1)

            def gather(e, b3, b6, wait_buffer):
                pool.wait_ge(rows_ready, e + 1)
                if wait_buffer:
                    pool.wait_ge(xg_turned, e - XG + 1)
                pool.sem_inc(pool_go, 1)
                pool.indirect_dma_start(
                    xg[0:SLOTS, b3].rearrange("p k n -> p (k n)"), None, xn_rows,
                    bass.IndirectOffsetOnAxis(row_idx[0:SLOTS, b6, 0:1], 0),
                    bounds_check=S - 1, oob_is_err=False).then_inc(gathered[b3], 16)

            def scatter(e, b2, b6):
                pool.wait_ge(y_ready, e + 1)
                pool.sem_inc(pool_go, 1)
                pool.indirect_dma_start(
                    y_rows, bass.IndirectOffsetOnAxis(row_idx[:, b6, 1:2], 0), y_exp[:, b2], None,
                    bounds_check=4 * S - 1, oob_is_err=False).then_inc(scattered[b2], 16)

            pool.wait_ge(xn2_stored, 16 * T)
            for e in range(AHEAD + 1):
                gather(e, e % XG, e % RING, e >= XG)
            pool.sem_inc(ov_free, 1)

            def extra(e):
                with extra_blocks(pool, e) as n:
                    pool.wait_ge(ov_rows, n + 1)
                    pool.sem_inc(pool_go, 1)
                    pool.indirect_dma_start(
                        xg_x[0:SLOTS].rearrange("p k n -> p (k n)"), None, xn_rows,
                        bass.IndirectOffsetOnAxis(row_idx_x[0:SLOTS, 0:1], 0),
                        bounds_check=S - 1, oob_is_err=False).then_inc(ov_gathered, 16)
                    pool.wait_ge(ov_y, n + 1)
                    pool.sem_inc(pool_go, 1)
                    pool.indirect_dma_start(
                        y_rows, bass.IndirectOffsetOnAxis(row_idx_x[:, 1:2], 0), y_exp_x, None,
                        bounds_check=4 * S - 1, oob_is_err=False).then_inc(ov_scattered, 16)
                    pool.wait_ge(ov_scattered, 16 * n + 16)
                    pool.sem_inc(ov_free, 1)

            for e in range(0, 2):
                if e:
                    gather(e + AHEAD, (e + AHEAD) % XG, (e + AHEAD) % RING, True)
                extra(e)
                scatter(e, e % 2, e % RING)
            with pool.Fori(0, 4) as i:
                for r in range(RING):
                    e = 2 + RING * i + r
                    gather(e + AHEAD, (2 + r + AHEAD) % XG, (2 + r + AHEAD) % RING, True)
                    extra(e)
                    scatter(e, r % 2, (2 + r) % RING)
            for e in range(NE - RING, NE):
                if e + AHEAD < NE:
                    gather(e + AHEAD, (e + AHEAD) % XG, (e + AHEAD) % RING, True)
                extra(e)
                scatter(e, e % 2, e % RING)
            for b in range(2):
                pool.wait_ge(scattered[b], 16 * NE // 2)
            pool.sem_inc(all_scattered, 1)

        @block.scalar
        def _(act):
            done = [0]

            def link(ins):
                ins.then_inc(act_order, 1)
                done[0] += 1
                act.wait_ge(act_order, done[0])

            for dst, src in (
                (c_col[:], col_of(c)), (gmix_col[:], col_of(g_mix)), (gffn_col[:], col_of(g_ffn)),
                (conv_raw[0:TAPS], conv_w[0]), (conv_raw[TAPS:TAPS + 1], conv_b),
                (conv_raw[TAPS + 1:TAPS + 2], conv_ln_g.rearrange("l g d -> l (g d)")),
                (conv_raw[TAPS + 2:TAPS + 3], conv_ln_b.rearrange("l g d -> l (g d)")),
                (w_sgu_raw, sgu_w[0].rearrange("h t s -> t h s")),
                (coarse_raw, w_coarse[0].rearrange("(p k) g -> p k g", k=KC)),
                (b_router[:, 0:G], b_coarse.to_broadcast([P, G])),
                (b_router[:, G:NR], b_fine.rearrange("l g e -> l (g e)").to_broadcast([P, NE])),
            ):
                act.dma_start(dst, src).then_inc(consts_in, 16)
            for g in range(G):
                act.dma_start(fine_raw[:, g], w_fine[0, g].rearrange("(p k) e -> p k e", k=KC)
                              ).then_inc(consts_in, 16)
            act.wait_ge(bada_zero, 1)
            bada_v = b_ada.rearrange("l (r q n) -> l r q n", q=4, n=HALF)
            for q in range(4):
                act.dma_start(bada_sb[32 * q:32 * q + 1], bada_v[:, :, q, :]).then_inc(bada_in, 16)

            act.wait_ge(consts_in, 16 * 15)
            act.activation(c_col[:], c_col[:], ACT.Silu).then_inc(c_act_ready, 1)
            act.wait_ge(pool_consts, 1)
            for t in range(T):
                act.wait_ge(x_in[t], 16)
                link(act.activation(xn[:, t, :], x_sb[:, t, :], ACT.Square, accum_out=stat[:, 0, t:t + 1]))
                act.activation(stat[:, 1, t:t + 1], stat[:, 0, t:t + 1], ACT.Sqrt, bias=eps_col[:],
                               scale=1.0 / D).then_inc(x_root, 1)
            act.wait_ge(xn_turned, 1)
            for k in range(1, KC, 2):
                link(act.copy(h_t[:, k, :], ps[:, k, :]))

            def mod_cols(r, rows, pairs):
                act.wait_ge(mod_rows_ready, r + 1)
                for q, v in pairs:
                    part = slice((q % 2) * P // 2, (q % 2) * P // 2 + P // 2)
                    act.dma_start(mod_col[part, v, :], rows[32 * q:32 * q + 1, :].rearrange(
                        "o (p k) -> o p k", k=KC)).then_inc(mod_cols_in[r], 16)

            mod_cols(0, mod01[:, 0], [(q, q // 2) for q in range(4)])
            act.wait_ge(a1_ready, 1)
            for k in range(1, KC, 2):
                act.activation(h_t[:, k, :], h_t[:, k, :], ACT.Identity, bias=mod_col[:, 0, k:k + 1],
                               scale=a1_col[:, k:k + 1]).then_inc(h_act, 1)

            for i in range(CT):
                act.wait_ge(z_done, 2 * i + 2)
                if i >= 2:
                    act.wait_ge(glu_ready, i - 1)
                act.activation(sig[:, i % 2, :], ps[:, (2 * i + 1) % 4, :], ACT.Sigmoid).then_inc(sig_ready, 1)
            for i in range(CT):
                n = 2 * CT + i
                act.wait_ge(z_done, n + 1)
                if i == 0:
                    mod_cols(1, mod01[:, 1], [(q, 2) for q in (2, 3)])
                act.activation(y_cat[:, CT + i, :], ps[:, n % 4, :], ACT.Gelu_apprx_tanh).then_inc(gelu_ready, 1)
            act.wait_ge(gt1_spread, 1)
            act.wait_ge(mod_cols_in[1], 32)
            link(act.copy(gt1b[:, 0:HALF], ps[:, 6, :]))
            act.copy(gt1b[:, HALF:D], ps[:, 7, :]).then_inc(gt1_ready, 1)
            mod_cols(2, mod2[:], [(q, 3) for q in (0, 1)])
            for t in range(T):
                n = 2 * CT + CT + t
                act.wait_ge(z_done, n + 1)
                act.activation(v_sb[:, t, :], ps[:, n % 4, :], ACT.Gelu_apprx_tanh).then_inc(gelu_ready, 1)
                act.wait_ge(v_centred, t + 1)
                act.activation(v_sq, v_sb[:, t, :], ACT.Square).then_inc(v_squared, 1)
                act.wait_ge(v_var, t + 1)
                act.activation(ln_stat[:, t % 2, :], ln_stat[:, t % 2, :], ACT.Sqrt, bias=eps_col[:],
                               scale=1.0 / HD).then_inc(v_root, 1)
            for i in range(CT):
                act.wait_ge(conv_centred, i + 1)
                if i >= 1:
                    act.wait_ge(conv_var, i)
                act.activation(conv_sq, conv_yc[:, i % 2, :], ACT.Square).then_inc(conv_squared, 1)
                act.wait_ge(conv_var, i + 1)
                if i >= 1:
                    act.wait_ge(conv_normed, i)
                act.activation(conv_rs, ps[:, (6, 4)[i % 2], :], ACT.Sqrt, bias=eps_col[:]).then_inc(conv_root, 1)
            for i in range(CT):
                act.wait_ge(conv_normed, i + 1)
                act.activation(y_cat[:, i, :], y_cat[:, i, :], ACT.Silu, bias=conv_c[:, i, TAPS + 2:TAPS + 3],
                               scale=conv_c[:, i, TAPS + 1:TAPS + 2]).then_inc(conv_out, 1)

            for t in range(T):
                act.wait_ge(x2_ready, 2 * t + 2)
                if t >= 1:
                    act.wait_ge(xn2_stored, 16 * t)
                    act.wait_ge(xn2_turned, t)
                link(act.activation(xn2.rearrange("p k n -> p (k n)"), x_sb[:, t, :], ACT.Square,
                                    accum_out=stat[:, 2, t:t + 1]))
                act.activation(stat[:, 3, t:t + 1], stat[:, 2, t:t + 1], ACT.Sqrt, bias=eps_col[:],
                               scale=1.0 / D).then_inc(x2_root, 1)
                act.wait_ge(xn2_ready, t + 1)
                act.dma_start(xn_rows[t * P:(t + 1) * P, :], xn2.rearrange("p k n -> p (k n)")
                              ).then_inc(xn2_stored, 16)
                act.wait_ge(xn2_turned, t + 1)
                act.wait_ge(a2_ready, 1)
                for k in range(KC // 2, KC):
                    act.activation(y_cat[:, k, t * P:(t + 1) * P], ps[:, 4 + k // 4, (k % 4) * P:(k % 4 + 1) * P],
                                   ACT.Identity, bias=mod_col[:, 2, k:k + 1], scale=a2_col[:, k:k + 1]
                                   ).then_inc(h2_act, 1)
            act.wait_ge(neg_max_ready, 1)
            for t in range(T):
                act.activation(c_exp[:, t, 0:G], logits[:, t, 0:G], ACT.Exp, bias=neg_max[:, t:t + 1],
                               accum_out=p_grp[:, t:t + 1]).then_inc(c_exp_ready, 1)
            act.wait_ge(diff_ready, 1)
            act.activation(e_diff, e_diff, ACT.Exp).then_inc(diff_exp, 1)

            def turn_out(dst, bank, used, at, got):
                act.wait_ge(used, at)
                for k in range(KC):
                    last = act.activation(dst[:, k, :], ps[:, bank, k * SLOTS:(k + 1) * SLOTS], ACT.Identity,
                                          bias=mod_col[:, 2, k:k + 1], scale=a2_col[:, k:k + 1])
                last.then_inc(got, 1)

            def silu(dst, bank, used, at, got):
                act.wait_ge(used, at)
                act.activation(dst, ps[:, bank, 0:P], ACT.Silu).then_inc(got, 1)

            def y_out(dst, bank, used, at, got):
                act.wait_ge(used, at)
                act.copy(dst, ps[:, bank, :]).then_inc(got, 1)

            def expert_step(e, b2, first, last):
                if not last:
                    if not first:
                        act.wait_ge(gate_up_done, e)
                    turn_out(xt[:, 1 - b2], 1 - b2, xg_turned, e + 2, xt_ready)
                if not first:
                    act.wait_ge(hid_ready, e)
                silu(gate_act[:, b2, :], 2 + b2, gate_up_done, e + 1, silu_ready)
                if not first:
                    y_out(y_exp[:, 1 - b2, :], 6 - b2, down_done, e, y_ready)
                with extra_blocks(act, e) as n:
                    turn_out(xt_x, b2, ov_turned, n + 1, ov_xt)
                    silu(gate_act_x, 3 - b2, ov_gate_up, n + 1, ov_silu)
                    y_out(y_exp_x, 5 + b2, ov_down, n + 1, ov_y)

            act.wait_ge(routed, 1)
            turn_out(xt[:, 0], 0, xg_turned, 1, xt_ready)
            expert_step(0, 0, True, False)
            for e in (1, 2):
                expert_step(e, e % 2, False, False)
            with act.Fori(0, 4) as i:
                for r in range(RING):
                    e = 3 + RING * i + r
                    act.wait_ge(scattered[r % 2], 16 * (3 * i + r // 2 + 1))
                    expert_step(e, (1 + r) % 2, False, False)
            for e in range(3 + 4 * RING, NE + 1):
                act.wait_ge(scattered[(e - 3) % 2], 16 * ((e - 3) // 2 + 1))
                if e < NE:
                    expert_step(e, e % 2, False, e == NE - 1)
                else:
                    y_out(y_exp[:, 1, :], 6, down_done, NE, y_ready)

            act.wait_ge(down_done, NE)
            act.dma_start(gfin, g_final.rearrange("(o d) -> o d", o=1).to_broadcast([P, D])
                          ).then_inc(gfin_in, 16)
            act.wait_ge(gt2_spread, 1)
            link(act.copy(gt2b[:, 0:HALF], ps[:, 0, :]))
            act.copy(gt2b[:, HALF:D], ps[:, 1, :]).then_inc(gt2_ready, 1)
            for t in range(T):
                act.wait_ge(y_in[t], 32)
                if t >= 2:
                    act.wait_ge(x3_ready, t - 1)
                act.activation(acc[:, t % 2, :], y_back[:, t, 0].rearrange("p h n -> p (h n)"), ACT.Copy,
                               scale=gate_k[:, 0, t:t + 1]).then_inc(y0_scaled, 1)
                act.wait_ge(x3_ready, t + 1)
                link(act.activation(sq_junk, x_sb[:, t, :], ACT.Square, accum_out=stat[:, 4, t:t + 1]))
                act.activation(stat[:, 5, t:t + 1], stat[:, 4, t:t + 1], ACT.Sqrt, bias=eps_col[:],
                               scale=1.0 / D).then_inc(x3_root, 1)

        @block.vector
        def _(dve):
            done = [0]

            def link(ins):
                ins.then_inc(dve_order, 1)
                done[0] += 1
                dve.wait_ge(dve_order, done[0])

            dve.wait_ge(c_act_ready, 1)
            dve.tensor_copy(c_rep, c_col[:].unsqueeze(2).to_broadcast([P, KC, 32])).then_inc(c_rep_ready, 1)
            dve.wait_ge(conv_c_turned, 1)
            dve.tensor_copy(conv_c[:], ps[:, 7, 0:CT * (TAPS + 3)].rearrange("p (i n) -> p i n", i=CT)
                            ).then_inc(conv_c_ready, 1)
            for t in range(T):
                dve.wait_ge(x_root, t + 1)
                link(dve.reciprocal(stat[:, 6, t:t + 1], stat[:, 1, t:t + 1]))
                dve.tensor_scalar(xn[:, t, :], x_sb[:, t, :], stat[:, 6, t:t + 1], None, ALU.mult
                                  ).then_inc(xn_ready, 1)
            dve.wait_ge(xn_turned, 1)
            for k in range(0, KC, 2):
                dve.tensor_copy(h_t[:, k, :], ps[:, k, :]).then_inc(xnt_ready_dve, 1)

            def mod_rows(r, rows, bank):
                dve.wait_ge(ada_used, KC * (r + 1))
                dve.tensor_tensor(rows, ps[:, bank, :], bada_sb[:, r, :], ALU.add).then_inc(mod_rows_ready, 1)

            dve.wait_ge(bada_in, 64)
            mod_rows(0, mod01[:, 0], 4)
            dve.wait_ge(mod_cols_in[0], 64)
            dve.scalar_tensor_tensor(a1_col[:], mod_col[:, 1, :], 1.0, gmix_col[:], ALU.add, ALU.mult
                                     ).then_inc(a1_ready, 1)
            dve.wait_ge(a1_ready, 1)
            dve.wait_ge(xnt_ready_dve, KC // 2)
            for k in range(0, KC, 2):
                dve.tensor_scalar(h_t[:, k, :], h_t[:, k, :], a1_col[:, k:k + 1], mod_col[:, 0, k:k + 1],
                                  ALU.mult, ALU.add).then_inc(h_dve, 1)
            dve.wait_ge(pool_consts, 1)

            def glu(i):
                dve.wait_ge(sig_ready, i + 1)
                dve.tensor_tensor(y_pad[:, i, PAD:PAD + S], ps[:, (2 * i) % 4, :], sig[:, i % 2, :], ALU.mult
                                  ).then_inc(glu_ready, 1)

            steps = [0]

            def conv(pair, first, last):
                for k in range(first, last):
                    for i in pair:
                        if k == 0:
                            dve.wait_ge(glu_ready, i + 1)
                            ins = dve.tensor_scalar(y_cat[:, i, :], y_pad[:, i, 0:S], conv_c[:, i, 0:1],
                                                    conv_c[:, i, TAPS:TAPS + 1], ALU.mult, ALU.add)
                        else:
                            dve.wait_ge(conv_step, steps[0] - 1)
                            ins = dve.scalar_tensor_tensor(y_cat[:, i, :], y_pad[:, i, k:k + S],
                                                           conv_c[:, i, k:k + 1], y_cat[:, i, :],
                                                           ALU.mult, ALU.add)
                        ins.then_inc(conv_step, 1)
                        steps[0] += 1

            dve.wait_ge(conv_c_ready, 1)
            glu(0)
            glu(1)
            conv((0, 1), 0, TAPS // 2)
            glu(2)
            conv((0, 1), TAPS // 2, TAPS)
            glu(3)
            mod_rows(1, mod01[:, 1], 4)
            for j in range(2):
                dve.wait_ge(sgu_w_turned, j + 1)
                dve.tensor_tensor(w_sgu_t[:, 4 * j:4 * j + 4, :],
                                  ps[:, 6 + j, :].rearrange("p (h n) -> p h n", h=4),
                                  tri.unsqueeze(1).to_broadcast([P, 4, P]), ALU.mult).then_inc(sgu_w_ready, 1)
            conv((2, 3), 0, TAPS // 2)
            mod_rows(2, mod2[:], 5)
            conv((2, 3), TAPS // 2, TAPS)
            dve.wait_ge(mod_cols_in[2], 32)
            dve.scalar_tensor_tensor(a2_col[:], mod_col[:, 3, :], 1.0, gffn_col[:], ALU.add, ALU.mult
                                     ).then_inc(a2_ready, 1)

            for t in range(T):
                vt = v_sb[:, t, :].rearrange("p (h d) -> p h d", h=HEADS)
                st = ln_stat[:, t % 2, :]
                dve.wait_ge(gelu_ready, CT + t + 1)
                if t >= 2:
                    dve.wait_ge(v_ready, t - 1)
                link(dve.reduce_sum(st, vt, AX_X))
                link(dve.tensor_scalar(st, st, 1.0 / HD, None, ALU.mult))
                dve.tensor_tensor(vt, vt, st.unsqueeze(2).to_broadcast([P, HEADS, HD]), ALU.subtract
                                  ).then_inc(v_centred, 1)
                dve.wait_ge(v_squared, t + 1)
                dve.wait_ge(v_centred, t + 1)
                dve.reduce_sum(st, v_sq.rearrange("p (h d) -> p h d", h=HEADS), AX_X).then_inc(v_var, 1)
                dve.wait_ge(v_root, t + 1)
                dve.reciprocal(st, st).then_inc(v_rstd, 1)

            for i in range(CT):
                dve.wait_ge(conv_mean, i + 1)
                dve.wait_ge(conv_step, TAPS * CT)
                dve.tensor_tensor(conv_yc[:, i % 2, :], y_cat[:, i, :], ps[:, (5, 7)[i % 2], :], ALU.subtract
                                  ).then_inc(conv_centred, 1)
                dve.wait_ge(conv_root, i + 1)
                link(dve.reciprocal(conv_rs, conv_rs))
                dve.tensor_tensor(y_cat[:, i, :], conv_yc[:, i % 2, :], conv_rs, ALU.mult).then_inc(conv_normed, 1)

            for i in range(CT):
                dve.wait_ge(sgu_mixed, 1)
                bank = ps[:, i, :].rearrange("p (c n) -> p c n", c=T)
                link(dve.tensor_tensor(bank, bank, sgu_b_row[:, i, :].unsqueeze(1).to_broadcast([P, T, P]),
                                       ALU.add))
                dve.tensor_tensor(y_cat[:, CT + i, :], ps[:, i, :], y_cat[:, CT + i, :], ALU.mult
                                  ).then_inc(sgu_out, 1)

            dve.wait_ge(gt1_ready, 1)

            def residual(t):
                for h in range(2):
                    bank = 2 * (t % 2) + h
                    cols = slice(h * HALF, (h + 1) * HALF)
                    dve.wait_ge(mix_done, 2 * t + h + 1)
                    link(dve.tensor_tensor(ps[:, bank, :], ps[:, bank, :], gt1b[:, cols], ALU.mult))
                    dve.tensor_tensor(x_sb[:, t, cols], x_sb[:, t, cols], ps[:, bank, :], ALU.add
                                      ).then_inc(x2_ready, 1)
                dve.wait_ge(x2_root, t + 1)
                dve.wait_ge(x2_ready, 2 * t + 2)
                link(dve.reciprocal(stat[:, 7, t:t + 1], stat[:, 3, t:t + 1]))
                dve.tensor_scalar(xn2, x_sb[:, t, :].rearrange("p (n k) -> p k n", k=KC),
                                  stat[:, 7, t:t + 1], None, ALU.mult).then_inc(xn2_ready, 1)

            def router_in(t):
                dve.wait_ge(xn2_turned, t + 1)
                dve.wait_ge(a2_ready, 1)
                for k in range(KC // 2):
                    dve.tensor_scalar(y_cat[:, k, t * P:(t + 1) * P], ps[:, 4 + k // 4, (k % 4) * P:(k % 4 + 1) * P],
                                      a2_col[:, k:k + 1], mod_col[:, 2, k:k + 1], ALU.mult, ALU.add
                                      ).then_inc(h2_dve, 1)

            def logits_out(t):
                dve.wait_ge(logits_done, t + 1)
                dve.tensor_tensor(logits[:, t, :], ps[:, 6 + t % 2, 0:NR], b_router[:], ALU.add
                                  ).then_inc(logits_ready, 1)

            for t in range(T):
                residual(t)
                if t >= 1:
                    logits_out(t - 1)
                router_in(t)
            logits_out(T - 1)
            dve.wait_ge(logits_ready, T)

            link(dve.memset(coarse8, -3.0e38))
            link(dve.tensor_copy(coarse8[:, :, 0:G], logits[:, :, 0:G]))
            for t in range(T):
                last = dve.max(top_c[:, t, :], coarse8[:, t, :])
            link(last)
            dve.tensor_scalar(neg_max, top_c[:, :, 0], -1.0, None, ALU.mult).then_inc(neg_max_ready, 1)
            for t in range(T):
                last = dve.max_index(top_ci[:, t, :], top_c[:, t, :], coarse8[:, t, :])
            link(last)
            link(dve.tensor_copy(grp, top_ci[:, :, 0]))
            small = slot_iota[:, 0:G].unsqueeze(1).to_broadcast([P, T, G])
            link(dve.tensor_tensor(grp_hot, small, grp.unsqueeze(2).to_broadcast([P, T, G]), ALU.is_equal))
            for t in range(T):
                last = dve.tensor_tensor(fine_m[:, t], logits[:, t, G:NR].rearrange("p (g e) -> p g e", g=G),
                                         grp_hot[:, t, :].unsqueeze(2).to_broadcast([P, G, EG]), ALU.mult)
            link(last)
            link(dve.reduce_sum(fine_s, fine_m.rearrange("p t g e -> p t e g"), AX_X))
            for t in range(T):
                last = dve.max(top_f[:, t, :], fine_s[:, t, :])
            link(last)
            dve.tensor_tensor(e_diff, top_f[:, :, 1], top_f[:, :, 0], ALU.subtract).then_inc(diff_ready, 1)
            for t in range(T):
                last = dve.max_index(top_fi[:, t, :], top_f[:, t, :], fine_s[:, t, :])
            link(last)
            for k in range(2):
                link(dve.tensor_copy(expert_k[:, k, :], top_fi[:, :, k]))
                link(dve.scalar_tensor_tensor(expert_k[:, k, :], grp, float(EG), expert_k[:, k, :],
                                              ALU.mult, ALU.add))
            wide = slot_iota[:, 0:NE].unsqueeze(1).to_broadcast([P, T, NE])
            for k, hot in enumerate((hot0, hot1)):
                link(dve.tensor_tensor(hot, wide, expert_k[:, k, :].unsqueeze(2).to_broadcast([P, T, NE]),
                                       ALU.is_equal))
            link(dve.tensor_tensor(hot0, hot0, hot1, ALU.add))
            link(dve.tensor_copy(hot16, hot0))
            link(dve.memset(pre16[:, 0, :], 0.0))
            for t in range(T):
                last = dve.tensor_tensor(pre16[:, t + 1, :], pre16[:, t, :], hot16[:, t, :], ALU.add)
                if t < T - 1:
                    link(last)
            last.then_inc(hot_ready, 1)
            link(dve.tensor_scalar(stat[:, 0, :], tok_id[:], -float(OOB), None, ALU.add))
            tok_b = stat[:, 0, :].unsqueeze(2).to_broadcast([P, T, NE])
            link(dve.tensor_copy(row_vals[:, :, :, 0], tok_b))
            link(dve.tensor_scalar(hot1, hot1, float(S), None, ALU.mult))
            link(dve.tensor_tensor(row_vals[:, :, :, 1], hot1, tok_b, ALU.add))
            dve.wait_ge(counted, 1)
            link(dve.scalar_tensor_tensor(place, ps[:, 7, 0:T * NE].rearrange("p (t e) -> p t e", t=T), 1.0, hot0,
                                          ALU.add, ALU.mult))
            link(dve.tensor_scalar(place, place, -1.0, None, ALU.add))
            info = block_info[:, 0, :]
            link(dve.tensor_scalar(info, ps[:, 7, T * NE:T * NE + NE], float(SLOTS - 1), None, ALU.add))
            link(dve.tensor_scalar(info, info, 6, None, ALU.logical_shift_right))
            link(dve.tensor_scalar(blocks_f[:, 0, :], info, -1.0, 0.0, ALU.add, ALU.max))
            link(dve.tensor_tensor_scan(blocks_f[:, 1, :], blocks_f[:, 0, :], blocks_f[:, 0, :], 0.0,
                                        ALU.add, ALU.bypass))
            link(dve.tensor_tensor(blocks_f[:, 1, :], blocks_f[:, 1, :], blocks_f[:, 0, :], ALU.subtract))
            link(dve.memset(xg, 0.0))
            link(dve.memset(xg_x, 0.0))
            dve.tensor_copy(block_info[:, 1, :], blocks_f[:, 1, :]).then_inc(routed, 1)
            dve.wait_ge(c_exp_ready, T)
            dve.wait_ge(diff_exp, 1)
            link(dve.reciprocal(p_grp, p_grp))
            link(dve.tensor_scalar(grp, e_diff, 1.0, None, ALU.add))
            link(dve.reciprocal(grp, grp))
            link(dve.tensor_tensor(gate_k[:, 0, :], grp, p_grp, ALU.mult))
            link(dve.tensor_tensor(gate_k[:, 1, :], gate_k[:, 0, :], e_diff, ALU.mult))

            iota_b = slot_iota[:].unsqueeze(1).to_broadcast([P, T, P])

            def pick(e, dst, got):
                dve.tensor_tensor(dst, iota_b, place[:, :, bass.ds(e, 1)].to_broadcast([P, T, P]),
                                  ALU.is_equal).then_inc(got, 1)

            def rows(dst, used, at, got):
                dve.wait_ge(used, at)
                dve.tensor_scalar(dst, ps[:, 7, 0:2], row_off[:], None, ALU.add).then_inc(got, 1)

            def hidden(dst, act_in, bank, used, at, got):
                dve.wait_ge(used, at)
                dve.tensor_tensor(dst, act_in, ps[:, bank, P:2 * P], ALU.mult).then_inc(got, 1)

            def hidden_t(dst, used, at, got):
                dve.wait_ge(used, at)
                dve.tensor_copy(dst, ps[:, 4, 0:P]).then_inc(got, 1)

            def step(e, b2, b6, first, pick_next, rows_next):
                if pick_next:
                    dve.wait_ge(rows_found, e + AHEAD)
                    pick(e + AHEAD + 1, picks[:, b2], picks_ready)
                if rows_next:
                    rows(row_idx[:, b6, :], rows_found, e + AHEAD + 1, rows_ready)
                if not first:
                    dve.wait_ge(hid_turned, e - 1)
                hidden(hid[:, b2, :], gate_act[:, b2, :], 2 + b2, silu_ready, e + 1, hid_ready)
                if not first:
                    dve.wait_ge(down_done, e - 1)
                hidden_t(hid_t[:, b2, :], hid_turned, e + 1, hid_t_ready)
                with extra_blocks(dve, e) as n:
                    past = place[:, :, bass.ds(e, 1)]
                    dve.tensor_scalar(past, past, -float(SLOTS), None, ALU.add).then_inc(ov_place, 1)
                    dve.wait_ge(ov_place, n + 1)
                    pick(e, picks_x, ov_picks)
                    dve.wait_ge(ov_free, n + 1)
                    rows(row_idx_x, ov_found, n + 1, ov_rows)
                    hidden(hid_x, gate_act_x, 3 - b2, ov_silu, n + 1, ov_hid)
                    hidden_t(hid_t_x, ov_hid_turned, n + 1, ov_hid_t)

            dve.wait_ge(routed, 1)
            for e in range(AHEAD + 1):
                if e >= 2:
                    dve.wait_ge(rows_found, e - 1)
                pick(e, picks[:, e % 2], picks_ready)
                if e >= 1:
                    rows(row_idx[:, e - 1, :], rows_found, e, rows_ready)
            for e in range(3):
                step(e, e % 2, (e + AHEAD) % RING, e < 2, True, True)
            with dve.Fori(0, 4) as i:
                for r in range(RING):
                    dve.wait_ge(scattered[r % 2], 16 * (3 * i + r // 2 + 1))
                    step(3 + RING * i + r, (3 + r) % 2, (3 + r + AHEAD) % RING, False, True, True)
            for e in range(3 + 4 * RING, NE):
                if e + AHEAD < NE:
                    dve.wait_ge(scattered[(e - 3) % 2], 16 * ((e - 3) // 2 + 1))
                step(e, e % 2, (e + AHEAD) % RING, False, e + AHEAD + 1 < NE, e + AHEAD < NE)

            dve.wait_ge(gt2_ready, 1)
            dve.wait_ge(gfin_in, 16)
            for t in range(T):
                a = acc[:, t % 2, :]
                dve.wait_ge(y0_scaled, t + 1)
                link(dve.scalar_tensor_tensor(a, y_back[:, t, 1].rearrange("p h n -> p (h n)"),
                                              gate_k[:, 1, t:t + 1], a, ALU.mult, ALU.add))
                link(dve.tensor_tensor(a, a, gt2b, ALU.mult))
                dve.tensor_tensor(x_sb[:, t, :], x_sb[:, t, :], a, ALU.add).then_inc(x3_ready, 1)
                dve.wait_ge(x3_root, t + 1)
                link(dve.reciprocal(stat[:, 6, t:t + 1], stat[:, 5, t:t + 1]))
                dve.scalar_tensor_tensor(x_sb[:, t, :], x_sb[:, t, :], stat[:, 6, t:t + 1], gfin,
                                         ALU.mult, ALU.mult).then_inc(out_ready, 1)

        @block.tensor
        def _(pe):
            pe.wait_ge(pool_consts, 1)
            pe.wait_ge(consts_in, 16 * 15)
            for i in range(CT):
                last = pe.transpose(ps[:, 7, i * (TAPS + 3):(i + 1) * (TAPS + 3)], conv_raw[:, i * P:(i + 1) * P],
                                    ident[0:TAPS + 3, 0:TAPS + 3])
            last.then_inc(conv_c_turned, 1)
            pe.wait_ge(conv_c_ready, 1)
            for t in range(T):
                pe.wait_ge(xn_ready, t + 1)
                for k in range(KC):
                    last = pe.transpose(ps[:, k, t * P:(t + 1) * P],
                                        xn[:, t, :].rearrange("p (n k) -> p k n", k=KC)[:, k, :], ident[:])
            last.then_inc(xn_turned, 1)

            def ada(n, bank):
                r, k = n // KC, n % KC
                pe.wait_ge(ada_in[n % ADA_BUFS], 16 * (n // ADA_BUFS + 1))
                for q in range(4):
                    last = pe.matmul(ps[32 * q:32 * q + 32, bank, :], c_rep[:, k, :],
                                     ada_buf(n % ADA_BUFS)[:, q * HALF:(q + 1) * HALF],
                                     start=(k == 0), stop=(k == KC - 1))
                last.then_inc(ada_used, 1)

            pe.wait_ge(c_rep_ready, 1)
            pe.wait_ge(xnt_ready_dve, 3)
            for n in range(KC):
                ada(n, 4)

            def z_tile(n):
                bank = n % 4
                if n >= 4:
                    if n < 2 * CT + 4:
                        old = n - 4
                        if old < 2 * CT:
                            pe.wait_ge(sig_ready if old % 2 else glu_ready, old // 2 + 1)
                    if n - 4 >= 2 * CT:
                        pe.wait_ge(gelu_ready, n - 4 - 2 * CT + 1)
                if n < 2 * CT:
                    q, w, cols = (n % 2), (win_a, win_g)[n % 2], n // 2
                elif n < 3 * CT:
                    q, w, cols = 2, win_u, n - 2 * CT
                else:
                    q, w, cols = 3, win_v, n - 3 * CT
                pe.wait_ge(win_in[q], 16)
                for k in range(KC):
                    if n == 0:
                        pe.wait_ge(h_act if k % 2 else h_dve, k // 2 + 1)
                    c128 = slice(cols * P, (cols + 1) * P)
                    if q < 3:
                        last = pe.matmul(ps[:, bank, :], w[:, k, c128], h_t[:, k, :],
                                         start=(k == 0), stop=(k == KC - 1))
                    else:
                        last = pe.matmul(ps[:, bank, :], h_t[:, k, c128], w[:, k, :],
                                         start=(k == 0), stop=(k == KC - 1))
                last.then_inc(z_done, 1)

            for n in range(16):
                z_tile(n)
                if 4 <= n < 12:
                    if n == 4:
                        pe.wait_ge(mod_rows_ready, 1)
                    for m in range(2):
                        u = KC + 2 * (n - 4) + m
                        ada(u, 4 if u < 2 * KC else 5)
                if n == 8:
                    for j in range(2):
                        for h in range(4):
                            last = pe.transpose(ps[:, 6 + j, h * P:(h + 1) * P], w_sgu_raw[:, 4 * j + h, :], ident[:])
                        last.then_inc(sgu_w_turned, 1)
                if n == 11:
                    pe.wait_ge(sgu_w_ready, 2)
                    pe.wait_ge(mod_rows_ready, 2)
                    for j in range(2):
                        last = pe.matmul(ps[:, 6 + j, :], ones[32 * j:32 * j + 1, :],
                                         mod01[32 * j:32 * j + 1, 1, :], start=True, stop=True)
                    last.then_inc(gt1_spread, 1)

            def conv_stat(i, rhs, bank, got):
                pe.matmul(ps[:, bank, :], group_mean[:], rhs, start=True, stop=True).then_inc(got, 1)

            pe.wait_ge(conv_step, TAPS * CT)
            pe.wait_ge(gt1_ready, 1)
            pe.wait_ge(mod_rows_ready, 3)
            conv_stat(0, y_cat[:, 0, :], 5, conv_mean)
            conv_stat(1, y_cat[:, 1, :], 7, conv_mean)
            pe.wait_ge(gelu_ready, CT + T)
            pe.wait_ge(sgu_w_ready, 2)
            for ch in range(T):
                pe.wait_ge(v_ready, ch + 1)
                for h in range(HEADS):
                    last = pe.matmul(ps[HD * (h % 2):HD * (h % 2) + HD, h // 2, ch * P:(ch + 1) * P],
                                     v_sb[:, ch, h * HD:(h + 1) * HD], w_sgu_t[:, h, :], start=True, stop=True,
                                     skip_group_check=True)
            last.then_inc(sgu_mixed, 1)
            for i in range(CT):
                pe.wait_ge(conv_squared, i + 1)
                conv_stat(i, conv_sq, (6, 4)[i % 2], conv_var)
                if i + 2 < CT:
                    pe.wait_ge(conv_centred, i + 1)
                    conv_stat(i + 2, y_cat[:, i + 2, :], (5, 7)[i % 2], conv_mean)

            def mix(t):
                for h in range(2):
                    bank = 2 * (t % 2) + h
                    if t >= 2:
                        pe.wait_ge(x2_ready, 2 * (t - 2) + h + 1)
                    for m in range(2 * CT):
                        last = pe.matmul(ps[:, bank, :], y_cat[:, m, t * P:(t + 1) * P],
                                         wout_sb[:, m, h * HALF:(h + 1) * HALF], start=(m == 0),
                                         stop=(m == 2 * CT - 1))
                    last.then_inc(mix_done, 1)

            def route(t):
                pe.wait_ge(xn2_ready, t + 1)
                if t >= 1:
                    pe.wait_ge(h2_act, KC // 2 * t)
                    pe.wait_ge(h2_dve, KC // 2 * t)
                for k in range(KC):
                    last = pe.transpose(ps[:, 4 + k // 4, (k % 4) * P:(k % 4 + 1) * P], xn2[:, k, :], ident[:])
                last.then_inc(xn2_turned, 1)
                if t >= 2:
                    pe.wait_ge(logits_ready, t - 1)
                pe.wait_ge(h2_act, KC // 2 * (t + 1))
                pe.wait_ge(h2_dve, KC // 2 * (t + 1))
                for k in range(KC):
                    last = pe.matmul(ps[:, 6 + t % 2, 0:NR], y_cat[:, k, t * P:(t + 1) * P],
                                     w_router[:, k, :], start=(k == 0), stop=(k == KC - 1), skip_group_check=True)
                last.then_inc(logits_done, 1)

            pe.wait_ge(conv_out, CT)
            pe.wait_ge(sgu_out, CT)
            pe.wait_ge(wout_in, 16)
            pe.wait_ge(router_packed, 1)
            mix(0)
            mix(1)
            for t in range(T):
                route(t)
                if t + 2 < T:
                    mix(t + 2)
            pe.wait_ge(hot_ready, 1)
            pe.matmul(ps[:, 7, 0:T * NE], before16[:], hot16.rearrange("p t e -> p (t e)"), start=True, stop=False,
                      skip_group_check=True)
            pe.matmul(ps[:, 7, 0:T * NE], ones16[:], pre16[:, 0:T].rearrange("p t e -> p (t e)"), start=False,
                      stop=True, skip_group_check=True)
            pe.matmul(ps[:, 7, T * NE:T * NE + NE], ones16[:], pre16[:, T], start=False, stop=True,
                      skip_group_check=True).then_inc(counted, 1)

            def find_rows(e, src, got):
                for t in range(T):
                    last = pe.matmul(ps[:, 7, 0:2], src[:, t, :],
                                     row_vals[:, t, bass.ds(e, 1), :].rearrange("p o v -> p (o v)"),
                                     start=(t == 0), stop=(t == T - 1), skip_group_check=True)
                last.then_inc(got, 1)

            def turn(src, bank, got):
                pe.sem_inc(tokens_here, 1)
                for k in range(KC):
                    last = pe.transpose(ps[:, bank, k * SLOTS:(k + 1) * SLOTS], src[0:SLOTS, k, :],
                                        ident[0:SLOTS, 0:SLOTS])
                last.then_inc(got, 1)

            def gate_up(src, bank, slot, got):
                w = ring[:, slot * SLOT_W:slot * SLOT_W + GU_W].rearrange("p (g k f) -> p g k f", g=2, k=KC)
                for k in range(KC):
                    for j in range(2):
                        last = pe.matmul(ps[SLOTS * j:SLOTS * (j + 1), bank, 0:2 * P].rearrange(
                            "p (g f) -> p g f", g=2), src[:, k, :], w[:, :, k, j * P:(j + 1) * P],
                            start=(k == 0), stop=(k == KC - 1), skip_group_check=True)
                last.then_inc(got, 1)

            def turn_hidden(src, got):
                pe.transpose(ps[:, 4, 0:P], src, ident[:]).then_inc(got, 1)

            def down(src, bank, slot, got):
                w = ring[:, slot * SLOT_W + GU_W:(slot + 1) * SLOT_W].rearrange("p (c n) -> p c n", c=FC)
                for f in range(FC):
                    for j in range(2):
                        last = pe.matmul(ps[SLOTS * j:SLOTS * (j + 1), bank, :], src[:, f * SLOTS:(f + 1) * SLOTS],
                                         w[:, f, j * HALF:(j + 1) * HALF], start=(f == 0), stop=(f == FC - 1),
                                         skip_group_check=True)
                last.then_inc(got, 1)

            def step(e, b2, slot, b3, tokens, weights, first, y_free, find, nxt):
                if find:
                    pe.wait_ge(picks_ready, e + AHEAD + 1)
                    pe.wait_ge(rows_ready, e + AHEAD)
                    find_rows(e + AHEAD, picks[:, 1 - b2], rows_found)
                if nxt:
                    if not first:
                        pe.wait_ge(xt_ready, e)
                    pe.wait_ge(gathered[b3], tokens)
                    turn(xg[:, b3], 1 - b2, xg_turned)
                pe.wait_ge(xt_ready, e + 1)
                if not first:
                    pe.wait_ge(hid_ready, e)
                pe.wait_ge(expert_in[slot], weights)
                gate_up(xt[:, b2], 2 + b2, slot, gate_up_done)
                if not first:
                    if y_free:
                        pe.wait_ge(y_ready, e - 2)
                    pe.wait_ge(hid_t_ready, e)
                    down(hid_t[:, 1 - b2], 6 - b2, (slot - 1) % RING, down_done)
                pe.wait_ge(hid_ready, e + 1)
                turn_hidden(hid[:, b2, :], hid_turned)
                with extra_blocks(pe, e) as n:
                    pe.wait_ge(hid_t_ready, e + 1)
                    if find:
                        pe.wait_ge(rows_ready, e + AHEAD + 1)
                    if y_free or b2 == 0 and not first:
                        pe.wait_ge(y_ready, e - 1)
                    pe.wait_ge(ov_picks, n + 1)
                    find_rows(e, picks_x, ov_found)
                    pe.wait_ge(ov_gathered, 16 * n + 16)
                    turn(xg_x, b2, ov_turned)
                    pe.wait_ge(ov_xt, n + 1)
                    gate_up(xt_x, 3 - b2, slot, ov_gate_up)
                    pe.wait_ge(ov_hid, n + 1)
                    turn_hidden(hid_x, ov_hid_turned)
                    pe.wait_ge(ov_hid_t, n + 1)
                    down(hid_t_x, 5 + b2, slot, ov_down)
                    pe.wait_ge(ov_y, n + 1)
                    pe.sem_inc(ov_passed, 1)

            pe.wait_ge(routed, 1)
            for e in range(AHEAD):
                pe.wait_ge(picks_ready, e + 1)
                if e:
                    pe.wait_ge(rows_ready, e)
                find_rows(e, picks[:, e % 2], rows_found)
            pe.wait_ge(gathered[0], 16)
            turn(xg[:, 0], 0, xg_turned)
            for e in range(3):
                step(e, e % 2, e, (e + 1) % XG, 16 * ((e + 1) // XG + 1), 48, e == 0, False, True, True)
            with pe.Fori(0, 4) as i:
                for r in range(RING):
                    s = (3 + r) % RING
                    step(3 + RING * i + r, (1 + r) % 2, s, (4 + r) % XG, 16 * (2 * i + (4 + r) // XG + 1),
                         48 * (i + (3 + r) // RING + 1), False, True, True, True)
            for e in range(3 + 4 * RING, NE):
                step(e, e % 2, e % RING, (e + 1) % XG, 16 * ((e + 1) // XG + 1), 48 * (e // RING + 1),
                     False, True, e + AHEAD < NE, e + 1 < NE)
            pe.wait_ge(y_ready, NE - 2)
            pe.wait_ge(hid_t_ready, NE)
            down(hid_t[:, (NE - 1) % 2], 6, (NE - 1) % RING, down_done)

            for j in range(2):
                q = 32 * (2 + j)
                last = pe.matmul(ps[:, j, :], ones[q:q + 1, :], mod2[q:q + 1, :], start=True, stop=True)
            last.then_inc(gt2_spread, 1)


_INS = ["x", "c", "w_ada", "b_ada", "g_mix", "w_in", "conv_w", "conv_b", "conv_ln_g", "conv_ln_b",
        "sgu_ln_g", "sgu_ln_b", "sgu_w", "sgu_b", "w_out", "g_ffn", "w_coarse", "b_coarse",
        "w_fine", "b_fine", "w_gate", "w_up", "w_down", "g_final"]


def kernel(**inputs):
    import numpy as _np
    import concourse.bacc as _bacc
    from concourse import mybir as _mybir
    from concourse.bass_utils import run_bass_kernel_spmd as _run

    nc = _bacc.Bacc("TRN2", target_bir_lowering=False, num_devices=1, dynamic_dma_scratch_size=8192)
    arrays, args = {}, []
    for name in _INS:
        a = _np.ascontiguousarray(inputs[name])
        arrays[f"in_{name}"] = a
        args.append(nc.dram_tensor(f"in_{name}", a.shape, _mybir.dt.from_np(a.dtype), kind="ExternalInput").ap())
    shape = inputs["x"].shape
    out = nc.dram_tensor("out", shape, _mybir.dt.float32, kind="ExternalOutput").ap()
    build_block(nc, *args, out)
    r = _run(nc, [arrays], core_ids=[0])
    return r.results[0]["out"]
```

```python
from contextlib import ExitStack, contextmanager

import concourse.bass as bass
from concourse import mybir

P = 128
F32 = mybir.dt.float32
F16 = mybir.dt.float16
I32 = mybir.dt.int32
U32 = mybir.dt.uint32
ALU = mybir.AluOpType
ACT = mybir.ActivationFunctionType
AX_X = mybir.AxisListType.X


def build_block(nc, x, c, w_ada, b_ada, g_mix, w_in, conv_w, conv_b, conv_ln_g, conv_ln_b,
                sgu_ln_g, sgu_ln_b, sgu_w, sgu_b, w_out, g_ffn, w_coarse, b_coarse,
                w_fine, b_fine, w_gate, w_up, w_down, g_final, out):
    S, D = x.shape[1], x.shape[2]
    KC = D // P
    T = S // P
    CW = conv_w.shape[2]
    CT = CW // P
    TAPS = conv_w.shape[1]
    PAD = TAPS - 1
    HEADS = sgu_w.shape[1]
    HD = CW // HEADS
    G = w_coarse.shape[2]
    EG = w_fine.shape[3]
    NE = G * EG
    DE = w_gate.shape[3]
    FC = DE // P
    NV = TAPS + 5 + 2
    HALF = D // 2
    SLOTS = 64
    NR = G + NE
    EPS = 1e-6
    RING = 6
    N_CONST = 6
    SLOT_W = 2 * KC * DE + FC * D
    GU_W = 2 * KC * DE
    ADA_BUFS = 5
    ROUND = 4 * HALF
    ROUNDS = w_ada.shape[2] // ROUND
    AHEAD = 4
    OOB = 2 * S * 2
    XG = 4
    ROWS = 12
    assert (S, D, CW, HD, NE, DE, OOB) == (512, 1024, 512, 64, 32, 256, 2048)

    xn_rows = nc.dram_tensor("xn_rows", [S, D], F32).ap()
    y_rows = nc.dram_tensor("y_rows", [2 * 2 * S, HALF], F32).ap()

    with ExitStack() as ctx:
        def sb(name, shape, dt=F32):
            return ctx.enter_context(nc.sbuf_tensor(name, shape, dt))

        def sem(name):
            return ctx.enter_context(nc.semaphore(name))

        ps = ctx.enter_context(nc.psum_tensor("ps", [P, 8, HALF], F32))

        ring = sb("ring", [P, RING * SLOT_W])
        work = sb("work", [P, 12288])
        x_sb = sb("x_sb", [P, T, D])
        mod2 = sb("mod2", [P, HALF])
        ident = sb("ident", [P, P])
        ones = sb("ones", [P, P])
        group_mean = sb("group_mean", [P, P])
        slot_iota = sb("slot_iota", [P, P])
        before16 = sb("before16", [P, P], F16)
        ones16 = sb("ones16", [P, P], F16)
        w_router = sb("w_router", [P, KC, NR])
        conv_c = sb("conv_c", [P, CT, NV])
        b_router = sb("b_router", [P, NR])
        c_col = sb("c_col", [P, KC])
        logits = sb("logits", [P, T, NR])
        gffn_col = sb("gffn_col", [P, KC])
        mod1_nat = sb("mod1_nat", [P, 2, KC])
        mod_col = sb("mod_col", [P, 2, KC])
        a1_col = sb("a1_col", [P, KC])
        a2_col = sb("a2_col", [P, KC])
        eps_col = sb("eps_col", [P, 1])
        row_off = sb("row_off", [P, 2])
        tok_id = sb("tok_id", [P, T])
        stat = sb("stat", [P, 8, T])

        def ring_at(off, n):
            return ring[:, off:off + n]

        def ada_buf(b):
            return ring_at(b * ROUND, ROUND)
        o = ADA_BUFS * ROUND
        bada_sb = ring_at(o, ROUNDS * HALF).rearrange("p (r n) -> p r n", r=ROUNDS)
        c_rep = ring_at(o + ROUNDS * HALF, KC * 32).rearrange("p (k m) -> p k m", k=KC)
        o = 2 * SLOT_W
        win_u = ring_at(o, KC * CW).rearrange("p (k n) -> p k n", k=KC)
        win_v = ring_at(o + 4096, KC * CW).rearrange("p (k n) -> p k n", k=KC)
        h_t = ring_at(o + 8192, KC * S).rearrange("p (k n) -> p k n", k=KC)
        o = 4 * SLOT_W
        win_a = ring_at(o, KC * CW).rearrange("p (k n) -> p k n", k=KC)
        win_g = ring_at(o + 4096, KC * CW).rearrange("p (k n) -> p k n", k=KC)
        y_pad = ring_at(o + 8192, CT * (S + PAD)).rearrange("p (i n) -> p i n", i=CT)
        v_sb = ring_at(o, T * CW).rearrange("p (t n) -> p t n", t=T)
        v_t = ring_at(o + 2048, CT * S).rearrange("p (i n) -> p i n", i=CT)
        w_sgu_t = ring_at(o + 4096, HEADS * P).rearrange("p (h n) -> p h n", h=HEADS)
        ln_sq = ring_at(o + 5120, S)
        sgu_b_row = ring_at(o + 6144, CT * P).rearrange("p (i n) -> p i n", i=CT)
        ln_yc = ring_at(o + 6656, 2 * S).rearrange("p (b n) -> p b n", b=2)
        ln_root = ring_at(o + 7680, S)
        xn2 = ring_at(o + 8192, 2 * D).rearrange("p (b k n) -> p b k n", b=2, k=KC)
        gt1b = ring_at(o + 11264, D)

        wout_sb = work[:, 0:8192].rearrange("p (m n) -> p m n", m=KC)
        y_cat = work[:, 8192:12288].rearrange("p (m n) -> p m n", m=KC)
        xn = work[:, 0:4096].rearrange("p (t n) -> p t n", t=T)
        sig = work[:, 4096:5120].rearrange("p (b n) -> p b n", b=2)
        w_sgu_raw = work[:, 5120:6144].rearrange("p (h n) -> p h n", h=HEADS)
        conv_raw = work[0:NV, 6144:6656]
        fine_raw = work[:, 6656:6912].rearrange("p (g k e) -> p g k e", g=G, k=KC)
        coarse_raw = work[:, 6912:6944].rearrange("p (k g) -> p k g", k=KC)

        tri = work[:, 6944:7072]
        mod01 = work[:, 0:2 * HALF].rearrange("p (r n) -> p r n", r=2)

        xg = work[:, 0:XG * D].rearrange("p (b k n) -> p b k n", b=XG, k=KC)
        o = [XG * D]

        def rt(n, dt=F32):
            a = work[:, o[0]:o[0] + n]
            o[0] += n
            return a if dt == F32 else a.bitcast(dt)
        coarse8 = rt(T * 8).rearrange("p (t n) -> p t n", t=T)
        top_c = rt(T * 8).rearrange("p (t n) -> p t n", t=T)
        top_ci = rt(T * 8, U32).rearrange("p (t n) -> p t n", t=T)
        c_exp = rt(T * 8).rearrange("p (t n) -> p t n", t=T)
        neg_max = rt(T)
        p_grp = rt(T)
        grp = rt(T)
        grp_hot = rt(T * G).rearrange("p (t g) -> p t g", t=T)
        fine_m = rt(T * NE).rearrange("p (t g e) -> p t g e", t=T, g=G)
        fine_s = rt(T * EG).rearrange("p (t e) -> p t e", t=T)
        top_f = rt(T * 8).rearrange("p (t n) -> p t n", t=T)
        top_fi = rt(T * 8, U32).rearrange("p (t n) -> p t n", t=T)
        gate_k = rt(2 * T).rearrange("p (k t) -> p k t", k=2)
        expert_k = rt(2 * T).rearrange("p (k t) -> p k t", k=2)
        e_diff = rt(T)
        hot0 = rt(T * NE).rearrange("p (t e) -> p t e", t=T)
        hot1 = rt(T * NE).rearrange("p (t e) -> p t e", t=T)
        place = rt(T * NE).rearrange("p (t e) -> p t e", t=T)
        hot16 = rt(T * NE // 2, F16).rearrange("p (t e) -> p t e", t=T)
        row_vals = rt(T * NE, F16).rearrange("p (t e v) -> p t e v", t=T, v=2)
        row_idx = rt(2 * ROWS, U32).rearrange("p (b v) -> p b v", v=2)
        blocks_f = rt(2 * NE).rearrange("p (v e) -> p v e", v=2)
        block_info = rt(2 * NE, I32).rearrange("p (v e) -> p v e", v=2)
        row_idx_x = rt(2, U32)
        assert o[0] <= 8192
        xt = rt(D).rearrange("p (b k n) -> p b k n", b=2, k=KC)
        gate_act = rt(2 * P).rearrange("p (b n) -> p b n", b=2)
        hid = rt(2 * P).rearrange("p (b n) -> p b n", b=2)
        hid_t = rt(2 * P).rearrange("p (b n) -> p b n", b=2)
        y_exp = rt(2 * HALF).rearrange("p (b n) -> p b n", b=2)
        picks = rt(T * P, F16).rearrange("p (b t n) -> p b t n", b=2, t=T)
        xg_x = rt(D).rearrange("p (k n) -> p k n", k=KC)
        xt_x = rt(KC * SLOTS).rearrange("p (k n) -> p k n", k=KC)
        gate_act_x, hid_x, hid_t_x = rt(P), rt(P), rt(P)
        y_exp_x = rt(HALF)
        gt2_exp = rt(HALF)
        picks_x = rt(T * P // 2, F16).rearrange("p (t n) -> p t n", t=T)
        assert o[0] <= 12288


        y_back = ring_at(0, T * 2 * D).rearrange("p (t k h n) -> p t k h n", t=T, k=2, h=2)
        acc = ring_at(T * 2 * D, T * D).rearrange("p (t n) -> p t n", t=T)
        gfin = ring_at(T * 3 * D, D)

        x_in = [sem(f"x_in{t}") for t in range(T)]
        c_in = sem("c_in")
        rows_in = sem("rows_in")
        consts_in = sem("consts_in")
        norm_ready = sem("norm_ready")
        bada_in = sem("bada_in")
        ada_in = [sem(f"ada_in{b}") for b in range(ADA_BUFS)]
        win_in = [sem(f"win_in_{n}") for n in "aguv"]
        sgu_rows_in = sem("sgu_rows_in")
        wout_in = sem("wout_in")
        expert_in = [sem(f"expert_in{r}") for r in range(RING)]
        pool_consts = sem("pool_consts")
        pool_order = sem("pool_order")
        bada_zero = sem("bada_zero")
        router_packed = sem("router_packed")
        act_order = sem("act_order")
        dve_order = sem("dve_order")
        c_act_ready = sem("c_act_ready")
        c_rep_ready = sem("c_rep_ready")
        x_root = sem("x_root")
        xn_ready = sem("xn_ready")
        conv_c_turned = sem("conv_c_turned")
        conv_c_ready = sem("conv_c_ready")
        xn_turned = sem("xn_turned")
        xnt_ready_dve = sem("xnt_ready_dve")
        xnt_ready_act = sem("xnt_ready_act")
        mod0_turned = sem("mod0_turned")
        mod1_ready = sem("mod1_ready")
        ada_used = sem("ada_used")
        mod_rows_ready = sem("mod_rows_ready")
        mod_cols_in = [sem(f"mod_cols_in{r}") for r in range(2)]
        a1_ready = sem("a1_ready")
        h_dve = sem("h_dve")
        h_act = sem("h_act")
        z_done = sem("z_done")
        sig_ready = sem("sig_ready")
        glu_ready = sem("glu_ready")
        gelu_ready = sem("gelu_ready")
        conv_step = sem("conv_step")
        sgu_w_turned = sem("sgu_w_turned")
        sgu_w_ready = sem("sgu_w_ready")
        gt1_spread = sem("gt1_spread")
        gt1_ready = sem("gt1_ready")
        ln_mean = sem("ln_mean")
        ln_centred = sem("ln_centred")
        ln_squared = sem("ln_squared")
        ln_var = sem("ln_var")
        ln_rooted = sem("ln_rooted")
        ln_rstd = sem("ln_rstd")
        ln_normed = sem("ln_normed")
        v_scaled = sem("v_scaled")
        v_turned = sem("v_turned")
        v_ready = sem("v_ready")
        conv_out = sem("conv_out")
        sgu_mixed = sem("sgu_mixed")
        sgu_out = sem("sgu_out")
        mix_done = sem("mix_done")
        x2_ready = sem("x2_ready")
        x2_squared = sem("x2_squared")
        x2_root = sem("x2_root")
        xn2_ready = sem("xn2_ready")
        xn2_stored = [sem(f"xn2_stored{b}") for b in range(2)]
        xn2_turned = sem("xn2_turned")
        a2_ready = sem("a2_ready")
        h2_dve = sem("h2_dve")
        h2_act = sem("h2_act")
        logits_done = sem("logits_done")
        logits_ready = sem("logits_ready")
        neg_max_ready = sem("neg_max_ready")
        c_exp_ready = sem("c_exp_ready")
        diff_ready = sem("diff_ready")
        diff_exp = sem("diff_exp")
        hot_ready = sem("hot_ready")
        counted = sem("counted")
        rows_from = sem("rows_from")
        places_ready = sem("places_ready")
        routed = sem("routed")
        picks_ready = sem("picks_ready")
        rows_found = sem("rows_found")
        rows_ready = sem("rows_ready")
        gathered = [sem(f"gathered{b}") for b in range(XG)]
        xg_turned = sem("xg_turned")
        xt_ready = sem("xt_ready")
        gate_up_done = sem("gate_up_done")
        silu_ready = sem("silu_ready")
        hid_ready = sem("hid_ready")
        hid_turned = sem("hid_turned")
        hid_t_ready = sem("hid_t_ready")
        down_done = sem("down_done")
        y_ready = sem("y_ready")
        scattered = [sem(f"scattered{b}") for b in range(2)]
        ov_place = sem("ov_place")
        ov_free = sem("ov_free")
        ov_picks = sem("ov_picks")
        ov_found = sem("ov_found")
        ov_rows = sem("ov_rows")
        ov_gathered = sem("ov_gathered")
        ov_turned = sem("ov_turned")
        ov_xt = sem("ov_xt")
        ov_gate_up = sem("ov_gate_up")
        ov_silu = sem("ov_silu")
        ov_hid = sem("ov_hid")
        ov_hid_turned = sem("ov_hid_turned")
        ov_hid_t = sem("ov_hid_t")
        ov_down = sem("ov_down")
        ov_y = sem("ov_y")
        ov_scattered = sem("ov_scattered")
        ov_passed = sem("ov_passed")
        pool_go = sem("pool_go")
        tokens_here = sem("tokens_here")
        all_scattered = sem("all_scattered")
        gfin_in = sem("gfin_in")
        gt2_spread = sem("gt2_spread")
        gt2_ready = sem("gt2_ready")
        y_in = [sem(f"y_in{t}") for t in range(T)]
        x3_ready = sem("x3_ready")
        x3_squared = sem("x3_squared")
        x3_root = sem("x3_root")
        x3_rstd = sem("x3_rstd")
        x3_normed = sem("x3_normed")
        out_ready = sem("out_ready")
        out_stored = sem("out_stored")

        x_rows = x.rearrange("b (t p) d -> (b t) p d", p=P)
        out_rows = out.rearrange("b (t p) d -> (b t) p d", p=P)
        ada_v = w_ada.rearrange("l (p k) n -> (l p) k n", k=KC)
        win_dram = w_in.rearrange("l (k p) n -> (l p) k n", k=KC)
        wout_dram = w_out.rearrange("l (m p) n -> (l p) m n", p=P)
        gate_dram = w_gate.rearrange("l e (p k) f -> (l e) p (k f)", k=KC)
        up_dram = w_up.rearrange("l e (p k) f -> (l e) p (k f)", k=KC)
        down_dram = w_down.rearrange("l e (c p) n -> (l e) p c n", p=P)

        def col_of(v):
            return v.rearrange("l (p k) -> (l p) k", k=KC)

        def load_expert(eng, e, slot, done):
            base = ring[:, slot * SLOT_W:(slot + 1) * SLOT_W]
            eng.dma_start(base[:, 0:GU_W // 2], gate_dram[e]).then_inc(done, 16)
            eng.dma_start(base[:, GU_W // 2:GU_W], up_dram[e]).then_inc(done, 16)
            eng.dma_start(base[:, GU_W:SLOT_W].rearrange("p (c n) -> p c n", c=FC),
                          down_dram[e]).then_inc(done, 16)

        block = ctx.enter_context(nc.Block())

        @contextmanager
        def extra_blocks(eng, e):
            blocks = eng.value_load(block_info[0:1, 0, bass.ds(e, 1)], min_val=0, max_val=S // SLOTS)
            with eng.If(blocks > 1):
                before = eng.value_load(block_info[0:1, 1, bass.ds(e, 1)], min_val=0, max_val=2 * S // SLOTS)
                with eng.Fori(1, blocks) as j:
                    yield before + j - 1

        @block.sync
        def _(sp):
            for t in range(T):
                sp.dma_start(x_sb[:, t, :], x_rows[t]).then_inc(x_in[t], 16)

            def ada_unit(n):
                b = n % ADA_BUFS
                if n >= ADA_BUFS:
                    sp.wait_ge(ada_used, n - ADA_BUFS + 1)
                r, k = n // KC, n % KC
                sp.dma_start(ada_buf(b), ada_v[:, k, r * ROUND:(r + 1) * ROUND]).then_inc(ada_in[b], 16)

            for n in range(KC):
                ada_unit(n)
            for q, dst, first in ((0, win_a, 0), (1, win_g, CW), (3, win_v, 3 * CW), (2, win_u, 2 * CW)):
                sp.dma_start(dst, win_dram[:, :, first:first + CW]).then_inc(win_in[q], 16)
            for n in range(KC, ROUNDS * KC):
                ada_unit(n)
            sp.wait_ge(z_done, 2 * CT)
            for h in range(HEADS):
                rows = slice(HD * (h % 2), HD * (h % 2) + HD)
                sp.dma_start(sgu_b_row[rows, h // 2, :], sgu_b[0, h:h + 1, :].to_broadcast([HD, P])
                             ).then_inc(sgu_rows_in, 16)
            sp.wait_ge(glu_ready, CT)
            sp.wait_ge(sgu_w_ready, 2)
            sp.wait_ge(router_packed, 1)
            sp.wait_ge(gt1_spread, 2)
            sp.wait_ge(mod_cols_in[0], 32)
            sp.dma_start(wout_sb, wout_dram).then_inc(wout_in, 16)

            sp.wait_ge(ada_used, ROUNDS * KC)
            sp.wait_ge(mod_rows_ready, ROUNDS)
            load_expert(sp, 0, 0, expert_in[0])
            load_expert(sp, 1, 1, expert_in[1])
            sp.wait_ge(z_done, 2 * CT + CT + T)
            load_expert(sp, 2, 2, expert_in[2])
            load_expert(sp, 3, 3, expert_in[3])
            sp.wait_ge(conv_out, CT)
            sp.wait_ge(sgu_out, CT)
            load_expert(sp, 4, 4, expert_in[4])
            sp.wait_ge(xn2_turned, T)
            for b in range(2):
                sp.wait_ge(xn2_stored[b], 16 * T // 2)
            sp.wait_ge(x2_ready, 2 * T)
            load_expert(sp, 5, 5, expert_in[5])

            with sp.Fori(0, (NE - RING) // RING) as i:
                for r in range(RING):
                    e = RING + RING * i + r
                    sp.wait_ge(down_done, RING * i + r + 1)
                    load_expert(sp, e, r, expert_in[r])
            for e in range(NE - NE % RING, NE):
                sp.wait_ge(down_done, e - RING + 1)
                load_expert(sp, e, e % RING, expert_in[e % RING])

            sp.wait_ge(all_scattered, 1)
            back = y_rows.rearrange("(h k t p) n -> t k p h n", h=2, k=2, p=P)
            for t in range(T):
                for k in range(2):
                    sp.dma_start(y_back[:, t, k], back[t, k]).then_inc(y_in[t], 16)
            sp.dma_start(gfin, g_final.rearrange("(o d) -> o d", o=1).to_broadcast([P, D])
                         ).then_inc(gfin_in, 16)
            for t in range(T):
                sp.wait_ge(out_ready, t + 1)
                sp.dma_start(out_rows[t], acc[:, t, :]).then_inc(out_stored, 16)
            sp.wait_ge(out_stored, 16 * T)

        @block.gpsimd
        def _(pool):
            done = [0]

            def link(ins):
                ins.then_inc(pool_order, 1)
                done[0] += 1
                pool.wait_ge(pool_order, done[0])

            link(pool.memset(eps_col[:], EPS))
            link(pool.memset(ident[:], 1.0))
            pool.affine_select(out=ident[:], in_=ident[:], compare_op=ALU.is_equal, fill=0.0, base=0,
                               pattern=[[1, P]], channel_multiplier=-1).then_inc(norm_ready, 1)
            pool.memset(bada_sb, 0.0).then_inc(bada_zero, 1)
            pool.wait_ge(bada_zero, 1)
            bada_v = b_ada.rearrange("l (r q n) -> l r q n", q=4, n=HALF)
            for q in range(4):
                pool.dma_start(bada_sb[32 * q:32 * q + 1], bada_v[:, :, q, :]).then_inc(bada_in, 16)
            link(pool.memset(ones[:], 1.0))
            link(pool.memset(group_mean[:], 0.0))
            link(pool.memset(group_mean[0:HD, 0:HD], 1.0 / HD))
            link(pool.memset(group_mean[HD:P, HD:P], 1.0 / HD))
            link(pool.memset(tri, 1.0))
            link(pool.affine_select(out=tri, in_=tri, compare_op=ALU.is_ge, fill=0.0, base=0,
                                    pattern=[[1, P]], channel_multiplier=-1))
            link(pool.memset(ones16[:], 1.0))
            link(pool.affine_select(out=before16[:], in_=ones16[:], compare_op=ALU.is_gt, fill=0.0, base=0,
                                    pattern=[[1, P]], channel_multiplier=-1))
            slot_i = slot_iota[:].bitcast(I32)
            link(pool.iota(slot_i, pattern=[[0, 2], [1, SLOTS]], base=0, channel_multiplier=0))
            link(pool.tensor_copy(slot_iota[:], slot_i))
            tok_i = tok_id[:].bitcast(I32)
            link(pool.iota(tok_i, pattern=[[P, T]], base=-OOB, channel_multiplier=1))
            link(pool.tensor_copy(tok_id[:], tok_i))
            link(pool.memset(row_off[:], float(OOB)))
            link(pool.memset(row_off[SLOTS:P, 1:2], float(OOB + 2 * S)))
            pool.memset(y_pad[:, :, 0:PAD], 0.0).then_inc(pool_consts, 1)
            pool.wait_ge(consts_in, 16 * N_CONST)
            link(pool.tensor_copy(w_router[:, :, 0:G], coarse_raw))
            for g in range(G):
                copied = pool.tensor_copy(w_router[:, :, G + g * EG:G + (g + 1) * EG], fine_raw[:, g])
                if g < G - 1:
                    link(copied)
            copied.then_inc(router_packed, 1)

            pool.wait_ge(mix_done, 2 * T)
            pool.tensor_copy(row_vals[:, :, :, 0], tok_id[:].unsqueeze(2).to_broadcast([P, T, NE])
                             ).then_inc(rows_from, 1)
            link(pool.memset(xg, 0.0))
            pool.wait_ge(logits_done, T)
            link(pool.memset(xg_x, 0.0))

            def gather(e, b, r, wait_buffer):
                pool.wait_ge(rows_ready, e + 1)
                if wait_buffer:
                    pool.wait_ge(xg_turned, e - XG + 1)
                pool.sem_inc(pool_go, 1)
                pool.indirect_dma_start(
                    xg[0:SLOTS, b].rearrange("p k n -> p (k n)"), None, xn_rows,
                    bass.IndirectOffsetOnAxis(row_idx[0:SLOTS, r, 0:1], 0),
                    bounds_check=S - 1, oob_is_err=False).then_inc(gathered[b], 16)

            def scatter(e, b2, r):
                pool.wait_ge(y_ready, e + 1)
                pool.sem_inc(pool_go, 1)
                pool.indirect_dma_start(
                    y_rows, bass.IndirectOffsetOnAxis(row_idx[:, r, 1:2], 0), y_exp[:, b2], None,
                    bounds_check=4 * S - 1, oob_is_err=False).then_inc(scattered[b2], 16)

            for b in range(2):
                pool.wait_ge(xn2_stored[b], 16 * T // 2)
            for e in range(AHEAD + 1):
                gather(e, e % XG, e % ROWS, e >= XG)
            pool.sem_inc(ov_free, 1)
            pool.wait_ge(routed, 1)

            def extra(e):
                with extra_blocks(pool, e) as n:
                    pool.wait_ge(ov_rows, n + 1)
                    pool.sem_inc(pool_go, 1)
                    pool.indirect_dma_start(
                        xg_x[0:SLOTS].rearrange("p k n -> p (k n)"), None, xn_rows,
                        bass.IndirectOffsetOnAxis(row_idx_x[0:SLOTS, 0:1], 0),
                        bounds_check=S - 1, oob_is_err=False).then_inc(ov_gathered, 16)
                    pool.wait_ge(ov_y, n + 1)
                    pool.sem_inc(pool_go, 1)
                    pool.indirect_dma_start(
                        y_rows, bass.IndirectOffsetOnAxis(row_idx_x[:, 1:2], 0), y_exp_x, None,
                        bounds_check=4 * S - 1, oob_is_err=False).then_inc(ov_scattered, 16)
                    pool.wait_ge(ov_scattered, 16 * n + 16)
                    pool.sem_inc(ov_free, 1)

            for e in range(2):
                if e:
                    gather(e + AHEAD, (e + AHEAD) % XG, (e + AHEAD) % ROWS, e + AHEAD >= XG)
                extra(e)
                scatter(e, e % 2, e % ROWS)
            with pool.Fori(0, 2) as i:
                for r in range(ROWS):
                    e = 2 + ROWS * i + r
                    gather(e + AHEAD, (2 + r + AHEAD) % XG, (2 + r + AHEAD) % ROWS, True)
                    extra(e)
                    scatter(e, r % 2, (2 + r) % ROWS)
            for e in range(2 + 2 * ROWS, NE):
                if e + AHEAD < NE:
                    gather(e + AHEAD, (e + AHEAD) % XG, (e + AHEAD) % ROWS, True)
                extra(e)
                scatter(e, e % 2, e % ROWS)
            for b in range(2):
                pool.wait_ge(scattered[b], 16 * NE // 2)
            pool.sem_inc(all_scattered, 1)

        @block.scalar
        def _(act):
            done = [0]

            def link(ins):
                ins.then_inc(act_order, 1)
                done[0] += 1
                act.wait_ge(act_order, done[0])

            act.dma_start(c_col[:], col_of(c)).then_inc(c_in, 16)
            flat = "l g d -> l (g d)"
            for row, src in (
                (0, conv_w[0]), (TAPS, conv_b), (TAPS + 1, conv_ln_g.rearrange(flat)),
                (TAPS + 2, conv_ln_b.rearrange(flat)), (TAPS + 3, sgu_ln_g.rearrange(flat)),
                (TAPS + 4, sgu_ln_b.rearrange(flat)), (TAPS + 5, g_mix.rearrange("l (h n) -> (l h) n", h=2)),
            ):
                act.dma_start(conv_raw[row:row + src.shape[0]], src).then_inc(rows_in, 16)
            for dst, src in (
                (w_sgu_raw, sgu_w[0].rearrange("h t s -> t h s")),
                (gffn_col[:], col_of(g_ffn)),
                (coarse_raw, w_coarse[0].rearrange("(p k) g -> p k g", k=KC)),
                (fine_raw, w_fine[0].rearrange("g (p k) e -> p g k e", k=KC)),
                (b_router[:, 0:G], b_coarse.to_broadcast([P, G])),
                (b_router[:, G:NR], b_fine.rearrange("l g e -> l (g e)").to_broadcast([P, NE])),
            ):
                act.dma_start(dst, src).then_inc(consts_in, 16)
            act.wait_ge(c_in, 16)
            act.activation(c_col[:], c_col[:], ACT.Silu).then_inc(c_act_ready, 1)
            act.wait_ge(norm_ready, 1)
            for t in range(T):
                act.wait_ge(x_in[t], 16)
                link(act.activation(xn[:, t, :], x_sb[:, t, :], ACT.Square, accum_out=stat[:, 0, t:t + 1]))
                act.activation(stat[:, 1, t:t + 1], stat[:, 0, t:t + 1], ACT.Sqrt, bias=eps_col[:],
                               scale=1.0 / D).then_inc(x_root, 1)
            act.wait_ge(xn_turned, 1)
            for k in range(1, KC, 2):
                act.copy(h_t[:, k, :], ps[:, k, :]).then_inc(xnt_ready_act, 1)

            def mod_cols(r, rows, pairs):
                act.wait_ge(mod_rows_ready, r + 1)
                for q, v in pairs:
                    part = slice((q % 2) * P // 2, (q % 2) * P // 2 + P // 2)
                    act.dma_start(mod_col[part, v, :], rows[32 * q:32 * q + 1, :].rearrange(
                        "o (p k) -> o p k", k=KC)).then_inc(mod_cols_in[r - 1], 16)

            act.wait_ge(a1_ready, 1)
            act.wait_ge(xnt_ready_act, KC // 2)
            for k in range(1, KC, 2):
                act.activation(h_t[:, k, :], h_t[:, k, :], ACT.Identity, bias=mod1_nat[:, 0, k:k + 1],
                               scale=a1_col[:, k:k + 1]).then_inc(h_act, 1)

            for i in range(CT):
                act.wait_ge(z_done, 2 * i + 2)
                if i >= 2:
                    act.wait_ge(glu_ready, i - 1)
                act.activation(sig[:, i % 2, :], ps[:, (2 * i + 1) % 4, :], ACT.Sigmoid).then_inc(sig_ready, 1)

            def ln_square(n):
                act.wait_ge(ln_centred, n + 1)
                if n >= 1:
                    act.wait_ge(ln_var, n)
                act.activation(ln_sq, ln_yc[:, n % 2, :], ACT.Square).then_inc(ln_squared, 1)

            def ln_sqrt(n):
                act.wait_ge(ln_var, n + 1)
                if n >= 1:
                    act.wait_ge(ln_normed, n)
                act.activation(ln_root, ps[:, 6, :], ACT.Sqrt, bias=eps_col[:]).then_inc(ln_rooted, 1)

            def v_scale(n):
                act.wait_ge(ln_normed, n + 1)
                act.activation(v_t[:, n, :], v_t[:, n, :], ACT.Identity, bias=conv_c[:, n, TAPS + 4:TAPS + 5],
                               scale=conv_c[:, n, TAPS + 3:TAPS + 4]).then_inc(v_scaled, 1)

            def v_out(n):
                act.wait_ge(v_turned, n + 1)
                act.copy(v_sb[:, :, n * P:(n + 1) * P], ps[:, 7, :].rearrange("p (t n) -> p t n", t=T)
                         ).then_inc(v_ready, 1)

            for n in range(2 * CT, 4 * CT):
                act.wait_ge(z_done, n + 1)
                dst = v_t[:, n - 2 * CT, :] if n < 3 * CT else y_cat[:, n - 2 * CT, :]
                act.activation(dst, ps[:, n % 4, :], ACT.Gelu_apprx_tanh).then_inc(gelu_ready, 1)
                if n == 2 * CT:
                    mod_cols(1, mod01[:, 1], [(q, 0) for q in (2, 3)])
                if n >= 10:
                    ln_sqrt(n - 10)
                if 10 <= n < 14:
                    v_scale(n - 10)
                if n >= 9:
                    ln_square(n - 9)
                if 9 <= n < 11:
                    act.wait_ge(gt1_spread, n - 8)
                    act.copy(gt1b[:, (n - 9) * HALF:(n - 8) * HALF], ps[:, 7, :]).then_inc(gt1_ready, 1)
                if 11 <= n < 15:
                    v_out(n - 11)
                if n == 13:
                    mod_cols(2, mod2[:], [(q, 1) for q in (0, 1)])
            for n in range(6, 8):
                ln_sqrt(n)
                if n + 1 < 8:
                    ln_square(n + 1)
            for i in range(CT):
                act.wait_ge(ln_normed, CT + i + 1)
                act.activation(y_cat[:, i, :], y_cat[:, i, :], ACT.Silu, bias=conv_c[:, i, TAPS + 2:TAPS + 3],
                               scale=conv_c[:, i, TAPS + 1:TAPS + 2]).then_inc(conv_out, 1)

            def norm2(t):
                row = xn2[:, t % 2].rearrange("p k n -> p (k n)")
                act.wait_ge(x2_ready, 2 * t + 2)
                if t >= 2:
                    act.wait_ge(xn2_stored[t % 2], 16)
                    act.wait_ge(xn2_turned, t - 1)
                link(act.activation(row, x_sb[:, t, :], ACT.Square, accum_out=stat[:, 2, t:t + 1]))
                act.activation(stat[:, 3, t:t + 1], stat[:, 2, t:t + 1], ACT.Sqrt, bias=eps_col[:],
                               scale=1.0 / D).then_inc(x2_root, 1)
                act.wait_ge(xn2_ready, t + 1)
                act.dma_start(xn_rows[t * P:(t + 1) * P, :], row).then_inc(xn2_stored[t % 2], 16)

            def h2_out(t):
                act.wait_ge(xn2_turned, t + 1)
                act.wait_ge(a2_ready, 1)
                for k in range(KC // 2, KC):
                    act.activation(y_cat[:, k, t * P:(t + 1) * P], ps[:, 4 + k // 4, (k % 4) * P:(k % 4 + 1) * P],
                                   ACT.Identity, bias=mod_col[:, 0, k:k + 1], scale=a2_col[:, k:k + 1]
                                   ).then_inc(h2_act, 1)

            norm2(0)
            for t in range(T):
                if t + 1 < T:
                    norm2(t + 1)
                h2_out(t)
            act.wait_ge(neg_max_ready, 1)
            for t in range(T):
                act.activation(c_exp[:, t, 0:G], logits[:, t, 0:G], ACT.Exp, bias=neg_max[:, t:t + 1],
                               accum_out=p_grp[:, t:t + 1]).then_inc(c_exp_ready, 1)
            act.wait_ge(diff_ready, 1)
            act.activation(e_diff, e_diff, ACT.Exp).then_inc(diff_exp, 1)
            act.wait_ge(gt2_spread, 1)
            act.copy(gt2_exp, ps[:, 0, :]).then_inc(gt2_ready, 1)

            def turn_out(dst, bank, used, at, got):
                act.wait_ge(used, at)
                for k in range(KC):
                    last = act.activation(dst[:, k, :], ps[:, bank, k * SLOTS:(k + 1) * SLOTS], ACT.Identity,
                                          bias=mod_col[:, 0, k:k + 1], scale=a2_col[:, k:k + 1])
                last.then_inc(got, 1)

            def silu(dst, bank, used, at, got):
                act.wait_ge(used, at)
                act.activation(dst, ps[:, bank, 0:P], ACT.Silu).then_inc(got, 1)

            def expert_step(e, b2, first, last):
                if not last:
                    if not first:
                        act.wait_ge(gate_up_done, e)
                    turn_out(xt[:, 1 - b2], 1 - b2, xg_turned, e + 2, xt_ready)
                if not first:
                    act.wait_ge(hid_ready, e)
                silu(gate_act[:, b2, :], 2 + b2, gate_up_done, e + 1, silu_ready)
                with extra_blocks(act, e) as n:
                    turn_out(xt_x, b2, ov_turned, n + 1, ov_xt)
                    silu(gate_act_x, 3 - b2, ov_gate_up, n + 1, ov_silu)

            turn_out(xt[:, 0], 0, xg_turned, 1, xt_ready)
            act.wait_ge(routed, 1)
            expert_step(0, 0, True, False)
            with act.Fori(0, 5) as i:
                for r in range(RING):
                    expert_step(1 + RING * i + r, (1 + r) % 2, False, False)
            expert_step(NE - 1, (NE - 1) % 2, False, True)

            for t in range(T):
                act.wait_ge(x3_ready, 2 * t + 2)
                link(act.activation(acc[:, t, :], x_sb[:, t, :], ACT.Square, accum_out=stat[:, 4, t:t + 1]))
                act.activation(stat[:, 5, t:t + 1], stat[:, 4, t:t + 1], ACT.Sqrt, bias=eps_col[:],
                               scale=1.0 / D).then_inc(x3_root, 1)
                act.wait_ge(x3_rstd, t + 1)
                act.activation(acc[:, t, :], x_sb[:, t, :], ACT.Copy, scale=stat[:, 6, t:t + 1]
                               ).then_inc(x3_normed, 1)

        @block.vector
        def _(dve):
            done = [0]

            def link(ins):
                ins.then_inc(dve_order, 1)
                done[0] += 1
                dve.wait_ge(dve_order, done[0])

            dve.wait_ge(c_act_ready, 1)
            dve.tensor_copy(c_rep, c_col[:].unsqueeze(2).to_broadcast([P, KC, 32])).then_inc(c_rep_ready, 1)
            for t in range(T):
                dve.wait_ge(x_root, t + 1)
                link(dve.reciprocal(stat[:, 6, t:t + 1], stat[:, 1, t:t + 1]))
                dve.tensor_scalar(xn[:, t, :], x_sb[:, t, :], stat[:, 6, t:t + 1], None, ALU.mult
                                  ).then_inc(xn_ready, 1)
            dve.wait_ge(xn_turned, 1)
            for k in range(0, KC, 2):
                dve.tensor_copy(h_t[:, k, :], ps[:, k, :]).then_inc(xnt_ready_dve, 1)

            def mod_rows(r, rows, bank):
                dve.wait_ge(ada_used, KC * (r + 1))
                dve.tensor_tensor(rows, ps[:, bank, :], bada_sb[:, r, :], ALU.add).then_inc(mod_rows_ready, 1)

            dve.wait_ge(bada_in, 64)
            mod_rows(0, mod01[:, 0], 4)
            dve.wait_ge(conv_c_turned, 1)
            dve.tensor_copy(conv_c[:], ps[:, 7, 0:CT * NV].rearrange("p (i n) -> p i n", i=CT)
                            ).then_inc(conv_c_ready, 1)
            dve.wait_ge(mod0_turned, 1)
            dve.tensor_copy(mod1_nat[:].rearrange("p v (h j) -> p (v h) j", h=2),
                            ps[:, 5, :].rearrange("p (j q m) -> p q j m", j=4, q=4)[:, :, :, 0]
                            ).then_inc(mod1_ready, 1)
            dve.wait_ge(mod1_ready, 1)
            dve.wait_ge(conv_c_ready, 1)
            dve.scalar_tensor_tensor(a1_col[:].rearrange("p (h j) -> p h j", h=2),
                                     mod1_nat[:, 1, :].rearrange("p (h j) -> p h j", h=2), 1.0,
                                     conv_c[:, :, TAPS + 5:TAPS + 7].rearrange("p j h -> p h j"),
                                     ALU.add, ALU.mult).then_inc(a1_ready, 1)
            dve.wait_ge(a1_ready, 1)
            dve.wait_ge(xnt_ready_dve, KC // 2)
            for k in range(0, KC, 2):
                dve.tensor_scalar(h_t[:, k, :], h_t[:, k, :], a1_col[:, k:k + 1], mod1_nat[:, 0, k:k + 1],
                                  ALU.mult, ALU.add).then_inc(h_dve, 1)
            dve.wait_ge(pool_consts, 1)

            def glu(i):
                dve.wait_ge(sig_ready, i + 1)
                dve.tensor_tensor(y_pad[:, i, PAD:PAD + S], ps[:, (2 * i) % 4, :], sig[:, i % 2, :], ALU.mult
                                  ).then_inc(glu_ready, 1)

            steps, tap_at = [0], {}

            def conv(pair, first, last):
                for k in range(first, last):
                    for i in pair:
                        if k == 0:
                            dve.wait_ge(glu_ready, i + 1)
                            ins = dve.tensor_scalar(y_cat[:, i, :], y_pad[:, i, 0:S], conv_c[:, i, 0:1],
                                                    conv_c[:, i, TAPS:TAPS + 1], ALU.mult, ALU.add)
                        else:
                            dve.wait_ge(conv_step, tap_at[i])
                            ins = dve.scalar_tensor_tensor(y_cat[:, i, :], y_pad[:, i, k:k + S],
                                                           conv_c[:, i, k:k + 1], y_cat[:, i, :],
                                                           ALU.mult, ALU.add)
                        ins.then_inc(conv_step, 1)
                        steps[0] += 1
                        tap_at[i] = steps[0]

            def ln_centre(n):
                src = v_t[:, n, :] if n < CT else y_cat[:, n - CT, :]
                dve.wait_ge(ln_mean, n + 1)
                dve.tensor_tensor(ln_yc[:, n % 2, :], src, ps[:, 5, :], ALU.subtract).then_inc(ln_centred, 1)

            def ln_norm(n):
                dst = v_t[:, n, :] if n < CT else y_cat[:, n - CT, :]
                dve.wait_ge(ln_rooted, n + 1)
                dve.reciprocal(ln_root, ln_root).then_inc(ln_rstd, 1)
                dve.wait_ge(ln_rstd, n + 1)
                dve.tensor_tensor(dst, ln_yc[:, n % 2, :], ln_root, ALU.mult).then_inc(ln_normed, 1)

            def sgu_weights(j):
                dve.wait_ge(sgu_w_turned, j + 1)
                dve.tensor_tensor(w_sgu_t[:, 4 * j:4 * j + 4, :],
                                  ps[:, 7, :].rearrange("p (h n) -> p h n", h=4),
                                  tri.unsqueeze(1).to_broadcast([P, 4, P]), ALU.mult).then_inc(sgu_w_ready, 1)

            glu(0)
            conv((0,), 0, 18)
            glu(1)
            conv((1,), 0, 18)
            glu(2)
            conv((0, 1), 18, 25)
            mod_rows(1, mod01[:, 1], 4)
            conv((0, 1), 25, TAPS)
            glu(3)
            conv((2, 3), 0, 3)
            sgu_weights(0)
            conv((2, 3), 3, 10)
            sgu_weights(1)
            conv((2, 3), 10, 13)
            for n in range(CT):
                ln_centre(n)
                conv((2, 3), 13 + 4 * n, 17 + 4 * n)
                if n == 2:
                    mod_rows(2, mod2[:], 4)
                ln_norm(n)
            conv((2, 3), 29, TAPS)
            dve.wait_ge(conv_step, TAPS * CT)
            for n in range(CT, CT + 2):
                ln_centre(n)
                ln_norm(n)
            ln_centre(CT + 2)
            for i in range(CT):
                dve.wait_ge(sgu_mixed, 1)
                dve.wait_ge(sgu_rows_in, 16 * HEADS)
                bank = ps[:, i, :].rearrange("p (c n) -> p c n", c=T)
                link(dve.tensor_tensor(bank, bank, sgu_b_row[:, i, :].unsqueeze(1).to_broadcast([P, T, P]),
                                       ALU.add))
                dve.tensor_tensor(y_cat[:, CT + i, :], ps[:, i, :], y_cat[:, CT + i, :], ALU.mult
                                  ).then_inc(sgu_out, 1)

            ln_norm(CT + 2)
            ln_centre(CT + 3)
            ln_norm(CT + 3)
            dve.wait_ge(mod_cols_in[0], 32)
            dve.wait_ge(mod_cols_in[1], 32)
            dve.scalar_tensor_tensor(a2_col[:], mod_col[:, 1, :], 1.0, gffn_col[:], ALU.add, ALU.mult
                                     ).then_inc(a2_ready, 1)

            dve.wait_ge(gt1_ready, 2)

            def residual(t):
                for h in range(2):
                    bank = 2 * (t % 2) + h
                    cols = slice(h * HALF, (h + 1) * HALF)
                    dve.wait_ge(mix_done, 2 * t + h + 1)
                    link(dve.tensor_tensor(ps[:, bank, :], ps[:, bank, :], gt1b[:, cols], ALU.mult))
                    dve.tensor_tensor(x_sb[:, t, cols], x_sb[:, t, cols], ps[:, bank, :], ALU.add
                                      ).then_inc(x2_ready, 1)
                dve.wait_ge(x2_root, t + 1)
                dve.wait_ge(x2_ready, 2 * t + 2)
                link(dve.reciprocal(stat[:, 7, t:t + 1], stat[:, 3, t:t + 1]))
                dve.tensor_scalar(xn2[:, t % 2], x_sb[:, t, :].rearrange("p (n k) -> p k n", k=KC),
                                  stat[:, 7, t:t + 1], None, ALU.mult).then_inc(xn2_ready, 1)

            def router_in(t):
                dve.wait_ge(xn2_turned, t + 1)
                dve.wait_ge(a2_ready, 1)
                for k in range(KC // 2):
                    dve.tensor_scalar(y_cat[:, k, t * P:(t + 1) * P], ps[:, 4 + k // 4, (k % 4) * P:(k % 4 + 1) * P],
                                      a2_col[:, k:k + 1], mod_col[:, 0, k:k + 1], ALU.mult, ALU.add
                                      ).then_inc(h2_dve, 1)

            def logits_out(t):
                dve.wait_ge(logits_done, t + 1)
                dve.tensor_tensor(logits[:, t, :], ps[:, 6 + t % 2, 0:NR], b_router[:], ALU.add
                                  ).then_inc(logits_ready, 1)

            residual(0)
            for t in range(T):
                if t + 1 < T:
                    residual(t + 1)
                if t >= 1:
                    logits_out(t - 1)
                router_in(t)
            logits_out(T - 1)
            dve.wait_ge(logits_ready, T)

            link(dve.memset(coarse8, -3.0e38))
            link(dve.tensor_copy(coarse8[:, :, 0:G], logits[:, :, 0:G]))
            for t in range(T):
                last = dve.max(top_c[:, t, :], coarse8[:, t, :])
            link(last)
            dve.tensor_scalar(neg_max, top_c[:, :, 0], -1.0, None, ALU.mult).then_inc(neg_max_ready, 1)
            for t in range(T):
                last = dve.max_index(top_ci[:, t, :], top_c[:, t, :], coarse8[:, t, :])
            link(last)
            small = slot_iota[:, 0:G].unsqueeze(1).to_broadcast([P, T, G])
            link(dve.tensor_tensor(grp_hot, small, top_ci[:, :, 0:1].to_broadcast([P, T, G]), ALU.is_equal))
            for t in range(T):
                last = dve.tensor_tensor(fine_m[:, t], logits[:, t, G:NR].rearrange("p (g e) -> p g e", g=G),
                                         grp_hot[:, t, :].unsqueeze(2).to_broadcast([P, G, EG]), ALU.mult)
            link(last)
            link(dve.reduce_sum(fine_s, fine_m.rearrange("p t g e -> p t e g"), AX_X))
            for t in range(T):
                last = dve.max(top_f[:, t, :], fine_s[:, t, :])
            link(last)
            dve.tensor_tensor(e_diff, top_f[:, :, 1], top_f[:, :, 0], ALU.subtract).then_inc(diff_ready, 1)
            for t in range(T):
                last = dve.max_index(top_fi[:, t, :], top_f[:, t, :], fine_s[:, t, :])
            link(last)
            for k in range(2):
                last = dve.scalar_tensor_tensor(expert_k[:, k, :], top_ci[:, :, 0], float(EG), top_fi[:, :, k],
                                                ALU.mult, ALU.add)
            link(last)
            wide = slot_iota[:, 0:NE].unsqueeze(1).to_broadcast([P, T, NE])
            for k, hot in enumerate((hot0, hot1)):
                last = dve.tensor_tensor(hot, wide, expert_k[:, k, :].unsqueeze(2).to_broadcast([P, T, NE]),
                                         ALU.is_equal)
            link(last)
            dve.tensor_tensor(hot16, hot0, hot1, ALU.add).then_inc(hot_ready, 1)
            dve.wait_ge(rows_from, 1)
            dve.scalar_tensor_tensor(row_vals[:, :, :, 1], hot1, float(S), row_vals[:, :, :, 0], ALU.mult, ALU.add
                                     ).then_inc(dve_order, 1)
            done[0] += 1
            dve.wait_ge(counted, 1)
            dve.wait_ge(hot_ready, 1)
            link(dve.scalar_tensor_tensor(place, ps[:, 7, 0:T * NE].rearrange("p (t e) -> p t e", t=T), 1.0, hot16,
                                          ALU.add, ALU.mult))
            link(dve.tensor_scalar(place, place, -1.0, None, ALU.add))
            dve.tensor_copy(blocks_f[:, 1, :], ps[:, 7, T * NE:T * NE + NE]).then_inc(places_ready, 1)

            iota_b = slot_iota[:].unsqueeze(1).to_broadcast([P, T, P])

            def pick(e, dst, got):
                dve.tensor_tensor(dst, iota_b, place[:, :, bass.ds(e, 1)].to_broadcast([P, T, P]),
                                  ALU.is_equal).then_inc(got, 1)

            def rows(dst, used, at, got):
                dve.wait_ge(used, at)
                dve.tensor_tensor(dst, ps[:, 7, 0:2], row_off[:], ALU.add).then_inc(got, 1)

            def hidden(dst, act_in, bank, used, at, got):
                dve.wait_ge(used, at)
                dve.tensor_tensor(dst, act_in, ps[:, bank, P:2 * P], ALU.mult).then_inc(got, 1)

            def hidden_t(dst, used, at, got):
                dve.wait_ge(used, at)
                dve.tensor_copy(dst, ps[:, 4, 0:P]).then_inc(got, 1)

            def y_out(dst, bank, used, at, got):
                dve.wait_ge(used, at)
                dve.tensor_tensor(dst, ps[:, bank, :], gt2_exp, ALU.mult).then_inc(got, 1)

            def step(e, b2, r, first, pick_next, rows_next, scat):
                if pick_next:
                    dve.wait_ge(rows_found, e + AHEAD)
                    pick(e + AHEAD + 1, picks[:, 1 - b2], picks_ready)
                if rows_next:
                    rows(row_idx[:, r, :], rows_found, e + AHEAD + 1, rows_ready)
                if first < 2:
                    dve.wait_ge(hid_turned, e - 1)
                hidden(hid[:, b2, :], gate_act[:, b2, :], 2 + b2, silu_ready, e + 1, hid_ready)
                if first < 3:
                    if scat is not None:
                        dve.wait_ge(*scat)
                    y_out(y_exp[:, 1 - b2, :], 6 - b2, down_done, e, y_ready)
                hidden_t(hid_t[:, b2, :], hid_turned, e + 1, hid_t_ready)
                with extra_blocks(dve, e) as n:
                    past = place[:, :, bass.ds(e, 1)]
                    dve.tensor_scalar(past, past, -float(SLOTS), None, ALU.add).then_inc(ov_place, 1)
                    dve.wait_ge(ov_place, n + 1)
                    pick(e, picks_x, ov_picks)
                    dve.wait_ge(ov_free, n + 1)
                    rows(row_idx_x, ov_found, n + 1, ov_rows)
                    hidden(hid_x, gate_act_x, 3 - b2, ov_silu, n + 1, ov_hid)
                    hidden_t(hid_t_x, ov_hid_turned, n + 1, ov_hid_t)
                    y_out(y_exp_x, 5 + b2, ov_down, n + 1, ov_y)

            for e in range(AHEAD + 1):
                if e >= 2:
                    dve.wait_ge(rows_found, e - 1)
                pick(e, picks[:, e % 2], picks_ready)
                if e >= 1:
                    rows(row_idx[:, e - 1, :], rows_found, e, rows_ready)
            info = block_info[:, 0, :]
            dve.wait_ge(places_ready, 1)
            link(dve.tensor_scalar(info, blocks_f[:, 1, :], float(SLOTS - 1), None, ALU.add))
            link(dve.tensor_scalar(info, info, 6, None, ALU.logical_shift_right))
            link(dve.tensor_scalar(blocks_f[:, 0, :], info, -1.0, 0.0, ALU.add, ALU.max))
            link(dve.tensor_tensor_scan(blocks_f[:, 1, :], blocks_f[:, 0, :], blocks_f[:, 0, :], 0.0,
                                        ALU.add, ALU.bypass))
            dve.tensor_tensor(block_info[:, 1, :], blocks_f[:, 1, :], blocks_f[:, 0, :], ALU.subtract
                              ).then_inc(routed, 1)
            dve.wait_ge(c_exp_ready, T)
            dve.wait_ge(diff_exp, 1)
            link(dve.reciprocal(p_grp, p_grp))
            link(dve.tensor_scalar(grp, e_diff, 1.0, None, ALU.add))
            link(dve.reciprocal(grp, grp))
            link(dve.tensor_tensor(gate_k[:, 0, :], grp, p_grp, ALU.mult))
            link(dve.tensor_tensor(gate_k[:, 1, :], gate_k[:, 0, :], e_diff, ALU.mult))
            dve.wait_ge(routed, 1)
            dve.wait_ge(gt2_ready, 1)
            for e in range(3):
                step(e, e % 2, (e + AHEAD) % ROWS, 3 - e, True, True, None)
            with dve.Fori(0, 2) as i:
                for r in range(ROWS):
                    step(3 + ROWS * i + r, (3 + r) % 2, (3 + r + AHEAD) % ROWS, 0, True, True,
                         (scattered[r % 2], 16 * (ROWS // 2 * i + r // 2 + 1)))
            for e in range(3 + 2 * ROWS, NE):
                step(e, e % 2, (e + AHEAD) % ROWS, 0, e + AHEAD + 1 < NE, e + AHEAD < NE,
                     (scattered[(e - 3) % 2], 16 * ((e - 3) // 2 + 1)))
            dve.wait_ge(scattered[(NE - 3) % 2], 16 * ((NE - 3) // 2 + 1))
            y_out(y_exp[:, (NE - 1) % 2, :], 6, down_done, NE, y_ready)

            def gated(t):
                for k in range(2):
                    dve.wait_ge(y_in[t], 32)
                    if k:
                        dve.wait_ge(x3_ready, 2 * t + 1)
                    dve.scalar_tensor_tensor(x_sb[:, t, :], y_back[:, t, k].rearrange("p h n -> p (h n)"),
                                             gate_k[:, k, t:t + 1], x_sb[:, t, :], ALU.mult, ALU.add
                                             ).then_inc(x3_ready, 1)

            def rstd3(t):
                dve.wait_ge(x3_root, t + 1)
                dve.reciprocal(stat[:, 6, t:t + 1], stat[:, 5, t:t + 1]).then_inc(x3_rstd, 1)

            def final(t):
                dve.wait_ge(x3_normed, t + 1)
                dve.wait_ge(gfin_in, 16)
                dve.tensor_tensor(acc[:, t, :], acc[:, t, :], gfin, ALU.mult).then_inc(out_ready, 1)

            gated(0)
            for t in range(T):
                if t + 1 < T:
                    gated(t + 1)
                rstd3(t)
                if t >= 1:
                    final(t - 1)
            final(T - 1)

        @block.tensor
        def _(pe):
            pe.wait_ge(norm_ready, 1)
            for t in range(T):
                pe.wait_ge(xn_ready, t + 1)
                for k in range(KC):
                    last = pe.transpose(ps[:, k, t * P:(t + 1) * P],
                                        xn[:, t, k * P:(k + 1) * P], ident[:])
            last.then_inc(xn_turned, 1)

            def ada(n, bank):
                r, k = n // KC, n % KC
                pe.wait_ge(ada_in[n % ADA_BUFS], 16 * (n // ADA_BUFS + 1))
                for q in range(4):
                    last = pe.matmul(ps[32 * q:32 * q + 32, bank, :], c_rep[:, k, :],
                                     ada_buf(n % ADA_BUFS)[:, q * HALF:(q + 1) * HALF],
                                     start=(k == 0), stop=(k == KC - 1))
                last.then_inc(ada_used, 1)

            pe.wait_ge(c_rep_ready, 1)
            pe.wait_ge(xnt_ready_dve, 3)
            for n in range(KC):
                ada(n, 4)
            pe.wait_ge(rows_in, 16 * 7)
            pe.wait_ge(xnt_ready_act, KC // 2)
            for i in range(CT):
                last = pe.transpose(ps[:, 7, i * NV:(i + 1) * NV], conv_raw[:, i * P:(i + 1) * P],
                                    ident[0:NV, 0:NV])
            last.then_inc(conv_c_turned, 1)
            pe.wait_ge(mod_rows_ready, 1)
            for j in range(4):
                last = pe.transpose(ps[:, 5, j * P:(j + 1) * P], mod01[:, 0, j * P:(j + 1) * P], ident[:])
            last.then_inc(mod0_turned, 1)

            def z_tile(n):
                bank = n % 4
                if n >= 4:
                    if n < 2 * CT + 4:
                        old = n - 4
                        if old < 2 * CT:
                            pe.wait_ge(sig_ready if old % 2 else glu_ready, old // 2 + 1)
                    if n - 4 >= 2 * CT:
                        pe.wait_ge(gelu_ready, n - 4 - 2 * CT + 1)
                if n < 2 * CT:
                    q, w, cols = n % 2, (win_a, win_g)[n % 2], n // 2
                elif n < 3 * CT:
                    q, w, cols = 3, win_v, n - 2 * CT
                else:
                    q, w, cols = 2, win_u, n - 3 * CT
                pe.wait_ge(win_in[q], 16)
                for k in range(KC):
                    if n == 0:
                        pe.wait_ge(h_act if k % 2 else h_dve, k // 2 + 1)
                    last = pe.matmul(ps[:, bank, :], w[:, k, cols * P:(cols + 1) * P], h_t[:, k, :],
                                     start=(k == 0), stop=(k == KC - 1))
                last.then_inc(z_done, 1)

            def ln_mean_of(n):
                if n < CT:
                    pe.wait_ge(gelu_ready, n + 1)
                else:
                    pe.wait_ge(conv_step, TAPS * CT if n >= CT + 2 else TAPS * 2)
                if n >= 1:
                    pe.wait_ge(ln_centred, n)
                src = v_t[:, n, :] if n < CT else y_cat[:, n - CT, :]
                pe.matmul(ps[:, 5, :], group_mean[:], src, start=True, stop=True).then_inc(ln_mean, 1)

            def ln_var_of(n):
                pe.wait_ge(ln_squared, n + 1)
                if n >= 1:
                    pe.wait_ge(ln_rooted, n)
                pe.matmul(ps[:, 6, :], group_mean[:], ln_sq, start=True, stop=True).then_inc(ln_var, 1)

            def turn_v(n):
                pe.wait_ge(v_scaled, n + 1)
                if n >= 1:
                    pe.wait_ge(v_ready, n)
                else:
                    pe.wait_ge(gt1_ready, 2)
                for t in range(T):
                    last = pe.transpose(ps[:, 7, t * P:(t + 1) * P], v_t[:, n, t * P:(t + 1) * P], ident[:])
                last.then_inc(v_turned, 1)

            for n in range(4 * CT):
                z_tile(n)
                if 3 <= n < 7:
                    if n == 3:
                        pe.wait_ge(mod_rows_ready, 1)
                    ada(KC + 2 * (n - 3), 4)
                    ada(KC + 2 * (n - 3) + 1, 4)
                if 8 <= n < 12:
                    if n == 8:
                        pe.wait_ge(mod_rows_ready, 2)
                    ada(2 * KC + 2 * (n - 8), 4)
                    ada(2 * KC + 2 * (n - 8) + 1, 4)
                if 7 <= n < 9:
                    if n == 7:
                        pe.wait_ge(consts_in, 16 * N_CONST)
                        pe.wait_ge(pool_consts, 1)
                        pe.wait_ge(conv_c_ready, 1)
                    else:
                        pe.wait_ge(sgu_w_ready, 1)
                    for h in range(4):
                        last = pe.transpose(ps[:, 7, h * P:(h + 1) * P], w_sgu_raw[:, 4 * (n - 7) + h, :], ident[:])
                    last.then_inc(sgu_w_turned, 1)
                if 9 <= n < 11:
                    if n == 9:
                        pe.wait_ge(sgu_w_ready, 2)
                    else:
                        pe.wait_ge(gt1_ready, 1)
                    q = 32 * (n - 9)
                    pe.matmul(ps[:, 7, :], ones[q:q + 1, :], mod01[q:q + 1, 1, :], start=True, stop=True
                              ).then_inc(gt1_spread, 1)
                if 11 <= n < 15:
                    turn_v(n - 11)
                if n >= 10:
                    ln_var_of(n - 10)
                if 9 <= n < 15:
                    ln_mean_of(n - 9)

            pe.wait_ge(gelu_ready, 2 * CT)
            pe.wait_ge(v_ready, CT)
            for ch in range(T):
                for h in range(HEADS):
                    last = pe.matmul(ps[HD * (h % 2):HD * (h % 2) + HD, h // 2, ch * P:(ch + 1) * P],
                                     v_sb[:, ch, h * HD:(h + 1) * HD], w_sgu_t[:, h, :], start=True, stop=True,
                                     skip_group_check=True)
            last.then_inc(sgu_mixed, 1)
            ln_mean_of(2 * CT - 2)
            ln_var_of(2 * CT - 2)
            ln_mean_of(2 * CT - 1)
            ln_var_of(2 * CT - 1)

            def mix(t, h):
                bank = 2 * (t % 2) + h
                if t >= 2:
                    pe.wait_ge(x2_ready, 2 * (t - 2) + h + 1)
                for m in (*range(CT, 2 * CT), *range(CT)):
                    if m == 0 and t == 0 and h == 0:
                        pe.wait_ge(conv_out, CT)
                    last = pe.matmul(ps[:, bank, :], y_cat[:, m, t * P:(t + 1) * P],
                                     wout_sb[:, m, h * HALF:(h + 1) * HALF], start=(m == CT), stop=(m == CT - 1))
                last.then_inc(mix_done, 1)

            def turn_xn2(t):
                pe.wait_ge(xn2_ready, t + 1)
                if t >= 1:
                    pe.wait_ge(h2_act, KC // 2 * t)
                    pe.wait_ge(h2_dve, KC // 2 * t)
                for k in range(KC):
                    last = pe.transpose(ps[:, 4 + k // 4, (k % 4) * P:(k % 4 + 1) * P], xn2[:, t % 2, k, :], ident[:])
                last.then_inc(xn2_turned, 1)

            def route(t):
                if t >= 2:
                    pe.wait_ge(logits_ready, t - 1)
                pe.wait_ge(h2_act, KC // 2 * (t + 1))
                pe.wait_ge(h2_dve, KC // 2 * (t + 1))
                for k in range(KC):
                    last = pe.matmul(ps[:, 6 + t % 2, 0:NR], y_cat[:, k, t * P:(t + 1) * P],
                                     w_router[:, k, :], start=(k == 0), stop=(k == KC - 1), skip_group_check=True)
                last.then_inc(logits_done, 1)

            pe.wait_ge(sgu_out, CT)
            pe.wait_ge(wout_in, 16)
            pe.wait_ge(router_packed, 1)
            for t in range(2):
                for h in range(2):
                    mix(t, h)
            for t in range(2, T):
                mix(t, 0)
                turn_xn2(t - 2)
                mix(t, 1)
                route(t - 2)
            for t in range(T - 2, T):
                turn_xn2(t)
                route(t)
            for j in range(2):
                q = 32 * (2 + j)
                last = pe.matmul(ps[SLOTS * j:SLOTS * (j + 1), 0, :], ones[q:q + 1, 0:SLOTS], mod2[q:q + 1, :],
                                 start=True, stop=True)
            last.then_inc(gt2_spread, 1)
            pe.wait_ge(hot_ready, 1)
            def count(tiles, lhs, t):
                n = tiles.stop - tiles.start
                return pe.matmul(ps[:, 7, tiles.start * NE:tiles.stop * NE], lhs,
                                 hot16[:, t, :].unsqueeze(1).to_broadcast([P, n, NE]), start=False,
                                 stop=(t == T - 1), skip_group_check=True)

            pe.matmul(ps[:, 7, 0:T * NE], before16[:], hot16.rearrange("p t e -> p (t e)"), start=True, stop=False,
                      skip_group_check=True)
            for t in range(T):
                if t < T - 1:
                    count(slice(t + 1, T), ones16[:], t)
                last = count(slice(T, T + 1), ones16[:], t)
            last.then_inc(counted, 1)

            def find_rows(e, src, got):
                for t in range(T):
                    last = pe.matmul(ps[:, 7, 0:2], src[:, t, :],
                                     row_vals[:, t, bass.ds(e, 1), :].rearrange("p o v -> p (o v)"),
                                     start=(t == 0), stop=(t == T - 1), skip_group_check=True)
                last.then_inc(got, 1)

            def turn(src, bank, got):
                pe.sem_inc(tokens_here, 1)
                for k in range(KC):
                    last = pe.transpose(ps[:, bank, k * SLOTS:(k + 1) * SLOTS], src[0:SLOTS, k, :],
                                        ident[0:SLOTS, 0:SLOTS])
                last.then_inc(got, 1)

            def gate_up(src, bank, slot, got):
                w = ring[:, slot * SLOT_W:slot * SLOT_W + GU_W].rearrange("p (g k f) -> p g k f", g=2, k=KC)
                for k in range(KC):
                    for j in range(2):
                        last = pe.matmul(ps[SLOTS * j:SLOTS * (j + 1), bank, 0:2 * P].rearrange(
                            "p (g f) -> p g f", g=2), src[:, k, :], w[:, :, k, j * P:(j + 1) * P],
                            start=(k == 0), stop=(k == KC - 1), skip_group_check=True)
                last.then_inc(got, 1)

            def turn_hidden(src, got):
                pe.transpose(ps[:, 4, 0:P], src, ident[:]).then_inc(got, 1)

            def down(src, bank, slot, got):
                w = ring[:, slot * SLOT_W + GU_W:(slot + 1) * SLOT_W].rearrange("p (c n) -> p c n", c=FC)
                for f in range(FC):
                    for j in range(2):
                        last = pe.matmul(ps[SLOTS * j:SLOTS * (j + 1), bank, :], src[:, f * SLOTS:(f + 1) * SLOTS],
                                         w[:, f, j * HALF:(j + 1) * HALF], start=(f == 0), stop=(f == FC - 1),
                                         skip_group_check=True)
                last.then_inc(got, 1)

            def step(e, b2, slot, bg, tokens, weights, first, y_free, find, nxt):
                if find:
                    pe.wait_ge(picks_ready, e + AHEAD + 1)
                    pe.wait_ge(rows_ready, e + AHEAD)
                    find_rows(e + AHEAD, picks[:, b2], rows_found)
                if nxt:
                    if not first:
                        pe.wait_ge(xt_ready, e)
                    pe.wait_ge(gathered[bg], tokens)
                    turn(xg[:, bg], 1 - b2, xg_turned)
                pe.wait_ge(xt_ready, e + 1)
                if not first:
                    pe.wait_ge(hid_ready, e)
                pe.wait_ge(expert_in[slot], weights)
                gate_up(xt[:, b2], 2 + b2, slot, gate_up_done)
                if not first:
                    if y_free:
                        pe.wait_ge(y_ready, e - 2)
                    pe.wait_ge(hid_t_ready, e)
                    down(hid_t[:, 1 - b2], 6 - b2, (slot - 1) % RING, down_done)
                pe.wait_ge(hid_ready, e + 1)
                turn_hidden(hid[:, b2, :], hid_turned)
                with extra_blocks(pe, e) as n:
                    pe.wait_ge(hid_t_ready, e + 1)
                    if find:
                        pe.wait_ge(rows_ready, e + AHEAD + 1)
                    if y_free or b2 == 0 and not first:
                        pe.wait_ge(y_ready, e - 1)
                    pe.wait_ge(ov_picks, n + 1)
                    find_rows(e, picks_x, ov_found)
                    pe.wait_ge(ov_gathered, 16 * n + 16)
                    turn(xg_x, b2, ov_turned)
                    pe.wait_ge(ov_xt, n + 1)
                    gate_up(xt_x, 3 - b2, slot, ov_gate_up)
                    pe.wait_ge(ov_hid, n + 1)
                    turn_hidden(hid_x, ov_hid_turned)
                    pe.wait_ge(ov_hid_t, n + 1)
                    down(hid_t_x, 5 + b2, slot, ov_down)
                    pe.wait_ge(ov_y, n + 1)
                    pe.sem_inc(ov_passed, 1)

            pe.wait_ge(places_ready, 1)
            for e in range(AHEAD):
                pe.wait_ge(picks_ready, e + 1)
                if e:
                    pe.wait_ge(rows_ready, e)
                find_rows(e, picks[:, e % 2], rows_found)
            pe.wait_ge(gathered[0], 16)
            pe.wait_ge(gt2_ready, 1)
            turn(xg[:, 0], 0, xg_turned)
            pe.wait_ge(routed, 1)
            for e in range(3):
                step(e, e % 2, e, (e + 1) % XG, 16 * ((e + 1) // XG + 1), 48, e == 0, False, True, True)
            with pe.Fori(0, 2) as i:
                for r in range(2 * RING):
                    step(3 + 2 * RING * i + r, (1 + r) % 2, (3 + r) % RING, (4 + r) % XG,
                         16 * (2 * RING // XG * i + (4 + r) // XG + 1), 48 * (2 * i + (3 + r) // RING + 1),
                         False, True, True, True)
            for e in range(3 + 4 * RING, NE):
                step(e, e % 2, e % RING, (e + 1) % XG, 16 * ((e + 1) // XG + 1), 48 * (e // RING + 1),
                     False, True, e + AHEAD < NE, e + 1 < NE)
            pe.wait_ge(y_ready, NE - 2)
            pe.wait_ge(hid_t_ready, NE)
            down(hid_t[:, (NE - 1) % 2], 6, (NE - 1) % RING, down_done)



_INS = ["x", "c", "w_ada", "b_ada", "g_mix", "w_in", "conv_w", "conv_b", "conv_ln_g", "conv_ln_b",
        "sgu_ln_g", "sgu_ln_b", "sgu_w", "sgu_b", "w_out", "g_ffn", "w_coarse", "b_coarse",
        "w_fine", "b_fine", "w_gate", "w_up", "w_down", "g_final"]


def kernel(**inputs):
    import numpy as _np
    import concourse.bacc as _bacc
    from concourse import mybir as _mybir
    from concourse.bass_utils import run_bass_kernel_spmd as _run

    nc = _bacc.Bacc("TRN2", target_bir_lowering=False, num_devices=1, dynamic_dma_scratch_size=8192)
    arrays, args = {}, []
    for name in _INS:
        a = _np.ascontiguousarray(inputs[name])
        arrays[f"in_{name}"] = a
        args.append(nc.dram_tensor(f"in_{name}", a.shape, _mybir.dt.from_np(a.dtype), kind="ExternalInput").ap())
    shape = inputs["x"].shape
    out = nc.dram_tensor("out", shape, _mybir.dt.float32, kind="ExternalOutput").ap()
    build_block(nc, *args, out)
    r = _run(nc, [arrays], core_ids=[0])
    return r.results[0]["out"]
```

```python
from contextlib import ExitStack, contextmanager

import concourse.bass as bass
from concourse import mybir

P = 128
F32 = mybir.dt.float32
F16 = mybir.dt.float16
I32 = mybir.dt.int32
U32 = mybir.dt.uint32
ALU = mybir.AluOpType
ACT = mybir.ActivationFunctionType
AX_X = mybir.AxisListType.X


def build_block(nc, x, c, w_ada, b_ada, g_mix, w_in, conv_w, conv_b, conv_ln_g, conv_ln_b,
                sgu_ln_g, sgu_ln_b, sgu_w, sgu_b, w_out, g_ffn, w_coarse, b_coarse,
                w_fine, b_fine, w_gate, w_up, w_down, g_final, out):
    S, D = x.shape[1], x.shape[2]
    KC = D // P
    T = S // P
    CW = conv_w.shape[2]
    CT = CW // P
    TAPS = conv_w.shape[1]
    PAD = TAPS - 1
    HEADS = sgu_w.shape[1]
    HD = CW // HEADS
    G = w_coarse.shape[2]
    EG = w_fine.shape[3]
    NE = G * EG
    DE = w_gate.shape[3]
    FC = DE // P
    NV = TAPS + 5 + 2
    HALF = D // 2
    SLOTS = 64
    NR = G + NE
    EPS = 1e-6
    RING = 6
    TAPS_BY = (8, 11, 14, 18, 22, 27, 31)
    XN_BANK = (0, 1, 2, 3, 5, 6, 7, 0)
    N_CONST = 6
    SLOT_W = 2 * KC * DE + FC * D
    GU_W = 2 * KC * DE
    ADA_BUFS = 5
    ROUND = 4 * HALF
    ROUNDS = w_ada.shape[2] // ROUND
    AHEAD = 4
    OOB = 2 * S * 2
    XG = 4
    YB = 3
    ROWS = 12
    assert (S, D, CW, HD, NE, DE, OOB, TAPS) == (512, 1024, 512, 64, 32, 256, 2048, 31)

    xn_rows = nc.dram_tensor("xn_rows", [S, D], F32).ap()
    y_rows = nc.dram_tensor("y_rows", [2 * 2 * S, HALF], F32).ap()

    with ExitStack() as ctx:
        def sb(name, shape, dt=F32):
            return ctx.enter_context(nc.sbuf_tensor(name, shape, dt))

        def sem(name):
            return ctx.enter_context(nc.semaphore(name))

        ps = ctx.enter_context(nc.psum_tensor("ps", [P, 8, HALF], F32))

        ring = sb("ring", [P, RING * SLOT_W])
        work = sb("work", [P, 12288])
        x_sb = sb("x_sb", [P, T, D])
        mod2 = sb("mod2", [P, HALF])
        ident = sb("ident", [P, P])
        ones = sb("ones", [P, P])
        group_mean = sb("group_mean", [P, P])
        slot_iota = sb("slot_iota", [P, P])
        before16 = sb("before16", [P, P], F16)
        ones16 = sb("ones16", [P, P], F16)
        w_router = sb("w_router", [P, KC, NR])
        conv_c = sb("conv_c", [P, CT, NV])
        b_router = sb("b_router", [P, NR])
        c_col = sb("c_col", [P, KC])
        logits = sb("logits", [P, T, NR])
        gffn_col = sb("gffn_col", [P, KC])
        mod1_nat = sb("mod1_nat", [P, 2, KC])
        mod_col = sb("mod_col", [P, 2, KC])
        a1_col = sb("a1_col", [P, KC])
        a2_col = sb("a2_col", [P, KC])
        eps_col = sb("eps_col", [P, 1])
        row_off = sb("row_off", [P, 2])
        tok_id = sb("tok_id", [P, T])
        stat = sb("stat", [P, 8, T])

        def ring_at(off, n):
            return ring[:, off:off + n]

        def ada_buf(b):
            return ring_at(b * ROUND, ROUND)
        o = ADA_BUFS * ROUND
        bada_sb = ring_at(o, ROUNDS * HALF).rearrange("p (r n) -> p r n", r=ROUNDS)
        c_rep = ring_at(o + ROUNDS * HALF, KC * 32).rearrange("p (k m) -> p k m", k=KC)
        o = 2 * SLOT_W
        win_u = ring_at(o, KC * CW).rearrange("p (k n) -> p k n", k=KC)
        win_v = ring_at(o + 4096, KC * CW).rearrange("p (k n) -> p k n", k=KC)
        h_t = ring_at(o + 8192, KC * S).rearrange("p (k n) -> p k n", k=KC)
        o = 4 * SLOT_W
        win_a = ring_at(o, KC * CW).rearrange("p (k n) -> p k n", k=KC)
        win_g = ring_at(o + 4096, KC * CW).rearrange("p (k n) -> p k n", k=KC)
        y_pad = ring_at(o + 8192, CT * (S + PAD)).rearrange("p (i n) -> p i n", i=CT)
        v_sb = ring_at(o, T * CW).rearrange("p (t n) -> p t n", t=T)
        v_t = ring_at(o + 2048, CT * S).rearrange("p (i n) -> p i n", i=CT)
        w_sgu_t = ring_at(o + 4096, HEADS * P).rearrange("p (h n) -> p h n", h=HEADS)
        ln_sq = ring_at(o + 5120, S)
        sgu_b_row = ring_at(o + 6144, CT * P).rearrange("p (i n) -> p i n", i=CT)
        ln_yc = ring_at(o + 6656, 2 * S).rearrange("p (b n) -> p b n", b=2)
        ln_root = ring_at(o + 7680, S)
        xn2 = ring_at(o + 8192, 2 * D).rearrange("p (b k n) -> p b k n", b=2, k=KC)
        gt1b = ring_at(o + 11264, D)

        wout_sb = work[:, 0:8192].rearrange("p (m n) -> p m n", m=KC)
        y_cat = work[:, 8192:12288].rearrange("p (m n) -> p m n", m=KC)
        xn = work[:, 0:4096].rearrange("p (t n) -> p t n", t=T)
        sig = work[:, 4096:5120].rearrange("p (b n) -> p b n", b=2)
        w_sgu_raw = work[:, 5120:6144].rearrange("p (h n) -> p h n", h=HEADS)
        conv_raw = work[0:NV, 6144:6656]
        fine_raw = work[:, 6656:6912].rearrange("p (g k e) -> p g k e", g=G, k=KC)
        coarse_raw = work[:, 6912:6944].rearrange("p (k g) -> p k g", k=KC)

        tri = work[:, 6944:7072]
        ada_acc = work[:, 2 * HALF:2 * HALF + ROUND]
        mod01 = work[:, 0:2 * HALF].rearrange("p (r n) -> p r n", r=2)

        xg = work[:, 0:XG * D].rearrange("p (b k n) -> p b k n", b=XG, k=KC)
        o = [XG * D]

        def rt(n, dt=F32):
            a = work[:, o[0]:o[0] + n]
            o[0] += n
            return a if dt == F32 else a.bitcast(dt)
        coarse8 = rt(T * 8).rearrange("p (t n) -> p t n", t=T)
        top_c = rt(T * 8).rearrange("p (t n) -> p t n", t=T)
        top_ci = rt(T * 8, U32).rearrange("p (t n) -> p t n", t=T)
        c_exp = rt(T * 8).rearrange("p (t n) -> p t n", t=T)
        neg_max = rt(T)
        p_grp = rt(T)
        grp = rt(T)
        grp_hot = rt(T * G).rearrange("p (t g) -> p t g", t=T)
        fine_m = rt(T * NE).rearrange("p (t g e) -> p t g e", t=T, g=G)
        fine_s = rt(T * EG).rearrange("p (t e) -> p t e", t=T)
        top_f = rt(T * 8).rearrange("p (t n) -> p t n", t=T)
        top_fi = rt(T * 8, U32).rearrange("p (t n) -> p t n", t=T)
        gate_k = rt(2 * T).rearrange("p (k t) -> p k t", k=2)
        expert_k = rt(2 * T).rearrange("p (k t) -> p k t", k=2)
        e_diff = rt(T)
        hot0 = rt(T * NE).rearrange("p (t e) -> p t e", t=T)
        hot1 = rt(T * NE).rearrange("p (t e) -> p t e", t=T)
        place = rt(T * (NE + 1)).rearrange("p (t e) -> p t e", t=T)
        hot16 = rt(T * NE // 2, F16).rearrange("p (t e) -> p t e", t=T)
        row_vals = rt(T * NE, F16).rearrange("p (t e v) -> p t e v", t=T, v=2)
        row_idx = rt(2 * ROWS, U32).rearrange("p (b v) -> p b v", v=2)
        blocks_f = rt(2 * NE).rearrange("p (v e) -> p v e", v=2)
        block_info = rt(2 * NE, I32).rearrange("p (v e) -> p v e", v=2)
        row_idx_x = rt(2, U32)
        assert o[0] <= 8192
        xt = rt(D).rearrange("p (b k n) -> p b k n", b=2, k=KC)
        gate_act = rt(2 * P).rearrange("p (b n) -> p b n", b=2)
        hid = rt(2 * P).rearrange("p (b n) -> p b n", b=2)
        hid_t = rt(2 * P).rearrange("p (b n) -> p b n", b=2)
        y_exp = rt(YB * HALF).rearrange("p (b n) -> p b n", b=YB)
        picks = rt(T * P, F16).rearrange("p (b t n) -> p b t n", b=2, t=T)
        xg_x = rt(D).rearrange("p (k n) -> p k n", k=KC)
        xt_x = rt(KC * SLOTS).rearrange("p (k n) -> p k n", k=KC)
        gate_act_x, hid_x, hid_t_x = rt(P), rt(P), rt(P)
        y_exp_x = rt(HALF)
        gt2_exp = rt(HALF)
        picks_x = rt(T * P // 2, F16).rearrange("p (t n) -> p t n", t=T)
        assert o[0] <= 12288


        y_back = ring_at(0, T * 2 * D).rearrange("p (t k h n) -> p t k h n", t=T, k=2, h=2)
        acc = ring_at(T * 2 * D, T * D).rearrange("p (t n) -> p t n", t=T)
        gfin = ring_at(T * 3 * D, D)

        x_in = [sem(f"x_in{t}") for t in range(T)]
        c_in = sem("c_in")
        rows_in = sem("rows_in")
        consts_in = sem("consts_in")
        norm_ready = sem("norm_ready")
        bada_in = sem("bada_in")
        ada_in = [sem(f"ada_in{b}") for b in range(ADA_BUFS)]
        win_in = [sem(f"win_in_{n}") for n in "aguv"]
        sgu_rows_in = sem("sgu_rows_in")
        wout_in = sem("wout_in")
        expert_in = [sem(f"expert_in{r}") for r in range(RING)]
        pool_consts = sem("pool_consts")
        pool_order = sem("pool_order")
        bada_zero = sem("bada_zero")
        router_packed = sem("router_packed")
        act_order = sem("act_order")
        dve_order = sem("dve_order")
        c_act_ready = sem("c_act_ready")
        c_rep_ready = sem("c_rep_ready")
        x_root = sem("x_root")
        xn_ready = sem("xn_ready")
        conv_c_turned = sem("conv_c_turned")
        conv_c_ready = sem("conv_c_ready")
        xn_turned = sem("xn_turned")
        xnt_ready_dve = sem("xnt_ready_dve")
        xnt_ready_act = sem("xnt_ready_act")
        mod0_turned = sem("mod0_turned")
        mod1_ready = sem("mod1_ready")
        ada_used = sem("ada_used")
        ada_scaled = sem("ada_scaled")
        ada_added = sem("ada_added")
        ada_summed = sem("ada_summed")
        mod_rows_ready = sem("mod_rows_ready")
        mod_cols_in = [sem(f"mod_cols_in{r}") for r in range(2)]
        a1_ready = sem("a1_ready")
        h_dve = sem("h_dve")
        h_act = sem("h_act")
        z_done = sem("z_done")
        sig_ready = sem("sig_ready")
        glu_ready = sem("glu_ready")
        gelu_ready = sem("gelu_ready")
        conv_step = sem("conv_step")
        sgu_w_turned = sem("sgu_w_turned")
        sgu_w_ready = sem("sgu_w_ready")
        gt1_spread = sem("gt1_spread")
        gt1_ready = sem("gt1_ready")
        ln_mean = sem("ln_mean")
        ln_centred = sem("ln_centred")
        ln_squared = sem("ln_squared")
        ln_var = sem("ln_var")
        ln_rooted = sem("ln_rooted")
        ln_rstd = sem("ln_rstd")
        ln_normed = sem("ln_normed")
        v_scaled = sem("v_scaled")
        v_turned = sem("v_turned")
        v_ready = sem("v_ready")
        conv_out = sem("conv_out")
        sgu_mixed = sem("sgu_mixed")
        sgu_out = sem("sgu_out")
        mix_done = sem("mix_done")
        x2_ready = sem("x2_ready")
        x2_root = sem("x2_root")
        xn2_ready = sem("xn2_ready")
        xn2_stored = [sem(f"xn2_stored{b}") for b in range(2)]
        xn2_turned = sem("xn2_turned")
        a2_ready = sem("a2_ready")
        h2_dve = sem("h2_dve")
        h2_act = sem("h2_act")
        logits_done = sem("logits_done")
        logits_ready = sem("logits_ready")
        neg_max_ready = sem("neg_max_ready")
        c_exp_ready = sem("c_exp_ready")
        diff_ready = sem("diff_ready")
        diff_exp = sem("diff_exp")
        hot_ready = sem("hot_ready")
        counted = sem("counted")
        rows_from = sem("rows_from")
        places_ready = sem("places_ready")
        routed = sem("routed")
        picks_ready = sem("picks_ready")
        rows_found = sem("rows_found")
        rows_ready = sem("rows_ready")
        gathered = [sem(f"gathered{b}") for b in range(XG)]
        xg_turned = sem("xg_turned")
        xt_ready = sem("xt_ready")
        gate_up_done = sem("gate_up_done")
        silu_ready = sem("silu_ready")
        hid_ready = sem("hid_ready")
        hid_turned = sem("hid_turned")
        hid_t_ready = sem("hid_t_ready")
        step_passed = sem("step_passed")
        down_done = sem("down_done")
        y_ready = sem("y_ready")
        scattered = [sem(f"scattered{b}") for b in range(YB)]
        ov_place = sem("ov_place")
        ov_free = sem("ov_free")
        ov_picks = sem("ov_picks")
        ov_found = sem("ov_found")
        ov_rows = sem("ov_rows")
        ov_gathered = sem("ov_gathered")
        ov_turned = sem("ov_turned")
        ov_xt = sem("ov_xt")
        ov_gate_up = sem("ov_gate_up")
        ov_silu = sem("ov_silu")
        ov_hid = sem("ov_hid")
        ov_hid_turned = sem("ov_hid_turned")
        ov_hid_t = sem("ov_hid_t")
        ov_down = sem("ov_down")
        ov_y = sem("ov_y")
        ov_scattered = sem("ov_scattered")
        ov_passed = sem("ov_passed")
        pool_go = sem("pool_go")
        tokens_here = sem("tokens_here")
        all_scattered = sem("all_scattered")
        gfin_in = sem("gfin_in")
        gt2_spread = sem("gt2_spread")
        gt2_ready = sem("gt2_ready")
        y_in = [sem(f"y_in{t}") for t in range(T)]
        x3_ready = sem("x3_ready")
        x3_root = sem("x3_root")
        x3_rstd = sem("x3_rstd")
        x3_normed = sem("x3_normed")
        out_ready = sem("out_ready")
        last_out_ready = sem("last_out_ready")
        out_stored = sem("out_stored")

        x_rows = x.rearrange("b (t p) d -> (b t) p d", p=P)
        out_rows = out.rearrange("b (t p) d -> (b t) p d", p=P)
        ada_v = w_ada.rearrange("l (p k) n -> (l p) k n", k=KC)
        win_dram = w_in.rearrange("l (k p) n -> (l p) k n", k=KC)
        wout_dram = w_out.rearrange("l (m p) n -> (l p) m n", p=P)
        gate_dram = w_gate.rearrange("l e (p k) f -> (l e) p (k f)", k=KC)
        up_dram = w_up.rearrange("l e (p k) f -> (l e) p (k f)", k=KC)
        down_dram = w_down.rearrange("l e (c p) n -> (l e) p c n", p=P)

        def col_of(v):
            return v.rearrange("l (p k) -> (l p) k", k=KC)

        def load_gate_up(eng, e, slot, done):
            base = ring[:, slot * SLOT_W:(slot + 1) * SLOT_W]
            eng.dma_start(base[:, 0:GU_W // 2], gate_dram[e]).then_inc(done, 16)
            eng.dma_start(base[:, GU_W // 2:GU_W], up_dram[e]).then_inc(done, 16)

        def load_down(eng, e, slot, done):
            base = ring[:, slot * SLOT_W:(slot + 1) * SLOT_W]
            eng.dma_start(base[:, GU_W:SLOT_W].rearrange("p (c n) -> p c n", c=FC),
                          down_dram[e]).then_inc(done, 16)

        def load_expert(eng, e, slot, done):
            load_gate_up(eng, e, slot, done)
            load_down(eng, e, slot, done)

        block = ctx.enter_context(nc.Block())

        @contextmanager
        def extra_blocks(eng, e):
            blocks = eng.value_load(block_info[0:1, 0, bass.ds(e, 1)], min_val=0, max_val=S // SLOTS)
            with eng.If(blocks > 1):
                before = eng.value_load(block_info[0:1, 1, bass.ds(e, 1)], min_val=0, max_val=2 * S // SLOTS)
                with eng.Fori(1, blocks) as j:
                    yield before + j - 1

        @block.sync
        def _(sp):
            for t in range(T):
                sp.dma_start(x_sb[:, t, :], x_rows[t]).then_inc(x_in[t], 16)

            def ada_unit(n):
                b = n % ADA_BUFS
                old = n - ADA_BUFS
                if old >= KC:
                    sp.wait_ge(ada_added, (old // KC - 1) * (KC - 1) + max(old % KC, 1))
                elif old >= 0:
                    sp.wait_ge(ada_used, old + 1)
                r, k = n // KC, n % KC
                sp.dma_start(ada_buf(b), ada_v[:, k, r * ROUND:(r + 1) * ROUND]).then_inc(ada_in[b], 16)

            for n in range(KC):
                ada_unit(n)
            for q, dst, first in ((0, win_a, 0), (1, win_g, CW), (3, win_v, 3 * CW), (2, win_u, 2 * CW)):
                sp.dma_start(dst, win_dram[:, :, first:first + CW]).then_inc(win_in[q], 16)
            for n in range(KC, ROUNDS * KC):
                ada_unit(n)
            sp.wait_ge(z_done, 2 * CT)
            for h in range(HEADS):
                rows = slice(HD * (h % 2), HD * (h % 2) + HD)
                sp.dma_start(sgu_b_row[rows, h // 2, :], sgu_b[0, h:h + 1, :].to_broadcast([HD, P])
                             ).then_inc(sgu_rows_in, 16)
            sp.wait_ge(glu_ready, CT)
            sp.wait_ge(sgu_w_ready, 2)
            sp.wait_ge(router_packed, 1)
            sp.wait_ge(gt1_spread, 2)
            sp.wait_ge(ada_summed, 2)
            sp.wait_ge(mod_cols_in[0], 32)
            sp.dma_start(wout_sb, wout_dram).then_inc(wout_in, 16)

            sp.wait_ge(ada_used, KC)
            sp.wait_ge(ada_added, (ROUNDS - 1) * (KC - 1))
            sp.wait_ge(mod_rows_ready, ROUNDS)
            load_expert(sp, 0, 0, expert_in[0])
            load_expert(sp, 1, 1, expert_in[1])
            sp.wait_ge(z_done, 2 * CT + CT + T)
            load_expert(sp, 2, 2, expert_in[2])
            load_expert(sp, 3, 3, expert_in[3])
            sp.wait_ge(conv_out, CT)
            sp.wait_ge(sgu_out, CT)
            load_expert(sp, 4, 4, expert_in[4])
            sp.wait_ge(xn2_turned, T)
            for b in range(2):
                sp.wait_ge(xn2_stored[b], 16 * T // 2)
            sp.wait_ge(x2_ready, 2 * T)
            load_expert(sp, 5, 5, expert_in[5])

            def reload(e, slot, old):
                sp.wait_ge(gate_up_done, old + 1)
                sp.wait_ge(step_passed, old + 1)
                load_gate_up(sp, e, slot, expert_in[slot])
                sp.wait_ge(down_done, old + 1)
                load_down(sp, e, slot, expert_in[slot])

            with sp.Fori(0, (NE - RING) // RING) as i:
                for r in range(RING):
                    reload(RING + RING * i + r, r, RING * i + r)
            for e in range(NE - NE % RING, NE):
                reload(e, e % RING, e - RING)

            sp.wait_ge(down_done, NE - NE % RING - RING + 3)
            sp.dma_start(gfin, g_final.rearrange("(o d) -> o d", o=1).to_broadcast([P, D])
                         ).then_inc(gfin_in, 16)
            sp.wait_ge(all_scattered, 1)
            back = y_rows.rearrange("(h k t p) n -> t k p h n", h=2, k=2, p=P)
            for t in range(T):
                for k in range(2):
                    sp.dma_start(y_back[:, t, k], back[t, k]).then_inc(y_in[t], 16)
            for t in range(T):
                if t < 2:
                    sp.wait_ge(out_ready, t + 1)
                else:
                    sp.wait_ge(last_out_ready, t - 1)
                sp.dma_start(out_rows[t], acc[:, t, :]).then_inc(out_stored, 16)
            sp.wait_ge(out_stored, 16 * T)

        @block.gpsimd
        def _(pool):
            done = [0]

            def link(ins):
                ins.then_inc(pool_order, 1)
                done[0] += 1
                pool.wait_ge(pool_order, done[0])

            link(pool.memset(eps_col[:], EPS))
            link(pool.memset(ident[:], 1.0))
            pool.affine_select(out=ident[:], in_=ident[:], compare_op=ALU.is_equal, fill=0.0, base=0,
                               pattern=[[1, P]], channel_multiplier=-1).then_inc(norm_ready, 1)
            pool.memset(bada_sb, 0.0).then_inc(bada_zero, 1)
            pool.wait_ge(bada_zero, 1)
            bada_v = b_ada.rearrange("l (r q n) -> l r q n", q=4, n=HALF)
            for q in range(4):
                pool.dma_start(bada_sb[32 * q:32 * q + 1], bada_v[:, :, q, :]).then_inc(bada_in, 16)
            link(pool.memset(ones[:], 1.0))
            link(pool.memset(group_mean[:], 0.0))
            link(pool.memset(group_mean[0:HD, 0:HD], 1.0 / HD))
            link(pool.memset(group_mean[HD:P, HD:P], 1.0 / HD))
            link(pool.memset(tri, 1.0))
            link(pool.affine_select(out=tri, in_=tri, compare_op=ALU.is_ge, fill=0.0, base=0,
                                    pattern=[[1, P]], channel_multiplier=-1))
            link(pool.memset(ones16[:], 1.0))
            link(pool.affine_select(out=before16[:], in_=ones16[:], compare_op=ALU.is_gt, fill=0.0, base=0,
                                    pattern=[[1, P]], channel_multiplier=-1))
            slot_i = slot_iota[:].bitcast(I32)
            link(pool.iota(slot_i, pattern=[[0, 2], [1, SLOTS]], base=0, channel_multiplier=0))
            link(pool.tensor_copy(slot_iota[:], slot_i))
            tok_i = tok_id[:].bitcast(I32)
            link(pool.iota(tok_i, pattern=[[P, T]], base=-OOB, channel_multiplier=1))
            link(pool.tensor_copy(tok_id[:], tok_i))
            link(pool.memset(row_off[:], float(OOB)))
            link(pool.memset(row_off[SLOTS:P, 1:2], float(OOB + 2 * S)))
            pool.memset(y_pad[:, :, 0:PAD], 0.0).then_inc(pool_consts, 1)
            def ada_round(r):
                for k in range(1, KC):
                    n = r * KC + k
                    adds = (r - 1) * (KC - 1) + k - 1
                    pool.wait_ge(ada_scaled, n - KC + 1)
                    if k == 1:
                        if r > 1:
                            pool.wait_ge(ada_summed, r - 1)
                        left = ada_buf((n - 1) % ADA_BUFS)
                    else:
                        pool.wait_ge(ada_added, adds)
                        left = ada_acc
                    pool.tensor_tensor(ada_acc, left, ada_buf(n % ADA_BUFS), ALU.add).then_inc(ada_added, 1)

            pool.wait_ge(xn_turned, 2)
            ada_round(1)
            pool.wait_ge(consts_in, 16 * N_CONST)
            link(pool.tensor_copy(w_router[:, :, 0:G], coarse_raw))
            for g in range(G):
                copied = pool.tensor_copy(w_router[:, :, G + g * EG:G + (g + 1) * EG], fine_raw[:, g])
                if g < G - 1:
                    link(copied)
            copied.then_inc(router_packed, 1)
            ada_round(2)

            pool.wait_ge(mix_done, 2 * T)
            pool.tensor_copy(row_vals[:, :, :, 0], tok_id[:].unsqueeze(2).to_broadcast([P, T, NE])
                             ).then_inc(rows_from, 1)
            link(pool.memset(xg, 0.0))
            pool.wait_ge(logits_done, T)
            link(pool.memset(xg_x, 0.0))

            def gather(e, b, r, wait_buffer):
                pool.wait_ge(rows_ready, e + 1)
                if wait_buffer:
                    pool.wait_ge(xg_turned, e - XG + 1)
                pool.sem_inc(pool_go, 1)
                pool.indirect_dma_start(
                    xg[0:SLOTS, b].rearrange("p k n -> p (k n)"), None, xn_rows,
                    bass.IndirectOffsetOnAxis(row_idx[0:SLOTS, r, 0:1], 0),
                    bounds_check=S - 1, oob_is_err=False).then_inc(gathered[b], 16)

            def scatter(e, b, r):
                pool.wait_ge(y_ready, e + 1)
                pool.sem_inc(pool_go, 1)
                pool.indirect_dma_start(
                    y_rows, bass.IndirectOffsetOnAxis(row_idx[:, r, 1:2], 0), y_exp[:, b], None,
                    bounds_check=4 * S - 1, oob_is_err=False).then_inc(scattered[b], 16)

            for b in range(2):
                pool.wait_ge(xn2_stored[b], 16 * T // 2)
            for e in range(AHEAD + 1):
                gather(e, e % XG, e % ROWS, e >= XG)
            pool.sem_inc(ov_free, 1)
            pool.wait_ge(routed, 1)

            def extra(e):
                with extra_blocks(pool, e) as n:
                    pool.wait_ge(ov_rows, n + 1)
                    pool.sem_inc(pool_go, 1)
                    pool.indirect_dma_start(
                        xg_x[0:SLOTS].rearrange("p k n -> p (k n)"), None, xn_rows,
                        bass.IndirectOffsetOnAxis(row_idx_x[0:SLOTS, 0:1], 0),
                        bounds_check=S - 1, oob_is_err=False).then_inc(ov_gathered, 16)
                    pool.wait_ge(ov_y, n + 1)
                    pool.sem_inc(pool_go, 1)
                    pool.indirect_dma_start(
                        y_rows, bass.IndirectOffsetOnAxis(row_idx_x[:, 1:2], 0), y_exp_x, None,
                        bounds_check=4 * S - 1, oob_is_err=False).then_inc(ov_scattered, 16)
                    pool.wait_ge(ov_scattered, 16 * n + 16)
                    pool.sem_inc(ov_free, 1)

            for e in range(3):
                if e:
                    gather(e + AHEAD, (e + AHEAD) % XG, (e + AHEAD) % ROWS, True)
                    scatter(e - 1, (e - 1) % YB, (e - 1) % ROWS)
                extra(e)
            with pool.Fori(0, 2) as i:
                for r in range(ROWS):
                    e = 3 + ROWS * i + r
                    gather(e + AHEAD, (3 + r + AHEAD) % XG, (3 + r + AHEAD) % ROWS, True)
                    scatter(e - 1, (2 + r) % YB, (2 + r) % ROWS)
                    extra(e)
            for e in range(3 + 2 * ROWS, NE):
                if e + AHEAD < NE:
                    gather(e + AHEAD, (e + AHEAD) % XG, (e + AHEAD) % ROWS, True)
                scatter(e - 1, (e - 1) % YB, (e - 1) % ROWS)
                extra(e)
            scatter(NE - 1, (NE - 1) % YB, (NE - 1) % ROWS)
            for b in range(YB):
                pool.wait_ge(scattered[b], 16 * len(range(b, NE, YB)))
            pool.sem_inc(all_scattered, 1)

            pool.wait_ge(gfin_in, 16)
            for t in range(2):
                pool.wait_ge(x3_normed, t + 1)
                pool.tensor_tensor(acc[:, t, :], acc[:, t, :], gfin, ALU.mult).then_inc(out_ready, 1)

        @block.scalar
        def _(act):
            done = [0]

            def link(ins):
                ins.then_inc(act_order, 1)
                done[0] += 1
                act.wait_ge(act_order, done[0])

            act.dma_start(c_col[:], col_of(c)).then_inc(c_in, 16)
            flat = "l g d -> l (g d)"
            for row, src in (
                (0, conv_w[0]), (TAPS, conv_b), (TAPS + 1, conv_ln_g.rearrange(flat)),
                (TAPS + 2, conv_ln_b.rearrange(flat)), (TAPS + 3, sgu_ln_g.rearrange(flat)),
                (TAPS + 4, sgu_ln_b.rearrange(flat)), (TAPS + 5, g_mix.rearrange("l (h n) -> (l h) n", h=2)),
            ):
                act.dma_start(conv_raw[row:row + src.shape[0]], src).then_inc(rows_in, 16)
            act.wait_ge(c_in, 16)
            act.activation(c_col[:], c_col[:], ACT.Silu).then_inc(c_act_ready, 1)
            act.wait_ge(norm_ready, 1)
            for t in range(T):
                act.wait_ge(x_in[t], 16)
                link(act.activation(xn[:, t, :], x_sb[:, t, :], ACT.Square, accum_out=stat[:, 0, t:t + 1]))
                act.activation(stat[:, 1, t:t + 1], stat[:, 0, t:t + 1], ACT.Sqrt, bias=eps_col[:],
                               scale=1.0 / D).then_inc(x_root, 1)
            act.wait_ge(xn_turned, 1)
            for k in range(1, KC, 2):
                if k == KC - 1:
                    act.wait_ge(xn_turned, 2)
                act.copy(h_t[:, k, :], ps[:, XN_BANK[k], :]).then_inc(xnt_ready_act, 1)

            def mod_cols(r, rows, pairs):
                act.wait_ge(mod_rows_ready, r + 1)
                for q, v in pairs:
                    part = slice((q % 2) * P // 2, (q % 2) * P // 2 + P // 2)
                    act.dma_start(mod_col[part, v, :], rows[32 * q:32 * q + 1, :].rearrange(
                        "o (p k) -> o p k", k=KC)).then_inc(mod_cols_in[r - 1], 16)

            act.wait_ge(a1_ready, 1)
            act.wait_ge(xnt_ready_act, KC // 2)
            for k in range(1, KC, 2):
                act.activation(h_t[:, k, :], h_t[:, k, :], ACT.Identity, bias=mod1_nat[:, 0, k:k + 1],
                               scale=a1_col[:, k:k + 1]).then_inc(h_act, 1)

            for dst, src in (
                (w_sgu_raw, sgu_w[0].rearrange("h t s -> t h s")),
                (gffn_col[:], col_of(g_ffn)),
                (coarse_raw, w_coarse[0].rearrange("(p k) g -> p k g", k=KC)),
                (fine_raw, w_fine[0].rearrange("g (p k) e -> p g k e", k=KC)),
                (b_router[:, 0:G], b_coarse.to_broadcast([P, G])),
                (b_router[:, G:NR], b_fine.rearrange("l g e -> l (g e)").to_broadcast([P, NE])),
            ):
                act.dma_start(dst, src).then_inc(consts_in, 16)

            def ada_scale(first, last):
                for u in range(first, last):
                    n = KC + u
                    act.wait_ge(ada_in[n % ADA_BUFS], 16 * (n // ADA_BUFS + 1))
                    act.wait_ge(c_act_ready, 1)
                    act.activation(ada_buf(n % ADA_BUFS), ada_buf(n % ADA_BUFS), ACT.Copy,
                                   scale=c_col[:, n % KC:n % KC + 1]).then_inc(ada_scaled, 1)

            for i in range(CT):
                act.wait_ge(z_done, 2 * i + 2)
                if i >= 2:
                    act.wait_ge(glu_ready, i - 1)
                act.activation(sig[:, i % 2, :], ps[:, (2 * i + 1) % 4, :], ACT.Sigmoid).then_inc(sig_ready, 1)
                ada_scale((0, 3, 5, 8)[i], (3, 5, 8, 10)[i])

            def ln_square(n):
                act.wait_ge(ln_centred, n + 1)
                if n >= 1:
                    act.wait_ge(ln_var, n)
                act.activation(ln_sq, ln_yc[:, n % 2, :], ACT.Square).then_inc(ln_squared, 1)

            def ln_sqrt(n):
                act.wait_ge(ln_var, n + 1)
                if n >= 1:
                    act.wait_ge(ln_normed, n)
                act.activation(ln_root, ps[:, 6, :], ACT.Sqrt, bias=eps_col[:]).then_inc(ln_rooted, 1)

            def v_scale(n):
                act.wait_ge(ln_normed, n + 1)
                act.activation(v_t[:, n, :], v_t[:, n, :], ACT.Identity, bias=conv_c[:, n, TAPS + 4:TAPS + 5],
                               scale=conv_c[:, n, TAPS + 3:TAPS + 4]).then_inc(v_scaled, 1)

            def v_out(n):
                act.wait_ge(v_turned, n + 1)
                act.copy(v_sb[:, :, n * P:(n + 1) * P], ps[:, 7, :].rearrange("p (t n) -> p t n", t=T)
                         ).then_inc(v_ready, 1)

            for n in range(2 * CT, 4 * CT):
                act.wait_ge(z_done, n + 1)
                dst = v_t[:, n - 2 * CT, :] if n < 3 * CT else y_cat[:, n - 2 * CT, :]
                act.activation(dst, ps[:, n % 4, :], ACT.Gelu_apprx_tanh).then_inc(gelu_ready, 1)
                if n == 2 * CT + 2:
                    mod_cols(1, mod01[:, 1], [(q, 0) for q in (2, 3)])
                if n >= 10:
                    ln_sqrt(n - 10)
                if 10 <= n < 14:
                    v_scale(n - 10)
                if n >= 9:
                    ln_square(n - 9)
                if 9 <= n < 11:
                    act.wait_ge(gt1_spread, n - 8)
                    act.copy(gt1b[:, (n - 9) * HALF:(n - 8) * HALF], ps[:, 7, :]).then_inc(gt1_ready, 1)
                if 11 <= n < 15:
                    v_out(n - 11)
                if n < 3 * CT:
                    ada_scale(*((10, 12), (12, 13), (13, 14), (14, 16))[n - 2 * CT])
                if n == 15:
                    mod_cols(2, mod2[:], [(q, 1) for q in (0, 1)])
            for n in range(6, 8):
                ln_sqrt(n)
                if n + 1 < 8:
                    ln_square(n + 1)
            for i in range(CT):
                act.wait_ge(ln_normed, CT + i + 1)
                act.activation(y_cat[:, i, :], y_cat[:, i, :], ACT.Silu, bias=conv_c[:, i, TAPS + 2:TAPS + 3],
                               scale=conv_c[:, i, TAPS + 1:TAPS + 2]).then_inc(conv_out, 1)

            def norm2(t):
                row = xn2[:, t % 2].rearrange("p k n -> p (k n)")
                act.wait_ge(x2_ready, 2 * t + 2)
                if t >= 2:
                    act.wait_ge(xn2_stored[t % 2], 16)
                    act.wait_ge(xn2_turned, t - 1)
                link(act.activation(row, x_sb[:, t, :], ACT.Square, accum_out=stat[:, 2, t:t + 1]))
                act.activation(stat[:, 3, t:t + 1], stat[:, 2, t:t + 1], ACT.Sqrt, bias=eps_col[:],
                               scale=1.0 / D).then_inc(x2_root, 1)
                act.wait_ge(xn2_ready, t + 1)
                act.dma_start(xn_rows[t * P:(t + 1) * P, :], row).then_inc(xn2_stored[t % 2], 16)

            def h2_out(t):
                act.wait_ge(xn2_turned, t + 1)
                act.wait_ge(a2_ready, 1)
                for k in range(KC // 2, KC):
                    act.activation(y_cat[:, k, t * P:(t + 1) * P], ps[:, 4 + k // 4, (k % 4) * P:(k % 4 + 1) * P],
                                   ACT.Identity, bias=mod_col[:, 0, k:k + 1], scale=a2_col[:, k:k + 1]
                                   ).then_inc(h2_act, 1)

            norm2(0)
            norm2(1)
            h2_out(0)
            norm2(2)
            h2_out(1)
            h2_out(2)
            norm2(3)
            h2_out(3)
            act.wait_ge(neg_max_ready, 1)
            for t in range(T):
                act.activation(c_exp[:, t, 0:G], logits[:, t, 0:G], ACT.Exp, bias=neg_max[:, t:t + 1],
                               accum_out=p_grp[:, t:t + 1]).then_inc(c_exp_ready, 1)
            act.wait_ge(diff_ready, 1)
            act.activation(e_diff, e_diff, ACT.Exp).then_inc(diff_exp, 1)
            act.wait_ge(gt2_spread, 1)
            act.copy(gt2_exp, ps[:, 0, :]).then_inc(gt2_ready, 1)

            def turn_out(dst, bank, used, at, got):
                act.wait_ge(used, at)
                for k in range(KC):
                    last = act.activation(dst[:, k, :], ps[:, bank, k * SLOTS:(k + 1) * SLOTS], ACT.Identity,
                                          bias=mod_col[:, 0, k:k + 1], scale=a2_col[:, k:k + 1])
                last.then_inc(got, 1)

            def silu(dst, bank, used, at, got):
                act.wait_ge(used, at)
                act.activation(dst, ps[:, bank, 0:P], ACT.Silu).then_inc(got, 1)

            def expert_step(e, b2, first, last):
                if not last:
                    if not first:
                        act.wait_ge(gate_up_done, e)
                    turn_out(xt[:, 1 - b2], 1 - b2, xg_turned, e + 2, xt_ready)
                if not first:
                    act.wait_ge(hid_ready, e)
                silu(gate_act[:, b2, :], 2 + b2, gate_up_done, e + 1, silu_ready)
                with extra_blocks(act, e) as n:
                    turn_out(xt_x, b2, ov_turned, n + 1, ov_xt)
                    silu(gate_act_x, 3 - b2, ov_gate_up, n + 1, ov_silu)

            turn_out(xt[:, 0], 0, xg_turned, 1, xt_ready)
            act.wait_ge(routed, 1)
            expert_step(0, 0, True, False)
            with act.Fori(0, 5) as i:
                for r in range(RING):
                    expert_step(1 + RING * i + r, (1 + r) % 2, False, False)
            expert_step(NE - 1, (NE - 1) % 2, False, True)

            for t in range(T):
                act.wait_ge(x3_ready, 2 * t + 2)
                link(act.activation(acc[:, t, :], x_sb[:, t, :], ACT.Square, accum_out=stat[:, 4, t:t + 1]))
                act.activation(stat[:, 5, t:t + 1], stat[:, 4, t:t + 1], ACT.Sqrt, bias=eps_col[:],
                               scale=1.0 / D).then_inc(x3_root, 1)
                if t < 2:
                    act.wait_ge(x3_rstd, t + 1)
                    act.activation(acc[:, t, :], x_sb[:, t, :], ACT.Copy, scale=stat[:, 6, t:t + 1]
                                   ).then_inc(x3_normed, 1)

        @block.vector
        def _(dve):
            done = [0]

            def link(ins):
                ins.then_inc(dve_order, 1)
                done[0] += 1
                dve.wait_ge(dve_order, done[0])

            dve.wait_ge(c_act_ready, 1)
            dve.tensor_copy(c_rep, c_col[:].unsqueeze(2).to_broadcast([P, KC, 32])).then_inc(c_rep_ready, 1)
            for t in range(T):
                dve.wait_ge(x_root, t + 1)
                link(dve.reciprocal(stat[:, 6, t:t + 1], stat[:, 1, t:t + 1]))
                dve.tensor_scalar(xn[:, t, :], x_sb[:, t, :], stat[:, 6, t:t + 1], None, ALU.mult
                                  ).then_inc(xn_ready, 1)
            dve.wait_ge(xn_turned, 1)
            for k in range(0, KC, 2):
                dve.tensor_copy(h_t[:, k, :], ps[:, XN_BANK[k], :]).then_inc(xnt_ready_dve, 1)

            def mod_rows(r, rows, bank):
                if r:
                    dve.wait_ge(ada_summed, r)
                else:
                    dve.wait_ge(ada_used, KC)
                dve.tensor_tensor(rows, ps[:, bank, :], bada_sb[:, r, :], ALU.add).then_inc(mod_rows_ready, 1)

            dve.wait_ge(bada_in, 64)
            dve.wait_ge(xn_turned, 2)
            mod_rows(0, mod01[:, 0], 4)
            dve.wait_ge(conv_c_turned, 1)
            dve.tensor_copy(conv_c[:], ps[:, 7, 0:CT * NV].rearrange("p (i n) -> p i n", i=CT)
                            ).then_inc(conv_c_ready, 1)
            dve.wait_ge(mod0_turned, 1)
            dve.tensor_copy(mod1_nat[:].rearrange("p v (h j) -> p (v h) j", h=2),
                            ps[:, 5, :].rearrange("p (j q m) -> p q j m", j=4, q=4)[:, :, :, 0]
                            ).then_inc(mod1_ready, 1)
            dve.wait_ge(mod1_ready, 1)
            dve.wait_ge(conv_c_ready, 1)
            dve.scalar_tensor_tensor(a1_col[:].rearrange("p (h j) -> p h j", h=2),
                                     mod1_nat[:, 1, :].rearrange("p (h j) -> p h j", h=2), 1.0,
                                     conv_c[:, :, TAPS + 5:TAPS + 7].rearrange("p j h -> p h j"),
                                     ALU.add, ALU.mult).then_inc(a1_ready, 1)
            dve.wait_ge(a1_ready, 1)
            dve.wait_ge(xnt_ready_dve, KC // 2)
            for k in range(0, KC, 2):
                dve.tensor_scalar(h_t[:, k, :], h_t[:, k, :], a1_col[:, k:k + 1], mod1_nat[:, 0, k:k + 1],
                                  ALU.mult, ALU.add).then_inc(h_dve, 1)
            dve.wait_ge(pool_consts, 1)

            def glu(i):
                dve.wait_ge(sig_ready, i + 1)
                dve.tensor_tensor(y_pad[:, i, PAD:PAD + S], ps[:, (2 * i) % 4, :], sig[:, i % 2, :], ALU.mult
                                  ).then_inc(glu_ready, 1)

            steps, tap_at = [0], {}

            def conv(pair, first, last):
                for k in range(first, last):
                    for i in pair:
                        if k == 0:
                            dve.wait_ge(glu_ready, i + 1)
                            ins = dve.tensor_scalar(y_cat[:, i, :], y_pad[:, i, 0:S], conv_c[:, i, 0:1],
                                                    conv_c[:, i, TAPS:TAPS + 1], ALU.mult, ALU.add)
                        else:
                            dve.wait_ge(conv_step, tap_at[i])
                            ins = dve.scalar_tensor_tensor(y_cat[:, i, :], y_pad[:, i, k:k + S],
                                                           conv_c[:, i, k:k + 1], y_cat[:, i, :],
                                                           ALU.mult, ALU.add)
                        ins.then_inc(conv_step, 1)
                        steps[0] += 1
                        tap_at[i] = steps[0]

            def ln_centre(n):
                src = v_t[:, n, :] if n < CT else y_cat[:, n - CT, :]
                dve.wait_ge(ln_mean, n + 1)
                dve.tensor_tensor(ln_yc[:, n % 2, :], src, ps[:, 5, :], ALU.subtract).then_inc(ln_centred, 1)

            def ln_norm(n):
                dst = v_t[:, n, :] if n < CT else y_cat[:, n - CT, :]
                dve.wait_ge(ln_rooted, n + 1)
                dve.reciprocal(ln_root, ln_root).then_inc(ln_rstd, 1)
                dve.wait_ge(ln_rstd, n + 1)
                dve.tensor_tensor(dst, ln_yc[:, n % 2, :], ln_root, ALU.mult).then_inc(ln_normed, 1)

            def sgu_weights(j):
                dve.wait_ge(sgu_w_turned, j + 1)
                dve.tensor_tensor(w_sgu_t[:, 4 * j:4 * j + 4, :],
                                  ps[:, 7 - j, :].rearrange("p (h n) -> p h n", h=4),
                                  tri.unsqueeze(1).to_broadcast([P, 4, P]), ALU.mult).then_inc(sgu_w_ready, 1)

            glu(0)
            conv((0,), 0, 18)
            glu(1)
            conv((1,), 0, 18)
            glu(2)
            conv((0, 1), 18, 26)
            glu(3)
            conv((0, 1), 26, TAPS)
            for j in range(2):
                sgu_weights(j)
            mod_rows(1, mod01[:, 1], 4)
            conv((2, 3), 0, TAPS_BY[0])
            for n in range(CT + 2):
                ln_centre(n)
                conv((2, 3), TAPS_BY[n], TAPS_BY[n + 1])
                if n == 5:
                    mod_rows(2, mod2[:], 4)
                ln_norm(n)
            dve.wait_ge(conv_step, TAPS * CT)
            ln_centre(CT + 2)
            for i in range(CT):
                dve.wait_ge(sgu_mixed, 1)
                dve.wait_ge(sgu_rows_in, 16 * HEADS)
                bank = ps[:, i, :].rearrange("p (c n) -> p c n", c=T)
                link(dve.tensor_tensor(bank, bank, sgu_b_row[:, i, :].unsqueeze(1).to_broadcast([P, T, P]),
                                       ALU.add))
                dve.tensor_tensor(y_cat[:, CT + i, :], ps[:, i, :], y_cat[:, CT + i, :], ALU.mult
                                  ).then_inc(sgu_out, 1)

            ln_norm(CT + 2)
            ln_centre(CT + 3)
            ln_norm(CT + 3)
            dve.wait_ge(mod_cols_in[0], 32)
            dve.wait_ge(mod_cols_in[1], 32)
            dve.scalar_tensor_tensor(a2_col[:], mod_col[:, 1, :], 1.0, gffn_col[:], ALU.add, ALU.mult
                                     ).then_inc(a2_ready, 1)

            dve.wait_ge(gt1_ready, 2)

            def residual(t):
                for h in range(2):
                    bank = 2 * (t % 2) + h
                    cols = slice(h * HALF, (h + 1) * HALF)
                    dve.wait_ge(mix_done, 2 * t + h + 1)
                    link(dve.tensor_tensor(ps[:, bank, :], ps[:, bank, :], gt1b[:, cols], ALU.mult))
                    dve.tensor_tensor(x_sb[:, t, cols], x_sb[:, t, cols], ps[:, bank, :], ALU.add
                                      ).then_inc(x2_ready, 1)
                dve.wait_ge(x2_root, t + 1)
                dve.wait_ge(x2_ready, 2 * t + 2)
                link(dve.reciprocal(stat[:, 7, t:t + 1], stat[:, 3, t:t + 1]))
                dve.tensor_scalar(xn2[:, t % 2], x_sb[:, t, :].rearrange("p (n k) -> p k n", k=KC),
                                  stat[:, 7, t:t + 1], None, ALU.mult).then_inc(xn2_ready, 1)

            def router_in(t):
                dve.wait_ge(xn2_turned, t + 1)
                dve.wait_ge(a2_ready, 1)
                for k in range(KC // 2):
                    dve.tensor_scalar(y_cat[:, k, t * P:(t + 1) * P], ps[:, 4 + k // 4, (k % 4) * P:(k % 4 + 1) * P],
                                      a2_col[:, k:k + 1], mod_col[:, 0, k:k + 1], ALU.mult, ALU.add
                                      ).then_inc(h2_dve, 1)

            def logits_out(t):
                dve.wait_ge(logits_done, t + 1)
                dve.tensor_tensor(logits[:, t, :], ps[:, 6 + t % 2, 0:NR], b_router[:], ALU.add
                                  ).then_inc(logits_ready, 1)

            residual(0)
            residual(1)
            router_in(0)
            residual(2)
            logits_out(0)
            router_in(1)
            router_in(2)
            logits_out(1)
            residual(3)
            logits_out(2)
            router_in(3)
            logits_out(3)
            dve.wait_ge(logits_ready, T)

            link(dve.memset(coarse8, -3.0e38))
            link(dve.tensor_copy(coarse8[:, :, 0:G], logits[:, :, 0:G]))
            for t in range(T):
                last = dve.max(top_c[:, t, :], coarse8[:, t, :])
            link(last)
            dve.tensor_scalar(neg_max, top_c[:, :, 0], -1.0, None, ALU.mult).then_inc(neg_max_ready, 1)
            for t in range(T):
                last = dve.max_index(top_ci[:, t, :], top_c[:, t, :], coarse8[:, t, :])
            link(last)
            small = slot_iota[:, 0:G].unsqueeze(1).to_broadcast([P, T, G])
            link(dve.tensor_tensor(grp_hot, small, top_ci[:, :, 0:1].to_broadcast([P, T, G]), ALU.is_equal))
            for t in range(T):
                last = dve.tensor_tensor(fine_m[:, t], logits[:, t, G:NR].rearrange("p (g e) -> p g e", g=G),
                                         grp_hot[:, t, :].unsqueeze(2).to_broadcast([P, G, EG]), ALU.mult)
            link(last)
            link(dve.reduce_sum(fine_s, fine_m.rearrange("p t g e -> p t e g"), AX_X))
            for t in range(T):
                last = dve.max(top_f[:, t, :], fine_s[:, t, :])
            link(last)
            dve.tensor_tensor(e_diff, top_f[:, :, 1], top_f[:, :, 0], ALU.subtract).then_inc(diff_ready, 1)
            for t in range(T):
                last = dve.max_index(top_fi[:, t, :], top_f[:, t, :], fine_s[:, t, :])
            link(last)
            for k in range(2):
                last = dve.scalar_tensor_tensor(expert_k[:, k, :], top_ci[:, :, 0], float(EG), top_fi[:, :, k],
                                                ALU.mult, ALU.add)
            link(last)
            wide = slot_iota[:, 0:NE].unsqueeze(1).to_broadcast([P, T, NE])
            for k, hot in enumerate((hot0, hot1)):
                last = dve.tensor_tensor(hot, wide, expert_k[:, k, :].unsqueeze(2).to_broadcast([P, T, NE]),
                                         ALU.is_equal)
            link(last)
            dve.tensor_tensor(hot16, hot0, hot1, ALU.add).then_inc(hot_ready, 1)
            dve.wait_ge(rows_from, 1)
            dve.scalar_tensor_tensor(row_vals[:, :, :, 1], hot1, float(S), row_vals[:, :, :, 0], ALU.mult, ALU.add
                                     ).then_inc(dve_order, 1)
            done[0] += 1
            link(dve.memset(place[:, :, NE:NE + 1], 0.0))
            dve.wait_ge(counted, 1)
            dve.wait_ge(hot_ready, 1)
            link(dve.scalar_tensor_tensor(place[:, :, 0:NE],
                                          ps[:, 7, 0:T * NE].rearrange("p (t e) -> p t e", t=T), 1.0, hot16,
                                          ALU.add, ALU.mult))
            link(dve.tensor_scalar(place, place, -1.0, None, ALU.add))
            dve.tensor_copy(blocks_f[:, 1, :], ps[:, 7, T * NE:T * NE + NE]).then_inc(places_ready, 1)

            iota_b = slot_iota[:].unsqueeze(1).to_broadcast([P, T, P])

            def pick(e, dst, got):
                dve.tensor_tensor(dst, iota_b, place[:, :, bass.ds(e, 1)].to_broadcast([P, T, P]),
                                  ALU.is_equal).then_inc(got, 1)

            def rows(dst, used, at, got):
                dve.wait_ge(used, at)
                dve.tensor_tensor(dst, ps[:, 7, 0:2], row_off[:], ALU.add).then_inc(got, 1)

            def hidden(dst, act_in, bank, used, at, got):
                dve.wait_ge(used, at)
                dve.tensor_tensor(dst, act_in, ps[:, bank, P:2 * P], ALU.mult).then_inc(got, 1)

            def hidden_t(dst, used, at, got):
                dve.wait_ge(used, at)
                dve.tensor_copy(dst, ps[:, 4, 0:P]).then_inc(got, 1)

            def y_out(dst, bank, used, at, got):
                dve.wait_ge(used, at)
                dve.tensor_tensor(dst, ps[:, bank, :], gt2_exp, ALU.mult).then_inc(got, 1)

            def step(e, b2, r, yb, first, pick_next, rows_next, scat):
                if pick_next:
                    dve.wait_ge(rows_found, e + AHEAD)
                    pick(e + AHEAD + 1, picks[:, 1 - b2], picks_ready)
                if rows_next:
                    rows(row_idx[:, r, :], rows_found, e + AHEAD + 1, rows_ready)
                if first < 2:
                    dve.wait_ge(hid_turned, e - 1)
                hidden(hid[:, b2, :], gate_act[:, b2, :], 2 + b2, silu_ready, e + 1, hid_ready)
                if first < 3:
                    if scat is not None:
                        dve.wait_ge(*scat)
                    y_out(y_exp[:, yb], 6 - b2, down_done, e, y_ready)
                hidden_t(hid_t[:, b2, :], hid_turned, e + 1, hid_t_ready)
                with extra_blocks(dve, e) as n:
                    past = place[:, :, bass.ds(e, 1)]
                    dve.tensor_scalar(past, past, -float(SLOTS), None, ALU.add).then_inc(ov_place, 1)
                    dve.wait_ge(ov_place, n + 1)
                    pick(e, picks_x, ov_picks)
                    dve.wait_ge(ov_free, n + 1)
                    rows(row_idx_x, ov_found, n + 1, ov_rows)
                    hidden(hid_x, gate_act_x, 3 - b2, ov_silu, n + 1, ov_hid)
                    hidden_t(hid_t_x, ov_hid_turned, n + 1, ov_hid_t)
                    y_out(y_exp_x, 5 + b2, ov_down, n + 1, ov_y)

            for e in range(AHEAD + 1):
                if e >= 2:
                    dve.wait_ge(rows_found, e - 1)
                pick(e, picks[:, e % 2], picks_ready)
                if e >= 1:
                    rows(row_idx[:, e - 1, :], rows_found, e, rows_ready)
            info = block_info[:, 0, :]
            dve.wait_ge(places_ready, 1)
            link(dve.tensor_scalar(info, blocks_f[:, 1, :], float(SLOTS - 1), None, ALU.add))
            link(dve.tensor_scalar(info, info, 6, None, ALU.logical_shift_right))
            link(dve.tensor_scalar(blocks_f[:, 0, :], info, -1.0, 0.0, ALU.add, ALU.max))
            link(dve.tensor_tensor_scan(blocks_f[:, 1, :], blocks_f[:, 0, :], blocks_f[:, 0, :], 0.0,
                                        ALU.add, ALU.bypass))
            dve.tensor_tensor(block_info[:, 1, :], blocks_f[:, 1, :], blocks_f[:, 0, :], ALU.subtract
                              ).then_inc(routed, 1)
            dve.wait_ge(c_exp_ready, T)
            dve.wait_ge(diff_exp, 1)
            link(dve.reciprocal(p_grp, p_grp))
            link(dve.tensor_scalar(grp, e_diff, 1.0, None, ALU.add))
            link(dve.reciprocal(grp, grp))
            link(dve.tensor_tensor(gate_k[:, 0, :], grp, p_grp, ALU.mult))
            link(dve.tensor_tensor(gate_k[:, 1, :], gate_k[:, 0, :], e_diff, ALU.mult))
            dve.wait_ge(routed, 1)
            dve.wait_ge(gt2_ready, 1)
            for e in range(YB + 1):
                step(e, e % 2, (e + AHEAD) % ROWS, (e - 1) % YB, max(3 - e, 0), True, True, None)
            with dve.Fori(0, 2) as i:
                for r in range(ROWS):
                    step(YB + 1 + ROWS * i + r, (YB + 1 + r) % 2, (YB + 1 + r + AHEAD) % ROWS, r % YB, 0, True, True,
                         (scattered[r % YB], 16 * (ROWS // YB * i + r // YB + 1)))
            for e in range(YB + 1 + 2 * ROWS, NE):
                step(e, e % 2, (e + AHEAD) % ROWS, (e - 1) % YB, 0, False, False,
                     (scattered[(e - 1) % YB], 16 * ((e - 1) // YB)))
            dve.wait_ge(scattered[(NE - 1) % YB], 16 * ((NE - 1) // YB))
            y_out(y_exp[:, (NE - 1) % YB], 6, down_done, NE, y_ready)

            def gated(t):
                for k in range(2):
                    dve.wait_ge(y_in[t], 32)
                    if k:
                        dve.wait_ge(x3_ready, 2 * t + 1)
                    dve.scalar_tensor_tensor(x_sb[:, t, :], y_back[:, t, k].rearrange("p h n -> p (h n)"),
                                             gate_k[:, k, t:t + 1], x_sb[:, t, :], ALU.mult, ALU.add
                                             ).then_inc(x3_ready, 1)

            def rstd3(t):
                dve.wait_ge(x3_root, t + 1)
                dve.reciprocal(stat[:, 6, t:t + 1], stat[:, 5, t:t + 1]).then_inc(x3_rstd, 1)

            gated(0)
            for t in range(T):
                if t + 1 < T:
                    gated(t + 1)
                rstd3(t)
                if t >= 2:
                    dve.wait_ge(x3_rstd, t + 1)
                    dve.wait_ge(gfin_in, 16)
                    dve.scalar_tensor_tensor(acc[:, t, :], x_sb[:, t, :], stat[:, 6, t:t + 1], gfin,
                                             ALU.mult, ALU.mult).then_inc(last_out_ready, 1)

        @block.tensor
        def _(pe):
            pe.wait_ge(norm_ready, 1)
            def ada(n, bank):
                k = n % KC
                pe.wait_ge(ada_in[n % ADA_BUFS], 16 * (n // ADA_BUFS + 1))
                for q in range(4):
                    last = pe.matmul(ps[32 * q:32 * q + 32, bank, :], c_rep[:, k, :],
                                     ada_buf(n % ADA_BUFS)[:, q * HALF:(q + 1) * HALF],
                                     start=(k == 0), stop=(k == KC - 1))
                last.then_inc(ada_used, 1)

            pe.wait_ge(c_rep_ready, 1)
            for t in range(T):
                ada(t, 4)
                pe.wait_ge(xn_ready, t + 1)
                for k in range(KC - 1):
                    last = pe.transpose(ps[:, XN_BANK[k], t * P:(t + 1) * P], xn[:, t, k * P:(k + 1) * P], ident[:])
            last.then_inc(xn_turned, 1)
            pe.wait_ge(xnt_ready_dve, 1)
            for t in range(T):
                last = pe.transpose(ps[:, XN_BANK[KC - 1], t * P:(t + 1) * P], xn[:, t, D - P:D], ident[:])
            last.then_inc(xn_turned, 1)
            for n in range(T, KC):
                ada(n, 4)
            pe.wait_ge(rows_in, 16 * 7)
            pe.wait_ge(xnt_ready_dve, KC // 2)
            pe.wait_ge(xnt_ready_act, KC // 2)
            for i in range(CT):
                last = pe.transpose(ps[:, 7, i * NV:(i + 1) * NV], conv_raw[:, i * P:(i + 1) * P],
                                    ident[0:NV, 0:NV])
            last.then_inc(conv_c_turned, 1)
            pe.wait_ge(mod_rows_ready, 1)
            for j in range(4):
                last = pe.transpose(ps[:, 5, j * P:(j + 1) * P], mod01[:, 0, j * P:(j + 1) * P], ident[:])
            last.then_inc(mod0_turned, 1)

            def z_tile(n):
                bank = n % 4
                if n >= 4:
                    if n < 2 * CT + 4:
                        old = n - 4
                        if old < 2 * CT:
                            pe.wait_ge(sig_ready if old % 2 else glu_ready, old // 2 + 1)
                    if n - 4 >= 2 * CT:
                        pe.wait_ge(gelu_ready, n - 4 - 2 * CT + 1)
                if n < 2 * CT:
                    q, w, cols = n % 2, (win_a, win_g)[n % 2], n // 2
                elif n < 3 * CT:
                    q, w, cols = 3, win_v, n - 2 * CT
                else:
                    q, w, cols = 2, win_u, n - 3 * CT
                pe.wait_ge(win_in[q], 16)
                for k in range(KC):
                    if n == 0:
                        pe.wait_ge(h_act if k % 2 else h_dve, k // 2 + 1)
                    last = pe.matmul(ps[:, bank, :], w[:, k, cols * P:(cols + 1) * P], h_t[:, k, :],
                                     start=(k == 0), stop=(k == KC - 1))
                last.then_inc(z_done, 1)

            def ln_mean_of(n):
                if n < CT:
                    pe.wait_ge(gelu_ready, n + 1)
                else:
                    pe.wait_ge(conv_step, TAPS * CT if n >= CT + 2 else TAPS * 2)
                if n >= 1:
                    pe.wait_ge(ln_centred, n)
                src = v_t[:, n, :] if n < CT else y_cat[:, n - CT, :]
                pe.matmul(ps[:, 5, :], group_mean[:], src, start=True, stop=True).then_inc(ln_mean, 1)

            def ln_var_of(n):
                pe.wait_ge(ln_squared, n + 1)
                if n >= 1:
                    pe.wait_ge(ln_rooted, n)
                pe.matmul(ps[:, 6, :], group_mean[:], ln_sq, start=True, stop=True).then_inc(ln_var, 1)

            def turn_v(n):
                pe.wait_ge(v_scaled, n + 1)
                if n >= 1:
                    pe.wait_ge(v_ready, n)
                else:
                    pe.wait_ge(gt1_ready, 2)
                for t in range(T):
                    last = pe.transpose(ps[:, 7, t * P:(t + 1) * P], v_t[:, n, t * P:(t + 1) * P], ident[:])
                last.then_inc(v_turned, 1)

            for n in range(4 * CT):
                z_tile(n)
                if n in (8, 14):
                    r = 1 if n == 8 else 2
                    pe.wait_ge(mod_rows_ready, r)
                    pe.wait_ge(ada_added, (KC - 1) * r)
                    for q in range(4):
                        last = pe.matmul(ps[32 * q:32 * q + 32, 4, :], ones[:, 0:32],
                                         ada_acc[:, q * HALF:(q + 1) * HALF], start=True, stop=True)
                    last.then_inc(ada_summed, 1)
                if n == 7:
                    pe.wait_ge(consts_in, 16 * N_CONST)
                    pe.wait_ge(pool_consts, 1)
                    pe.wait_ge(conv_c_ready, 1)
                    for j in range(2):
                        for h in range(4):
                            last = pe.transpose(ps[:, 7 - j, h * P:(h + 1) * P], w_sgu_raw[:, 4 * j + h, :], ident[:])
                        last.then_inc(sgu_w_turned, 1)
                if 9 <= n < 11:
                    if n == 9:
                        pe.wait_ge(mod_rows_ready, 2)
                        pe.wait_ge(sgu_w_ready, 2)
                    else:
                        pe.wait_ge(gt1_ready, 1)
                    q = 32 * (n - 9)
                    pe.matmul(ps[:, 7, :], ones[q:q + 1, :], mod01[q:q + 1, 1, :], start=True, stop=True
                              ).then_inc(gt1_spread, 1)
                if 11 <= n < 15:
                    turn_v(n - 11)
                if n >= 10:
                    ln_var_of(n - 10)
                if 9 <= n < 15:
                    ln_mean_of(n - 9)

            pe.wait_ge(gelu_ready, 2 * CT)
            pe.wait_ge(v_ready, CT)
            for ch in range(T):
                for h in range(HEADS):
                    last = pe.matmul(ps[HD * (h % 2):HD * (h % 2) + HD, h // 2, ch * P:(ch + 1) * P],
                                     v_sb[:, ch, h * HD:(h + 1) * HD], w_sgu_t[:, h, :], start=True, stop=True,
                                     skip_group_check=True)
            last.then_inc(sgu_mixed, 1)
            ln_mean_of(2 * CT - 2)
            ln_var_of(2 * CT - 2)
            ln_mean_of(2 * CT - 1)
            def mix(t, h, half):
                bank = 2 * (t % 2) + h
                for m in range(half * CT, (half + 1) * CT):
                    last = pe.matmul(ps[:, bank, :], y_cat[:, m, t * P:(t + 1) * P],
                                     wout_sb[:, m, h * HALF:(h + 1) * HALF], start=(m == CT), stop=(m == CT - 1))
                if half == 0:
                    last.then_inc(mix_done, 1)

            def turn_xn2(t):
                pe.wait_ge(xn2_ready, t + 1)
                if t >= 1:
                    pe.wait_ge(h2_act, KC // 2 * t)
                    pe.wait_ge(h2_dve, KC // 2 * t)
                for k in range(KC):
                    last = pe.transpose(ps[:, 4 + k // 4, (k % 4) * P:(k % 4 + 1) * P], xn2[:, t % 2, k, :], ident[:])
                last.then_inc(xn2_turned, 1)

            def route(t):
                if t >= 2:
                    pe.wait_ge(logits_ready, t - 1)
                pe.wait_ge(h2_act, KC // 2 * (t + 1))
                pe.wait_ge(h2_dve, KC // 2 * (t + 1))
                for k in range(KC):
                    last = pe.matmul(ps[:, 6 + t % 2, 0:NR], y_cat[:, k, t * P:(t + 1) * P],
                                     w_router[:, k, :], start=(k == 0), stop=(k == KC - 1), skip_group_check=True)
                last.then_inc(logits_done, 1)

            def mix_all(t, h):
                pe.wait_ge(x2_ready, 2 * (t - 2) + h + 1)
                mix(t, h, 1)
                mix(t, h, 0)

            pe.wait_ge(sgu_out, CT)
            pe.wait_ge(wout_in, 16)
            mix(0, 0, 1)
            ln_var_of(2 * CT - 1)
            mix(0, 1, 1)
            mix(1, 0, 1)
            mix(1, 1, 1)
            pe.wait_ge(conv_out, CT)
            for t in range(2):
                for h in range(2):
                    mix(t, h, 0)
            pe.wait_ge(router_packed, 1)
            mix_all(2, 0)
            turn_xn2(0)
            mix_all(2, 1)
            route(0)
            turn_xn2(1)
            mix_all(3, 0)
            route(1)
            turn_xn2(2)
            mix_all(3, 1)
            route(2)
            turn_xn2(3)
            route(3)
            for j in range(2):
                q = 32 * (2 + j)
                last = pe.matmul(ps[SLOTS * j:SLOTS * (j + 1), 0, :], ones[q:q + 1, 0:SLOTS], mod2[q:q + 1, :],
                                 start=True, stop=True)
            last.then_inc(gt2_spread, 1)
            pe.wait_ge(hot_ready, 1)
            def count(tiles, lhs, t):
                n = tiles.stop - tiles.start
                return pe.matmul(ps[:, 7, tiles.start * NE:tiles.stop * NE], lhs,
                                 hot16[:, t, :].unsqueeze(1).to_broadcast([P, n, NE]), start=False,
                                 stop=(t == T - 1), skip_group_check=True)

            pe.matmul(ps[:, 7, 0:T * NE], before16[:], hot16.rearrange("p t e -> p (t e)"), start=True, stop=False,
                      skip_group_check=True)
            for t in range(T):
                if t < T - 1:
                    count(slice(t + 1, T), ones16[:], t)
                last = count(slice(T, T + 1), ones16[:], t)
            last.then_inc(counted, 1)

            def find_rows(e, src, got):
                for t in range(T):
                    last = pe.matmul(ps[:, 7, 0:2], src[:, t, :],
                                     row_vals[:, t, bass.ds(e, 1), :].rearrange("p o v -> p (o v)"),
                                     start=(t == 0), stop=(t == T - 1), skip_group_check=True)
                last.then_inc(got, 1)

            def turn(src, bank, got):
                pe.sem_inc(tokens_here, 1)
                for k in range(KC):
                    last = pe.transpose(ps[:, bank, k * SLOTS:(k + 1) * SLOTS], src[0:SLOTS, k, :],
                                        ident[0:SLOTS, 0:SLOTS])
                last.then_inc(got, 1)

            def gate_up(src, bank, slot, got):
                w = ring[:, slot * SLOT_W:slot * SLOT_W + GU_W].rearrange("p (g k f) -> p g k f", g=2, k=KC)
                for k in range(KC):
                    for j in range(2):
                        last = pe.matmul(ps[SLOTS * j:SLOTS * (j + 1), bank, 0:2 * P].rearrange(
                            "p (g f) -> p g f", g=2), src[:, k, :], w[:, :, k, j * P:(j + 1) * P],
                            start=(k == 0), stop=(k == KC - 1), skip_group_check=True)
                last.then_inc(got, 1)

            def turn_hidden(src, got):
                pe.transpose(ps[:, 4, 0:P], src, ident[:]).then_inc(got, 1)

            def down(src, bank, slot, got):
                w = ring[:, slot * SLOT_W + GU_W:(slot + 1) * SLOT_W].rearrange("p (c n) -> p c n", c=FC)
                for f in range(FC):
                    for j in range(2):
                        last = pe.matmul(ps[SLOTS * j:SLOTS * (j + 1), bank, :], src[:, f * SLOTS:(f + 1) * SLOTS],
                                         w[:, f, j * HALF:(j + 1) * HALF], start=(f == 0), stop=(f == FC - 1),
                                         skip_group_check=True)
                last.then_inc(got, 1)

            def step(e, b2, slot, bg, tokens, weights, first, y_free, find, nxt):
                if find:
                    pe.wait_ge(picks_ready, e + AHEAD + 1)
                    pe.wait_ge(rows_ready, e + AHEAD)
                    find_rows(e + AHEAD, picks[:, b2], rows_found)
                if nxt:
                    if not first:
                        pe.wait_ge(xt_ready, e)
                    pe.wait_ge(gathered[bg], tokens)
                    turn(xg[:, bg], 1 - b2, xg_turned)
                pe.wait_ge(xt_ready, e + 1)
                if not first:
                    pe.wait_ge(hid_ready, e)
                pe.wait_ge(expert_in[slot], weights)
                gate_up(xt[:, b2], 2 + b2, slot, gate_up_done)
                if not first:
                    if y_free:
                        pe.wait_ge(y_ready, e - 2)
                    pe.wait_ge(hid_t_ready, e)
                    down(hid_t[:, 1 - b2], 6 - b2, (slot - 1) % RING, down_done)
                pe.wait_ge(hid_ready, e + 1)
                turn_hidden(hid[:, b2, :], hid_turned)
                with extra_blocks(pe, e) as n:
                    pe.wait_ge(hid_t_ready, e + 1)
                    if find:
                        pe.wait_ge(rows_ready, e + AHEAD + 1)
                    if y_free or b2 == 0 and not first:
                        pe.wait_ge(y_ready, e - 1)
                    pe.wait_ge(ov_picks, n + 1)
                    find_rows(e, picks_x, ov_found)
                    pe.wait_ge(ov_gathered, 16 * n + 16)
                    turn(xg_x, b2, ov_turned)
                    pe.wait_ge(ov_xt, n + 1)
                    gate_up(xt_x, 3 - b2, slot, ov_gate_up)
                    pe.wait_ge(ov_hid, n + 1)
                    turn_hidden(hid_x, ov_hid_turned)
                    pe.wait_ge(ov_hid_t, n + 1)
                    down(hid_t_x, 5 + b2, slot, ov_down)
                    pe.wait_ge(ov_y, n + 1)
                    pe.sem_inc(ov_passed, 1)
                pe.sem_inc(step_passed, 1)

            pe.wait_ge(places_ready, 1)
            for e in range(AHEAD):
                pe.wait_ge(picks_ready, e + 1)
                if e:
                    pe.wait_ge(rows_ready, e)
                find_rows(e, picks[:, e % 2], rows_found)
            pe.wait_ge(gathered[0], 16)
            pe.wait_ge(gt2_ready, 1)
            turn(xg[:, 0], 0, xg_turned)
            pe.wait_ge(routed, 1)
            for e in range(3):
                step(e, e % 2, e, (e + 1) % XG, 16 * ((e + 1) // XG + 1), 48, e == 0, False, True, True)
            with pe.Fori(0, 2) as i:
                for r in range(2 * RING):
                    step(3 + 2 * RING * i + r, (1 + r) % 2, (3 + r) % RING, (4 + r) % XG,
                         16 * (2 * RING // XG * i + (4 + r) // XG + 1), 48 * (2 * i + (3 + r) // RING + 1),
                         False, True, True, True)
            for e in range(3 + 4 * RING, NE):
                step(e, e % 2, e % RING, (e + 1) % XG, 16 * ((e + 1) // XG + 1), 48 * (e // RING + 1),
                     False, True, e + AHEAD < NE, e + 1 < NE)
            pe.wait_ge(y_ready, NE - 2)
            pe.wait_ge(hid_t_ready, NE)
            down(hid_t[:, (NE - 1) % 2], 6, (NE - 1) % RING, down_done)



_INS = ["x", "c", "w_ada", "b_ada", "g_mix", "w_in", "conv_w", "conv_b", "conv_ln_g", "conv_ln_b",
        "sgu_ln_g", "sgu_ln_b", "sgu_w", "sgu_b", "w_out", "g_ffn", "w_coarse", "b_coarse",
        "w_fine", "b_fine", "w_gate", "w_up", "w_down", "g_final"]


def kernel(**inputs):
    import numpy as _np
    import concourse.bacc as _bacc
    from concourse import mybir as _mybir
    from concourse.bass_utils import run_bass_kernel_spmd as _run

    nc = _bacc.Bacc("TRN2", target_bir_lowering=False, num_devices=1, dynamic_dma_scratch_size=8192)
    arrays, args = {}, []
    for name in _INS:
        a = _np.ascontiguousarray(inputs[name])
        arrays[f"in_{name}"] = a
        args.append(nc.dram_tensor(f"in_{name}", a.shape, _mybir.dt.from_np(a.dtype), kind="ExternalInput").ap())
    shape = inputs["x"].shape
    out = nc.dram_tensor("out", shape, _mybir.dt.float32, kind="ExternalOutput").ap()
    build_block(nc, *args, out)
    r = _run(nc, [arrays], core_ids=[0])
    return r.results[0]["out"]
```
